# Optimizing a Trainium2 kernel written in Bass

```python
import math, functools
import jax
import jax.numpy as jnp
from jax import lax
import numpy as np

D_MODEL = 1024
BATCH = 1
SEQ = 512
DEPTH = 2

GRID_W = 64
CTX_LEN = 256
N_MIXERS = 4
F32 = jnp.float32
RMS_EPS = 1e-6
L2_EPS = 1e-6
ROPE_BASE = 10000.0

NA_HEADS = 16
NA_HEAD_DIM = D_MODEL // NA_HEADS
NA_WIN_ROWS = 8
NA_WIN_COLS = 16
GDN_HEADS = 8
GDN_HEAD_DIM = D_MODEL // GDN_HEADS
GDN_WIDTH = GDN_HEADS * GDN_HEAD_DIM
GDN_CONV = 3
GDN_CHUNK = 64
DIFF_HEADS = 8
DIFF_HEAD_DIM = D_MODEL // (2 * DIFF_HEADS)
DIFF_Q_BLOCK = 128
HY_ORDER = 2
HY_CONV = 3
HY_EMB_DIM = 33
HY_FILTER_WIDTH = 64
HY_MAX_DECAY = math.log(1e-2) / 0.3
HY_MIN_DECAY = math.log(1e-2) / 1.5
FFN_DIM = 2816
MOE_EXPERTS = 8
MOE_TOP_K = 2
MOE_FFN_DIM = 1408

kernel_name = 'hybrid_latent_diffusion_block'

def _rmsnorm(x, g):
    x32 = x.astype(F32)
    y = x32 * lax.rsqrt(jnp.mean(x32 * x32, axis=-1, keepdims=True) + RMS_EPS)
    return y.astype(x.dtype) * g

def _l2norm(x):
    x32 = x.astype(F32)
    return x32 * lax.rsqrt(jnp.sum(x32 * x32, axis=-1, keepdims=True) + L2_EPS)

def _modulate(h, shift, scale):
    return h * (1.0 + scale) + shift

def _dwconv(x, w):
    k, ch = w.shape
    return lax.conv_general_dilated(x, w.astype(x.dtype)[:, None, :], window_strides=(1,),
                                    padding=[(k // 2, k // 2)],
                                    dimension_numbers=('NWC', 'WIO', 'NWC'),
                                    feature_group_count=ch)

def _axial_rope(x, rows, cols):
    half = x.shape[-1] // 2
    inv = ROPE_BASE ** (-jnp.arange(0, half, 2, dtype=F32) / half)
    bshape = (x.shape[1],) + (1,) * (x.ndim - 3) + (half,)

    def rot(xa, p):
        ang = p.astype(F32)[:, None] * inv[None, :]
        ang = jnp.concatenate([ang, ang], axis=-1).reshape(bshape)
        xa = xa.astype(F32)
        x1, x2 = jnp.split(xa, 2, axis=-1)
        return xa * jnp.cos(ang) + jnp.concatenate([-x2, x1], axis=-1) * jnp.sin(ang)

    return jnp.concatenate([rot(x[..., :half], rows), rot(x[..., half:], cols)], axis=-1).astype(x.dtype)

def _neighbourhood_attention(hl, hc, w_qkv, q_norm, k_norm, rpb, w_o):
    B, S, D = hl.shape
    R = S // GRID_W
    wr = min(NA_WIN_ROWS, R)
    scale = NA_HEAD_DIM ** -0.5

    def heads(h):
        q, k, v = jnp.split(h @ w_qkv, 3, axis=-1)
        shp = h.shape[:2] + (NA_HEADS, NA_HEAD_DIM)
        return _rmsnorm(q.reshape(shp), q_norm) * scale, _rmsnorm(k.reshape(shp), k_norm), v.reshape(shp)

    q, k, v = heads(hl)
    qc, kc, vc = heads(hc)
    pc = jax.nn.softmax(jnp.einsum('bqhd,bkhd->bhqk', qc, kc).astype(F32), axis=-1).astype(vc.dtype)
    yc = jnp.einsum('bhqk,bkhd->bqhd', pc, vc).reshape(hc.shape) @ w_o

    grid = lambda t: t.reshape(B, R, GRID_W, NA_HEADS, NA_HEAD_DIM)
    qg, kg, vg = grid(q), grid(k), grid(v)
    cols = jnp.arange(GRID_W)
    c0 = jnp.clip(cols - NA_WIN_COLS // 2, 0, GRID_W - NA_WIN_COLS)
    col_valid = (cols[None, :] >= c0[:, None]) & (cols[None, :] < c0[:, None] + NA_WIN_COLS)
    col_idx = jnp.clip(cols[None, :] - cols[:, None], 1 - NA_WIN_COLS, NA_WIN_COLS - 1) + NA_WIN_COLS - 1
    n_loc = wr * GRID_W

    def row_block(r):
        r0 = jnp.clip(r - wr // 2, 0, R - wr)
        q_r = lax.dynamic_index_in_dim(qg, r, axis=1, keepdims=False)
        k_r = lax.dynamic_slice_in_dim(kg, r0, wr, axis=1)
        v_r = lax.dynamic_slice_in_dim(vg, r0, wr, axis=1)
        row_idx = r0 + jnp.arange(wr) - r + NA_WIN_ROWS - 1
        bias = jnp.transpose(rpb[:, row_idx][:, :, col_idx], (0, 2, 1, 3))
        s_loc = jnp.einsum('bqhd,bikhd->bhqik', q_r, k_r).astype(F32) + bias
        s_loc = jnp.where(col_valid[:, None, :], s_loc, -jnp.inf).reshape(B, NA_HEADS, GRID_W, n_loc)
        s_ctx = jnp.einsum('bqhd,bchd->bhqc', q_r, kc).astype(F32)
        p = jax.nn.softmax(jnp.concatenate([s_loc, s_ctx], axis=-1), axis=-1).astype(v.dtype)
        p_loc = p[..., :n_loc].reshape(B, NA_HEADS, GRID_W, wr, GRID_W)
        return (jnp.einsum('bhqik,bikhd->bqhd', p_loc, v_r)
                + jnp.einsum('bhqc,bchd->bqhd', p[..., n_loc:], vc))

    o = lax.map(row_block, jnp.arange(R))
    yl = jnp.moveaxis(o, 0, 1).reshape(B, S, D) @ w_o
    return yl, yc

def _chunk_gated_delta(q, k, v, g, beta, state0):
    B, H, L, dk = q.shape
    dv = v.shape[-1]
    n = L // GDN_CHUNK
    C = GDN_CHUNK
    q = (q * dk ** -0.5).reshape(B, H, n, C, dk)
    k = k.reshape(B, H, n, C, dk)
    v = v.reshape(B, H, n, C, dv)
    beta = beta.reshape(B, H, n, C)
    gc = jnp.cumsum(g.reshape(B, H, n, C), axis=-1)
    idx = jnp.arange(C)
    incl = idx[:, None] >= idx[None, :]
    decay = jnp.exp(jnp.where(incl, gc[..., :, None] - gc[..., None, :], -jnp.inf))
    kb = k * beta[..., None]
    a_strict = jnp.einsum('bhnid,bhnjd->bhnij', kb, k) * decay * (idx[:, None] > idx[None, :])
    rhs = jnp.concatenate([v * beta[..., None], kb * jnp.exp(gc)[..., None]], axis=-1)
    sol = lax.linalg.triangular_solve(a_strict + jnp.eye(C, dtype=F32), rhs, left_side=True,
                                      lower=True, unit_diagonal=True)
    u, w = sol[..., :dv], sol[..., dv:]
    attn = jnp.einsum('bhnid,bhnjd->bhnij', q, k) * decay

    def step(S, inp):
        q_i, k_i, u_i, w_i, g_i, a_i = inp
        v_new = u_i - jnp.einsum('bhcd,bhde->bhce', w_i, S)
        o = (jnp.einsum('bhcd,bhde->bhce', q_i * jnp.exp(g_i)[..., None], S)
             + jnp.einsum('bhij,bhje->bhie', a_i, v_new))
        g_last = g_i[..., -1]
        S = (S * jnp.exp(g_last)[..., None, None]
             + jnp.einsum('bhcd,bhce->bhde', k_i * jnp.exp(g_last[..., None] - g_i)[..., None], v_new))
        return S, o

    xs = tuple(jnp.moveaxis(t, 2, 0) for t in (q, k, u, w, gc, attn))
    S, o = lax.scan(step, state0, xs)
    return jnp.moveaxis(o, 0, 2).reshape(B, H, L, dv), S

def _gated_deltanet(hl, hc, w_qkv, conv_w, w_gate, w_beta, w_decay, a_log, dt_bias, out_norm, w_o):
    def bidir(h, s0_f, s0_b):
        B, L, _ = h.shape
        u = jax.nn.silu(_dwconv(h @ w_qkv, conv_w))
        heads = lambda t: jnp.swapaxes(t.reshape(B, L, GDN_HEADS, GDN_HEAD_DIM), 1, 2)
        q, k, v = jnp.split(u, 3, axis=-1)
        q, k, v = _l2norm(heads(q)), _l2norm(heads(k)), heads(v).astype(F32)

        def gates(d):
            beta = jax.nn.sigmoid((h @ w_beta[d]).astype(F32))
            g = -jnp.exp(a_log[d].astype(F32)) * jax.nn.softplus((h @ w_decay[d]).astype(F32) + dt_bias[d])
            return jnp.swapaxes(g, 1, 2), jnp.swapaxes(beta, 1, 2)

        flip = lambda t: jnp.flip(t, axis=2)
        g_f, b_f = gates(0)
        g_b, b_b = gates(1)
        o_f, s_f = _chunk_gated_delta(q, k, v, g_f, b_f, s0_f)
        o_b, s_b = _chunk_gated_delta(flip(q), flip(k), flip(v), flip(g_b), flip(b_b), s0_b)
        o = jnp.swapaxes(o_f + flip(o_b), 1, 2)
        gate = jax.nn.silu(h @ w_gate).reshape(B, L, GDN_HEADS, GDN_HEAD_DIM)
        y = (_rmsnorm(o, out_norm) * gate).reshape(B, L, GDN_WIDTH) @ w_o
        return y, s_f, s_b

    zeros = jnp.zeros((hc.shape[0], GDN_HEADS, GDN_HEAD_DIM, GDN_HEAD_DIM), F32)
    yc, sc_f, sc_b = bidir(hc, zeros, zeros)
    yl, _, _ = bidir(hl, sc_f, sc_b)
    return yl, yc

def _diff_weights(s, lam):
    p = jax.nn.softmax(s, axis=-1)
    return p[:, 0] - lam * p[:, 1]

def _diff_attention(hl, hc, lambda_init, w_qkv, q_norm, k_norm, lam_vecs, out_norm, w_o):
    B, S, D = hl.shape
    hd = DIFF_HEAD_DIM
    lv = lam_vecs.astype(F32)
    lam = jnp.exp(jnp.sum(lv[0] * lv[1])) - jnp.exp(jnp.sum(lv[2] * lv[3])) + lambda_init

    def heads(h):
        q, k, v = jnp.split(h @ w_qkv, 3, axis=-1)
        shp = h.shape[:2] + (DIFF_HEADS, 2, hd)
        return (_rmsnorm(q.reshape(shp), q_norm), _rmsnorm(k.reshape(shp), k_norm),
                v.reshape(h.shape[:2] + (DIFF_HEADS, 2 * hd)))

    pos = jnp.arange(S)
    rows, cols = pos // GRID_W, pos % GRID_W
    q, k, v = heads(hl)
    q = _axial_rope(q, rows, cols) * hd ** -0.5
    k = _axial_rope(k, rows, cols)
    qc, kc, vc = heads(hc)
    qc = qc * hd ** -0.5
    ac = _diff_weights(jnp.einsum('bqhmd,bkhmd->bmhqk', qc, kc).astype(F32), lam).astype(vc.dtype)
    oc = jnp.einsum('bhqk,bkhe->bqhe', ac, vc)

    nb = S // DIFF_Q_BLOCK
    qb = jnp.moveaxis(q.reshape(B, nb, DIFF_Q_BLOCK, DIFF_HEADS, 2, hd), 1, 0)

    def block(q_blk):
        s = jnp.concatenate([jnp.einsum('bqhmd,bkhmd->bmhqk', q_blk, k),
                             jnp.einsum('bqhmd,bkhmd->bmhqk', q_blk, kc)], axis=-1).astype(F32)
        a = _diff_weights(s, lam).astype(v.dtype)
        return (jnp.einsum('bhqk,bkhe->bqhe', a[..., :S], v)
                + jnp.einsum('bhqc,bche->bqhe', a[..., S:], vc))

    ol = jnp.moveaxis(lax.map(block, qb), 0, 1).reshape(B, S, DIFF_HEADS, 2 * hd)
    out = lambda o: (_rmsnorm(o, out_norm) * (1.0 - lambda_init)).reshape(o.shape[:2] + (D,)) @ w_o
    return out(ol), out(oc)

def _hyena_filters(L, w1, b1, freq, w2, b2, w3, b3):
    D = w3.shape[1] // (2 * HY_ORDER)
    t = jnp.linspace(0.0, 1.0, L, dtype=F32)[:, None]
    bands = (HY_EMB_DIM - 1) // 2
    w = 2.0 * math.pi * jnp.arange(L, dtype=F32) / L
    f = jnp.linspace(1e-4, bands - 1, bands, dtype=F32)
    ang = w[:, None] * f[None, :]
    z = jnp.concatenate([t, jnp.cos(ang), -jnp.sin(ang)], axis=-1)
    hdn = jnp.sin(freq[0] * (z @ w1 + b1))
    hdn = jnp.sin(freq[1] * (hdn @ w2 + b2))
    h = (hdn @ w3 + b3).astype(F32).reshape(L, HY_ORDER, 2, D)
    deltas = jnp.abs(jnp.linspace(HY_MIN_DECAY, HY_MAX_DECAY, D, dtype=F32))
    h = h * jnp.exp(-t * deltas)[:, None, None, :]
    return h / jnp.sum(jnp.abs(h), axis=(0, 2), keepdims=True)

def _bidir_fftconv(u, h_fwd, h_bwd, skip):
    L = u.shape[1]
    u32 = u.astype(F32)
    kern = jnp.concatenate([h_fwd, jnp.zeros_like(h_fwd[:1]), h_bwd[:0:-1]], axis=0)
    y = jnp.fft.irfft(jnp.fft.rfft(u32, n=2 * L, axis=1) * jnp.fft.rfft(kern, n=2 * L, axis=0)[None],
                      n=2 * L, axis=1)[:, :L]
    return (y + u32 * skip).astype(u.dtype)

def _hyena(h, w_in, conv_w, f_w1, f_b1, f_freq, f_w2, f_b2, f_w3, f_b3, skip, w_o):
    L = h.shape[1]
    x1, x2, v = jnp.split(_dwconv(h @ w_in, conv_w), HY_ORDER + 1, axis=-1)
    filt = _hyena_filters(L, f_w1, f_b1, f_freq, f_w2, f_b2, f_w3, f_b3)
    z = v
    for n, gate in enumerate((x1, x2)):
        z = gate * _bidir_fftconv(z, filt[:, n, 0], filt[:, n, 1], skip[n])
    return z @ w_o

def _swiglu(h, w_in, w_out):
    a, b = jnp.split(h @ w_in, 2, axis=-1)
    return (jax.nn.silu(a) * b) @ w_out

def _moe(h, router, w_in, w_out):
    logits = (h @ router).astype(F32)
    top_v, top_i = lax.top_k(logits, MOE_TOP_K)
    top_w = jax.nn.softmax(top_v, axis=-1)
    gates = jnp.sum(jax.nn.one_hot(top_i, MOE_EXPERTS, dtype=F32) * top_w[..., None], axis=-2).astype(h.dtype)
    return sum(gates[..., e, None] * _swiglu(h, w_in[e], w_out[e]) for e in range(MOE_EXPERTS))

def setup_inputs(seed: int = 0) -> dict:
    key = jax.random.key(seed)
    keys = iter(jax.random.split(key, 64))
    D = D_MODEL
    n_dense, n_moe = (DEPTH + 1) // 2, DEPTH // 2

    def nrm(shape, scale):
        return jax.random.normal(next(keys), shape, F32) * scale

    def gain(shape):
        return 1.0 + nrm(shape, 0.05)

    dt = jnp.exp(jax.random.uniform(next(keys), (2, GDN_HEADS), F32, math.log(1e-3), math.log(1e-1)))
    a_log = jnp.log(jax.random.uniform(next(keys), (2, GDN_HEADS), F32, 1.0, 16.0))
    return {
        'x': nrm((BATCH, SEQ, D), 1.0),
        'c': nrm((BATCH, D), 1.0),
        'ctx': nrm((BATCH, CTX_LEN, D), 1.0),
        'c_ctx': nrm((D,), 1.0),
        'ada_w': nrm((DEPTH, D, 6 * D), 0.5 * D ** -0.5),
        'ada_b': nrm((DEPTH, 6 * D), 0.02),
        'norm_g': gain((DEPTH, 2, D)),
        'na_w_qkv': nrm((D, 3 * D), D ** -0.5),
        'na_q_norm': gain((NA_HEAD_DIM,)),
        'na_k_norm': gain((NA_HEAD_DIM,)),
        'na_rpb': nrm((NA_HEADS, 2 * NA_WIN_ROWS - 1, 2 * NA_WIN_COLS - 1), 0.1),
        'na_w_o': nrm((D, D), D ** -0.5),
        'gdn_w_qkv': nrm((D, 3 * GDN_WIDTH), D ** -0.5),
        'gdn_conv': nrm((GDN_CONV, 3 * GDN_WIDTH), GDN_CONV ** -0.5),
        'gdn_w_gate': nrm((D, GDN_WIDTH), D ** -0.5),
        'gdn_w_beta': nrm((2, D, GDN_HEADS), D ** -0.5),
        'gdn_w_decay': nrm((2, D, GDN_HEADS), 0.1 * D ** -0.5),
        'gdn_a_log': a_log,
        'gdn_dt_bias': dt + jnp.log(-jnp.expm1(-dt)),
        'gdn_out_norm': gain((GDN_HEAD_DIM,)),
        'gdn_w_o': nrm((GDN_WIDTH, D), GDN_WIDTH ** -0.5),
        'diff_w_qkv': nrm((D, 3 * D), D ** -0.5),
        'diff_q_norm': gain((DIFF_HEAD_DIM,)),
        'diff_k_norm': gain((DIFF_HEAD_DIM,)),
        'diff_lambda': nrm((4, DIFF_HEAD_DIM), 0.1),
        'diff_out_norm': gain((2 * DIFF_HEAD_DIM,)),
        'diff_w_o': nrm((D, D), D ** -0.5),
        'hy_w_in': nrm((D, (HY_ORDER + 1) * D), D ** -0.5),
        'hy_conv': nrm((HY_CONV, (HY_ORDER + 1) * D), HY_CONV ** -0.5),
        'hy_filt_w1': nrm((HY_EMB_DIM, HY_FILTER_WIDTH), HY_EMB_DIM ** -0.5),
        'hy_filt_b1': nrm((HY_FILTER_WIDTH,), 0.1),
        'hy_filt_freq': gain((2, HY_FILTER_WIDTH)),
        'hy_filt_w2': nrm((HY_FILTER_WIDTH, HY_FILTER_WIDTH), HY_FILTER_WIDTH ** -0.5),
        'hy_filt_b2': nrm((HY_FILTER_WIDTH,), 0.1),
        'hy_filt_w3': nrm((HY_FILTER_WIDTH, 2 * HY_ORDER * D), HY_FILTER_WIDTH ** -0.5),
        'hy_filt_b3': nrm((2 * HY_ORDER * D,), 0.02),
        'hy_skip': nrm((HY_ORDER, D), 1.0),
        'hy_w_o': nrm((D, D), D ** -0.5),
        'ffn_w_in': nrm((n_dense, D, 2 * FFN_DIM), D ** -0.5),
        'ffn_w_out': nrm((n_dense, FFN_DIM, D), FFN_DIM ** -0.5),
        'moe_router': nrm((n_moe, D, MOE_EXPERTS), D ** -0.5),
        'moe_w_in': nrm((n_moe, MOE_EXPERTS, D, 2 * MOE_FFN_DIM), D ** -0.5),
        'moe_w_out': nrm((n_moe, MOE_EXPERTS, MOE_FFN_DIM, D), MOE_FFN_DIM ** -0.5),
    }

def reference(x, c, ctx, c_ctx, ada_w, ada_b, norm_g,
              na_w_qkv, na_q_norm, na_k_norm, na_rpb, na_w_o,
              gdn_w_qkv, gdn_conv, gdn_w_gate, gdn_w_beta, gdn_w_decay, gdn_a_log, gdn_dt_bias,
              gdn_out_norm, gdn_w_o,
              diff_w_qkv, diff_q_norm, diff_k_norm, diff_lambda, diff_out_norm, diff_w_o,
              hy_w_in, hy_conv, hy_filt_w1, hy_filt_b1, hy_filt_freq, hy_filt_w2, hy_filt_b2,
              hy_filt_w3, hy_filt_b3, hy_skip, hy_w_o,
              ffn_w_in, ffn_w_out, moe_router, moe_w_in, moe_w_out):
    n_ctx = ctx.shape[1]
    silu_c = jax.nn.silu(c)
    silu_cc = jax.nn.silu(c_ctx)
    hyena = functools.partial(_hyena, w_in=hy_w_in, conv_w=hy_conv, f_w1=hy_filt_w1, f_b1=hy_filt_b1,
                              f_freq=hy_filt_freq, f_w2=hy_filt_w2, f_b2=hy_filt_b2, f_w3=hy_filt_w3,
                              f_b3=hy_filt_b3, skip=hy_skip, w_o=hy_w_o)
    xl, xc = x, ctx
    for i in range(DEPTH):
        last = i == DEPTH - 1
        kind = i % N_MIXERS
        ml = [m[:, None, :] for m in jnp.split(silu_c @ ada_w[i] + ada_b[i], 6, axis=-1)]
        mc = jnp.split(silu_cc @ ada_w[i] + ada_b[i], 6, axis=-1)
        hl = _modulate(_rmsnorm(xl, norm_g[i, 0]), ml[0], ml[1])
        ctx_needed = (not last) or kind != 3
        hc = _modulate(_rmsnorm(xc, norm_g[i, 0]), mc[0], mc[1]) if ctx_needed else None
        if kind == 0:
            yl, yc = _neighbourhood_attention(hl, hc, na_w_qkv, na_q_norm, na_k_norm, na_rpb, na_w_o)
        elif kind == 1:
            yl, yc = _gated_deltanet(hl, hc, gdn_w_qkv, gdn_conv, gdn_w_gate, gdn_w_beta, gdn_w_decay,
                                     gdn_a_log, gdn_dt_bias, gdn_out_norm, gdn_w_o)
        elif kind == 2:
            yl, yc = _diff_attention(hl, hc, 0.8 - 0.6 * math.exp(-0.3 * i), diff_w_qkv, diff_q_norm,
                                     diff_k_norm, diff_lambda, diff_out_norm, diff_w_o)
        else:
            yl = hyena(hl)
            yc = hyena(hc) if ctx_needed else None
        xl = xl + ml[2] * yl
        if not last:
            xc = xc + mc[2] * yc
        j = i // 2
        if i % 2 == 0:
            ffn = functools.partial(_swiglu, w_in=ffn_w_in[j], w_out=ffn_w_out[j])
        else:
            ffn = functools.partial(_moe, router=moe_router[j], w_in=moe_w_in[j], w_out=moe_w_out[j])
        hl = _modulate(_rmsnorm(xl, norm_g[i, 1]), ml[3], ml[4])
        if last:
            xl = xl + ml[5] * ffn(hl)
        else:
            hc = _modulate(_rmsnorm(xc, norm_g[i, 1]), mc[3], mc[4])
            y = ffn(jnp.concatenate([hc, hl], axis=1))
            xc = xc + mc[5] * y[:, :n_ctx]
            xl = xl + ml[5] * y[:, n_ctx:]
    return xl


_drawn_inputs = setup_inputs


def setup_inputs(seed=0):
    import zlib

    import numpy as np

    out = dict(_drawn_inputs(seed))
    spreads = {}
    factors = {'na_q_norm': 8.0,
     'na_k_norm': 8.0,
     'na_rpb': 8.0,
     'gdn_w_decay': 8.0,
     'gdn_out_norm': 4.921}
    for name, (base, spread) in spreads.items():
        noise = np.random.default_rng([zlib.crc32(name.encode()), seed]).standard_normal(out[name].shape)
        drawn = base * np.exp(spread * noise) if base else spread * noise
        out[name] = jnp.asarray(drawn.astype(out[name].dtype))
    for name, factor in factors.items():
        out[name] = (out[name] * factor).astype(out[name].dtype)
    return out
```

```python
from contextlib import ExitStack

import numpy as np

import concourse.bass as bass
from concourse import mybir

F32 = mybir.dt.float32
U32 = mybir.dt.uint32
ALU = mybir.AluOpType
ACT = mybir.ActivationFunctionType
AX = mybir.AxisListType

P = 128
D = 1024
KD = D // P
CTX, LAT = 256, 512
TOK = CTX + LAT
GRID_R, GRID_C = 8, 64
BANK = 512
EPS = 1e-6
SLOT = 4096
SLOTS = 4

NA_HEADS, NA_HD = 16, 64
NA_PAIRS = NA_HEADS // 2
WIN_R, WIN_C = 8, 16
DR = 2 * WIN_R - 1
DC = 2 * WIN_C - 1
BIAS_DC = 2 * DC + 1
BIAS_RUN = 48 * DR
WIN = 256
WIN_START = (0, 64, 192, 256)
WIN_VARIANT = (0, 1, 1, 2)
WIN_SHIFT = (16, 8, 0)
MASKED = -1e30

FFN = 2816
EXPERTS = 8
EFF = 1408

GH, GD = 8, 128
CH = 64

C_IDENT = 0
C_MEAN = C_IDENT + P
C_HALF = C_MEAN + P
C_ONES = C_HALF + P
C_WMASK = C_ONES + P
C_CUMF = C_WMASK + 96
C_CUMB = C_CUMF + P
C_BLK = C_CUMB + P
C_STRF = C_BLK + P
C_STRB = C_STRF + P
C_LEVF = C_STRB + P
C_LEVB = C_LEVF + 6 * P
C_IOTA = C_LEVB + 6 * P
C_EPS = C_IOTA + EXPERTS
C_ALL = C_EPS + 4


def constants():
    c = np.zeros((P, C_ALL), np.float32)
    i = np.arange(P)
    row, col = i[:, None], i[None, :]
    same = row // CH == col // CH
    c[:, C_IDENT:C_IDENT + P] = row == col
    c[:, C_MEAN:C_MEAN + P] = 1.0 / D
    c[:, C_HALF:C_HALF + P] = (row // NA_HD == col // NA_HD) / NA_HD
    c[:, C_ONES:C_ONES + P] = 1.0
    for v, (block, start) in enumerate(((0, 0), (1, 8), (3, 32))):
        qcol = 16 * block + i // 8
        c0 = np.clip(qcol - WIN_C // 2, 0, GRID_C - WIN_C)[:, None]
        kcol = start + np.arange(32)[None, :]
        c[:, C_WMASK + 32 * v:C_WMASK + 32 * v + 32] = np.where((kcol >= c0) & (kcol < c0 + WIN_C), 0.0, MASKED)
    c[:, C_CUMF:C_CUMF + P] = same & (row <= col)
    c[:, C_CUMB:C_CUMB + P] = same & (row >= col)
    c[:, C_BLK:C_BLK + P] = same
    c[:, C_STRF:C_STRF + P] = same & (row < col)
    c[:, C_STRB:C_STRB + P] = same & (row > col)
    for n in range(6):
        s = 1 << n
        pair = (row // (2 * s) == col // (2 * s)) & (row // s != col // s)
        c[:, C_LEVF + n * P:C_LEVF + n * P + P] = pair & (row > col)
        c[:, C_LEVB + n * P:C_LEVB + n * P + P] = pair & (row < col)
    c[:, C_IOTA:C_IOTA + EXPERTS] = np.arange(EXPERTS)
    c[:, C_EPS:C_EPS + 4] = (EPS, NA_HD * EPS, 1.0, GD * EPS)
    return c


S_C = 0
S_ADAB = S_C + 2 * KD
S_NORM = S_ADAB + 96
S_QN = S_NORM + 4 * KD
S_CONV = S_QN + 2
S_WBD = S_CONV + 72
S_ALOG = S_WBD + 32 * KD
S_DTB = S_ALOG + 2 * GH
S_ON = S_DTB + 2 * GH
S_RT = S_ON + 1
S_ALL = S_RT + EXPERTS * KD


def small_inputs(x):
    def groups(a):
        a = np.asarray(a)
        return np.moveaxis(a.reshape(a.shape[:-1] + (a.shape[-1] // P, P)), -1, 0)

    def rows(a):
        a = np.asarray(a)
        return a.reshape(a.shape[0] // P, P, a.shape[1]).transpose(1, 0, 2)

    gates = [x["gdn_w_beta"][0], x["gdn_w_beta"][1], x["gdn_w_decay"][0], x["gdn_w_decay"][1]]
    parts = [
        rows(np.stack([np.asarray(x["c"])[0], np.asarray(x["c_ctx"])], axis=1)),
        groups(x["ada_b"]), groups(x["norm_g"]),
        np.stack([np.tile(np.asarray(x["na_q_norm"]), 2), np.tile(np.asarray(x["na_k_norm"]), 2)], axis=1),
        groups(x["gdn_conv"]).transpose(0, 2, 1),
        rows(np.concatenate([np.asarray(g) for g in gates], axis=1)),
        np.broadcast_to(np.asarray(x["gdn_a_log"]).reshape(1, -1), (P, 2 * GH)),
        np.broadcast_to(np.asarray(x["gdn_dt_bias"]).reshape(1, -1), (P, 2 * GH)),
        np.asarray(x["gdn_out_norm"]).reshape(P, 1),
        rows(x["moe_router"][0]),
    ]
    return np.ascontiguousarray(np.concatenate([a.reshape(P, -1) for a in parts], axis=1))


def bias_table(rpb):
    rpb = np.asarray(rpb)
    t = np.zeros((NA_HEADS, BIAS_DC, DR), rpb.dtype)
    t[:, DC - 15:DC + 16, :] = rpb.transpose(0, 2, 1)[:, ::-1, ::-1]
    return np.concatenate([t.reshape(-1), np.zeros(BIAS_RUN, rpb.dtype)])


class Core:
    pass


def open_memory(nc, ctx, dram):
    m = Core()
    m.nc, m.ctx, m.dram = nc, ctx, dram

    def sb(name, cols):
        return ctx.enter_context(nc.sbuf_tensor(name, [P, cols], F32))

    m.xt = sb("residual", KD * TOK)
    m.ht = sb("hidden", KD * TOK)
    m.ring = sb("weight_ring", SLOTS * SLOT)
    m.work = sb("work", 19500)
    m.const = sb("constants", C_ALL)
    m.small = sb("small_inputs", S_ALL)
    m.mod = sb("modulation", 2 * 48 * 2)
    m.moda = sb("modulation_scale", 2 * 2 * KD * 2)
    m.psum = [ctx.enter_context(nc.psum_tensor(f"bank{i}", [P, BANK], F32)) for i in range(8)]
    m.X = m.xt[:, :].rearrange("p (k t) -> p k t", k=KD)
    m.H = m.ht[:, :].rearrange("p (k t) -> p k t", k=KD)
    m.MOD = m.mod[:, :].rearrange("p (l c k v) -> p l c k v", l=2, c=6, k=KD)
    m.MODA = m.moda[:, :].rearrange("p (l n k v) -> p l n k v", l=2, n=2, k=KD)
    return m


def cut(m, at, cols):
    return m.work[:, at:at + cols]


def const(m, at, cols=P):
    return m.const[:, at:at + cols]


def semaphores(m, phase, names):
    return [m.ctx.enter_context(m.nc.semaphore(f"{phase}_{n}")) for n in names.split()]


def slot(m, n):
    return m.ring[:, n * SLOT:(n + 1) * SLOT]


def load_and_modulation(m):
    nc, dram = m.nc, m.dram
    (small_in, tokens_in, turned, even_out, odd_out, silu_c, slab_used, mod_sum, mod_scale) = semaphores(
        m, "in", "small_in tokens_in turned even_out odd_out silu_c slab_used mod_sum mod_scale")
    slab_in = semaphores(m, "in", " ".join(f"slab_in{n}" for n in range(SLOTS)))
    raw = cut(m, 0, 6 * D).rearrange("p (t d) -> p t d", t=6)
    sig = cut(m, 6 * D, 2 * KD)
    sc = cut(m, 6 * D + 2 * KD, 2 * KD)
    ident = const(m, C_IDENT)
    lat = dram["x"][0].rearrange("(r c) d -> c r d", c=GRID_C)
    adaw = dram["ada_w"].rearrange("l (k p) n -> l p k n", p=P)
    slabs = 12

    with nc.Block() as block:

        @block.sync
        def _(sp):
            sp.dma_start(m.small[:, :], dram["small"]).then_inc(small_in, 16)
            sp.dma_start(m.const[:, :], dram["const"]).then_inc(small_in, 16)
            for t in range(6):
                src = dram["ctx"][0, t * P:(t + 1) * P, :] if t < 2 else lat[16 * (t - 2):16 * (t - 1)]
                sp.dma_start(raw[:, t, :], src).then_inc(tokens_in, 16)
            for l in range(2):
                with sp.Fori(0, slabs // SLOTS) as i:
                    for s in range(SLOTS):
                        sp.wait_ge(slab_used, i * SLOTS + (l * slabs + s + 1))
                        sp.dma_start(slot(m, s).rearrange("p (k n) -> p k n", k=KD),
                                     adaw[l][:, :, bass.ds(i * (SLOTS * BANK) + s * BANK, BANK)]).then_inc(slab_in[s], 16)

        @block.tensor
        def _(pe):
            pe.sem_inc(slab_used, SLOTS)
            pe.wait_ge(small_in, 32)
            pe.wait_ge(tokens_in, 96)
            for n in range(12):
                if n >= 6:
                    pe.wait_ge((even_out, odd_out)[n % 2], (n - 6) // 2 + 1)
                for k in range(4):
                    mm = nc.tensor.transpose(m.psum[n % 6][:, k * P:(k + 1) * P],
                                             raw[:, n // 2, (4 * (n % 2) + k) * P:(4 * (n % 2) + k + 1) * P], ident)
                mm.then_inc(turned, 1)
            pe.wait_ge(silu_c, 2)
            for l in range(2):
                with pe.Fori(0, slabs // SLOTS) as i:
                    for s in range(SLOTS):
                        pe.wait_ge(slab_in[s], i * 16 + (l * (slabs // SLOTS) * 16 + 16))
                        w = slot(m, s).rearrange("p (k n) -> p k n", k=KD)
                        for g in range(4):
                            for k in range(KD):
                                mm = nc.tensor.matmul(
                                    m.psum[6 + l][:, bass.ds(i * (8 * SLOTS) + (s * 4 + g) * 2, 2)],
                                    w[:, k, g * P:(g + 1) * P], sc[:, 2 * k:2 * k + 2], start=(k == 0), stop=(k == KD - 1))
                        mm.then_inc(slab_used, 1)

        @block.scalar
        def _(act):
            act.wait_ge(small_in, 32)
            nc.scalar.activation(sig, m.small[:, S_C:S_C + 2 * KD], ACT.Sigmoid).then_inc(silu_c, 1)
            for n in range(1, 12, 2):
                act.wait_ge(turned, n + 1)
                nc.scalar.copy(m.X[:, 4:8, (n // 2) * P:(n // 2 + 1) * P],
                               m.psum[n % 6][:, :].rearrange("p (k t) -> p k t", k=4)).then_inc(odd_out, 1)

        @block.vector
        def _(dve):
            dve.wait_ge(silu_c, 1)
            nc.vector.tensor_tensor(sc, sig, m.small[:, S_C:S_C + 2 * KD], ALU.mult).then_inc(silu_c, 1)
            for n in range(0, 12, 2):
                dve.wait_ge(turned, n + 1)
                nc.vector.tensor_copy(m.X[:, 0:4, (n // 2) * P:(n // 2 + 1) * P],
                                      m.psum[n % 6][:, :].rearrange("p (k t) -> p k t", k=4)).then_inc(even_out, 1)
            dve.wait_ge(slab_used, SLOTS + 2 * slabs)
            for l in range(2):
                b = m.small[:, S_ADAB + 48 * l:S_ADAB + 48 * l + 48].unsqueeze(2).broadcast_to([P, 48, 2])
                nc.vector.tensor_tensor(m.mod[:, 96 * l:96 * l + 96].rearrange("p (g v) -> p g v", v=2),
                                        m.psum[6 + l][:, 0:96].rearrange("p (g v) -> p g v", v=2), b, ALU.add).then_inc(mod_sum, 1)
            dve.wait_ge(mod_sum, 2)
            for l in range(2):
                for n in range(2):
                    g = m.small[:, S_NORM + (2 * l + n) * KD:S_NORM + (2 * l + n + 1) * KD]
                    nc.vector.scalar_tensor_tensor(
                        out=m.MODA[:, l, n], in0=m.MOD[:, l, 1 + 3 * n], scalar=1.0,
                        in1=g.unsqueeze(2).broadcast_to([P, KD, 2]), op0=ALU.add, op1=ALU.mult).then_inc(mod_scale, 1)


def norm_modulate(m, name, layer, norm, to_reference_order=False, first=0):
    nc = m.nc
    even_sq, odd_sq, summed, root, rstd_ok, scaled, hidden = semaphores(
        m, name, "even_sq odd_sq summed root rstd_ok scaled hidden")
    n_tok = TOK - first
    SQ = 4
    sq = cut(m, 0, SQ * TOK).rearrange("p (s t) -> p s t", s=SQ)
    rstd = cut(m, SQ * TOK, TOK)
    norm_x = cut(m, (SQ + 1) * TOK, KD * TOK).rearrange("p (k t) -> p k t", k=KD)
    parts = [(256, 768, 0)] + ([(0, 256, 1)] if first == 0 else [])
    with nc.Block() as block:

        @block.gpsimd
        def _(pool):
            for k in range(0, KD, 2):
                if k >= SQ:
                    pool.wait_ge(summed, k - SQ + 1)
                nc.gpsimd.tensor_tensor(sq[:, k % SQ, first:TOK], m.X[:, k, first:TOK], m.X[:, k, first:TOK],
                                        ALU.mult).then_inc(even_sq, 1)

        @block.tensor
        def _(pe):
            for k in range(KD):
                pe.wait_ge((even_sq, odd_sq)[k % 2], k // 2 + 1)
                for b, (t0, t1, _) in enumerate(parts):
                    mm = nc.tensor.matmul(m.psum[b][:, 0:t1 - t0], const(m, C_MEAN), sq[:, k % SQ, t0:t1],
                                          start=(k == 0), stop=(k == KD - 1))
                mm.then_inc(summed, 1)

        @block.scalar
        def _(act):
            for k in range(1, KD, 2):
                if k >= SQ:
                    act.wait_ge(summed, k - SQ + 1)
                nc.scalar.activation(sq[:, k % SQ, first:TOK], m.X[:, k, first:TOK], ACT.Square).then_inc(odd_sq, 1)
            act.wait_ge(summed, KD)
            for b, (t0, t1, _) in enumerate(parts):
                nc.scalar.activation(rstd[:, t0:t1], m.psum[b][:, 0:t1 - t0], ACT.Sqrt,
                                     bias=const(m, C_EPS, 1)).then_inc(root, 1)
            for k in range(KD):
                act.wait_ge(scaled, k + 1)
                for t0, t1, v in parts:
                    src, dst = norm_x[:, k, t0:t1], m.H[:, k, t0:t1]
                    if to_reference_order and v == 0:
                        src = src.rearrange("p (c r) -> p r c", r=GRID_R)
                        dst = dst.rearrange("p (r c) -> p r c", r=GRID_R)
                    nc.scalar.activation(dst, src, ACT.Identity, bias=m.MOD[:, layer, 3 * norm, k, v:v + 1],
                                         scale=m.MODA[:, layer, norm, k, v:v + 1]).then_inc(hidden, 1)

        @block.vector
        def _(dve):
            dve.wait_ge(root, len(parts))
            nc.vector.reciprocal(rstd[:, first:TOK], rstd[:, first:TOK]).then_inc(rstd_ok, 1)
            dve.wait_ge(rstd_ok, 1)
            for k in range(KD):
                nc.vector.tensor_tensor(norm_x[:, k, first:TOK], m.X[:, k, first:TOK], rstd[:, first:TOK],
                                        ALU.mult).then_inc(scaled, 1)


def neighbourhood_attention(m):
    nc, dram = m.nc, m.dram
    (projected, squared, stat, root, inv, qk_ready, v_ready, shifted, bias_ready, scored, biased, staged, maxed, exped, inverted, probs,
     turned, turned_out, weighted, out_copied, w_free, bias_free) = semaphores(
        m, "na", "projected squared stat root inv qk_ready v_ready shifted bias_ready scored biased staged maxed exped inverted probs "
                 "turned turned_out weighted out_copied w_free bias_free")
    w_in = semaphores(m, "na", "w_in0 w_in1")
    bias_in, = semaphores(m, "na", "bias_in")
    at = [0]

    def area(cols):
        at[0] += cols
        return cut(m, at[0] - cols, cols)

    m.O = area(KD * TOK).rearrange("p (k t) -> p k t", k=KD)
    m.O_first = 0
    q, k_, sq, rs = (area(TOK) for _ in range(4))
    sq2, rs2 = area(TOK), area(TOK)
    v = area(TOK).rearrange("p (t n) -> p t n", t=6)
    vs = area(3 * P).rearrange("p (t n) -> p t n", t=3)
    table = area(2 * BIAS_RUN).rearrange("p (h n) -> p h n", h=2)
    bm = area(6 * WIN).rearrange("p (h v n) -> p h v n", h=2, v=3)
    NS = 3
    S = area(NS * BANK).rearrange("p (s n) -> p s n", s=NS)
    PT = area(2 * BANK).rearrange("p (s n) -> p s n", s=2)
    stats = area(4 * NS)
    assert at[0] <= 19500
    ident = const(m, C_IDENT)
    wv = dram["na_w_qkv"].rearrange("(k p) (s n) -> p s k n", p=P, s=3)
    UNITS = [(h, j) for h in range(2) for j in range(6)]
    PAIRS_IN_BODY = 2

    def bias_source(pair, h):
        return bass.AP(tensor=dram["bias"].tensor, offset=(pair * 2 + h) * (BIAS_DC * DR),
                       ap=[[DR, 16], [1, 8], [1, BIAS_RUN]])

    with nc.Block() as block:

        @block.sync
        def _(sp):
            with sp.Fori(0, NA_PAIRS // PAIRS_IN_BODY) as i:
                for u in range(PAIRS_IN_BODY):
                    pair = i * PAIRS_IN_BODY + u
                    sp.wait_ge(w_free, pair + 1)
                    for s in range(3):
                        sp.dma_start(slot(m, u)[:, s * KD * P:(s + 1) * KD * P].rearrange("p (k n) -> p k n", k=KD),
                                     wv[:, s, :, bass.ds(pair * P, P)]).then_inc(w_in[u], 16)
                    sp.wait_ge(bias_free, pair + 1)
                    for h in range(2):
                        sp.dma_start(table[:, h, :], bias_source(pair, h)).then_inc(bias_in, 16)
                    sp.wait_ge(v_ready, pair * 2 + 2)
                    sp.wait_ge(weighted, pair * 12 + 1)
                    sp.dma_start(vs[0:64, :, :], v[64:128, 2:5, :]).then_inc(shifted, 16)
                    sp.dma_start(vs[64:128, :, :], v[0:64, 3:6, :]).then_inc(shifted, 16)

        @block.gpsimd
        def _(pool):
            pool.sem_inc(bias_free, 1)
            with pool.Fori(0, NA_PAIRS) as pair:
                pool.wait_ge(bias_in, pair * 32 + 32)
                pool.wait_ge(staged, pair * 12 + 1)
                for h in range(2):
                    for var in range(3):
                        src = table[:, h, :].rearrange("p (c r) -> p c r", r=DR)
                        last = 47 - WIN_SHIFT[var]
                        src = src[:, last - 31:last + 1, 0:WIN_R][:, ::-1, ::-1]
                        mask = const(m, C_WMASK + 32 * var, 32).unsqueeze(2).broadcast_to([P, 32, WIN_R])
                        op = nc.gpsimd.tensor_tensor(bm[:, h, var, :].rearrange("p (c r) -> p c r", r=WIN_R),
                                                     src, mask, ALU.add)
                        op.then_inc(bias_ready, 1)
                pool.wait_ge(bias_ready, pair * 6 + 6)
                pool.sem_inc(bias_free, 1)

        @block.tensor
        def _(pe):
            pe.sem_inc(weighted, 1)
            pe.sem_inc(stat, 1)

            def proj(bank, c0, w, t0, t1):
                for k in range(KD):
                    mm = nc.tensor.matmul(m.psum[bank][:, c0:c0 + t1 - t0], w[:, k, :], m.H[:, k, t0:t1],
                                          start=(k == 0), stop=(k == KD - 1))
                return mm

            with pe.Fori(0, NA_PAIRS // PAIRS_IN_BODY) as i:
                for u in range(PAIRS_IN_BODY):
                    pair = i * PAIRS_IN_BODY + u
                    w = [slot(m, u)[:, s * KD * P:(s + 1) * KD * P].rearrange("p (k n) -> p k n", k=KD) for s in range(3)]
                    pe.wait_ge(w_in[u], i * 48 + 48)
                    pe.wait_ge(out_copied, pair * 2 + 1)
                    proj(0, 0, w[0], CTX, TOK).then_inc(projected, 1)
                    proj(1, 0, w[1], CTX, TOK).then_inc(projected, 1)
                    proj(2, 0, w[0], 0, CTX)
                    proj(2, CTX, w[1], 0, CTX).then_inc(projected, 1)
                    for t in range(6):
                        for k in range(KD):
                            mm = nc.tensor.matmul(m.psum[3 + t // 4][:, (t % 4) * P:(t % 4 + 1) * P], m.H[:, k, t * P:(t + 1) * P],
                                                  w[2][:, k, :], start=(k == 0), stop=(k == KD - 1))
                        if t == 3:
                            mm.then_inc(projected, 1)
                    mm.then_inc(projected, 1)
                    for n, src in enumerate((sq[:, CTX:TOK], sq2[:, CTX:TOK], None)):
                        pe.wait_ge(squared, pair * 4 + (n + 1 if n < 2 else 4))
                        if n < 2:
                            nc.tensor.matmul(m.psum[5 + n][:, :], const(m, C_HALF), src, start=True, stop=True).then_inc(stat, 1)
                        else:
                            nc.tensor.matmul(m.psum[7][:, 0:CTX], const(m, C_HALF), sq[:, 0:CTX], start=True, stop=True)
                            nc.tensor.matmul(m.psum[7][:, CTX:2 * CTX], const(m, C_HALF), sq2[:, 0:CTX],
                                             start=True, stop=True).then_inc(stat, 1)

                    def scores(n):
                        h, j = UNITS[n]
                        at_h = slice(64 * h, 64 * h + 64)
                        if n >= 2:
                            pe.wait_ge(staged, pair * 12 + n)
                        out = m.psum[n % 2]
                        qs = q[at_h, CTX + j * P:CTX + (j + 1) * P] if j < 4 else q[at_h, (j - 4) * P:(j - 3) * P]
                        if j < 4:
                            k0 = CTX + WIN_START[j]
                            nc.tensor.matmul(out[:, 0:WIN], qs, k_[at_h, k0:k0 + WIN], start=True, stop=True)
                        nc.tensor.matmul(out[:, WIN:WIN + CTX], qs, k_[at_h, 0:CTX], start=True, stop=True).then_inc(scored, 1)

                    def turn(n):
                        pe.wait_ge(probs, pair * 12 + n + 1)
                        if n >= 2:
                            pe.wait_ge(turned_out, pair * 12 + n)
                        for c in range(0 if UNITS[n][1] < 4 else 2, 4):
                            mm = nc.tensor.transpose(m.psum[(5, 6)[n % 2]][:, c * P:(c + 1) * P], S[:, n % NS, c * P:(c + 1) * P], ident)
                        mm.then_inc(turned, 1)

                    def weigh(n):
                        h, j = UNITS[n]
                        pe.wait_ge(turned_out, pair * 12 + n + 2)
                        if j < 4:
                            near = [(v, 2), (vs, 0), (vs, 1), (v, 4)][j]
                            vals = [near[0][:, near[1], :], near[0][:, near[1] + 1, :], v[:, 0, :], v[:, 1, :]]
                            out = m.psum[3][64 * h:64 * h + 64, j * P:(j + 1) * P]
                            chunks = range(4)
                        else:
                            vals = [None, None, v[:, 0, :], v[:, 1, :]]
                            out = m.psum[4][64 * h:64 * h + 64, (j - 4) * P:(j - 3) * P]
                            chunks = range(2, 4)
                        for c in chunks:
                            mm = nc.tensor.matmul(out, vals[c][:, 64 * h:64 * h + 64], PT[:, n % 2, c * P:(c + 1) * P],
                                                  start=(c == chunks[0]), stop=(c == 3))
                        mm.then_inc(weighted, 1)

                    pe.wait_ge(qk_ready, pair * 4 + 4)
                    scores(0)
                    scores(1)
                    pe.wait_ge(v_ready, pair * 2 + 2)
                    pe.wait_ge(shifted, pair * 32 + 32)
                    for n in range(12):
                        turn(n)
                        if n + 2 < 12:
                            scores(n + 2)
                        if n:
                            weigh(n - 1)
                    weigh(11)

        @block.scalar
        def _(act):
            act.sem_inc(turned_out, 1)
            act.sem_inc(w_free, 2)
            with act.Fori(0, NA_PAIRS) as pair:
                act.wait_ge(projected, pair * 5 + 1)
                act.wait_ge(stat, pair * 3 + 1)
                nc.scalar.activation(sq[:, CTX:TOK], m.psum[0][:, :], ACT.Square).then_inc(squared, 1)
                act.wait_ge(projected, pair * 5 + 2)
                nc.scalar.activation(sq2[:, CTX:TOK], m.psum[1][:, :], ACT.Square).then_inc(squared, 1)
                act.wait_ge(projected, pair * 5 + 3)
                nc.scalar.activation(sq[:, 0:CTX], m.psum[2][:, 0:CTX], ACT.Square).then_inc(squared, 1)
                nc.scalar.activation(sq2[:, 0:CTX], m.psum[2][:, CTX:2 * CTX], ACT.Square).then_inc(squared, 1)
                act.wait_ge(weighted, pair * 12 + 1)
                act.wait_ge(projected, pair * 5 + 5)
                act.sem_inc(w_free, 1)
                nc.scalar.copy(v[:, 0:4, :], m.psum[3][:, :].rearrange("p (t n) -> p t n", t=4)).then_inc(v_ready, 1)
                nc.scalar.copy(v[:, 4:6, :], m.psum[4][:, 0:2 * P].rearrange("p (t n) -> p t n", t=2)).then_inc(v_ready, 1)
                e1, e64 = const(m, C_EPS, 1), const(m, C_EPS + 1, 1)
                for n, (dst, src, scale, eps) in enumerate((
                        (rs[:, CTX:TOK], m.psum[5][:, :], 64.0, e64), (rs2[:, CTX:TOK], m.psum[6][:, :], 1.0, e1),
                        (rs[:, 0:CTX], m.psum[7][:, 0:CTX], 64.0, e64), (rs2[:, 0:CTX], m.psum[7][:, CTX:2 * CTX], 1.0, e1))):
                    act.wait_ge(stat, pair * 3 + min(n, 2) + 2)
                    nc.scalar.activation(dst, src, ACT.Sqrt, bias=eps, scale=scale).then_inc(root, 1)

                def exp(n):
                    lo = 0 if UNITS[n][1] < 4 else WIN
                    b = 4 * (n % NS)
                    act.wait_ge(maxed, pair * 12 + n + 1)
                    nc.scalar.activation(S[:, n % NS, lo:BANK], S[:, n % NS, lo:BANK], ACT.Exp,
                                         bias=stats[:, b:b + 1], accum_out=stats[:, b + 2:b + 3]).then_inc(exped, 1)

                def copy_out(n):
                    lo = 0 if UNITS[n][1] < 4 else WIN
                    act.wait_ge(turned, pair * 12 + n + 1)
                    if n >= 2:
                        act.wait_ge(weighted, pair * 12 + n)
                    nc.scalar.copy(PT[:, n % 2, lo:BANK], m.psum[(5, 6)[n % 2]][:, lo:BANK]).then_inc(turned_out, 1)

                exp(0)
                for n in range(12):
                    if n + 1 < 12:
                        exp(n + 1)
                    copy_out(n)

        @block.vector
        def _(dve):
            dve.sem_inc(out_copied, 1)
            dve.sem_inc(staged, 1)
            with dve.Fori(0, NA_PAIRS) as pair:
                srcs = ((q, rs, CTX, TOK, m.psum[0][:, :], 0), (k_, rs2, CTX, TOK, m.psum[1][:, :], 1),
                        (q, rs, 0, CTX, m.psum[2][:, 0:CTX], 0), (k_, rs2, 0, CTX, m.psum[2][:, CTX:2 * CTX], 1))
                for n, (dst, r, t0, t1, src, g) in enumerate(srcs):
                    dve.wait_ge(root, pair * 4 + n + 1)
                    nc.vector.reciprocal(r[:, t0:t1], r[:, t0:t1]).then_inc(inv, 1)
                    dve.wait_ge(inv, pair * 4 + n + 1)
                    nc.vector.scalar_tensor_tensor(out=dst[:, t0:t1], in0=src, scalar=m.small[:, S_QN + g:S_QN + g + 1],
                                                   in1=r[:, t0:t1], op0=ALU.mult, op1=ALU.mult).then_inc(qk_ready, 1)

                def stage(n):
                    h, j = UNITS[n]
                    b = 4 * (n % NS)
                    lo = 0 if j < 4 else WIN
                    dve.wait_ge(scored, pair * 12 + n + 1)
                    if n >= NS:
                        dve.wait_ge(turned, pair * 12 + n - NS + 1)
                    if n == 0:
                        dve.wait_ge(bias_ready, pair * 6 + 6)
                    if j < 4:
                        nc.vector.tensor_tensor(S[:, n % NS, 0:WIN], m.psum[n % 2][:, 0:WIN], bm[:, h, WIN_VARIANT[j], :],
                                                ALU.add).then_inc(biased, 1)
                    nc.vector.tensor_copy(S[:, n % NS, WIN:BANK], m.psum[n % 2][:, WIN:BANK]).then_inc(staged, 1)
                    if j < 4:
                        dve.wait_ge(biased, pair * 8 + 4 * h + j + 1)
                    dve.wait_ge(staged, pair * 12 + n + 2)
                    nc.vector.tensor_reduce(stats[:, b:b + 1], S[:, n % NS, lo:BANK], AX.X, ALU.max, negate=True).then_inc(maxed, 1)

                def normalise(n):
                    b = 4 * (n % NS)
                    lo = 0 if UNITS[n][1] < 4 else WIN
                    dve.wait_ge(exped, pair * 12 + n + 1)
                    nc.vector.reciprocal(stats[:, b + 3:b + 4], stats[:, b + 2:b + 3]).then_inc(inverted, 1)
                    dve.wait_ge(inverted, pair * 12 + n + 1)
                    nc.vector.tensor_scalar(S[:, n % NS, lo:BANK], S[:, n % NS, lo:BANK], stats[:, b + 3:b + 4], None,
                                            ALU.mult).then_inc(probs, 1)

                order = [("s", 0)]
                for n in range(12):
                    order += ([("s", n + 1)] if n + 1 < 12 else []) + [("n", n)]
                for what, n in order:
                    (stage if what == "s" else normalise)(n)
                dve.wait_ge(weighted, pair * 12 + 13)
                nc.vector.tensor_copy(m.O[:, bass.ds(pair, 1), CTX:TOK], m.psum[3][:, :].unsqueeze(1)).then_inc(out_copied, 1)
                nc.vector.tensor_copy(m.O[:, bass.ds(pair, 1), 0:CTX], m.psum[4][:, 0:CTX].unsqueeze(1)).then_inc(out_copied, 1)


def ring_steps(n_slabs, n_slots):
    steps = []
    for j in range(n_slabs):
        same = [x for x in range(n_slabs) if x % n_slots == j % n_slots]
        at = same.index(j)
        before = n_slabs + same[at - 1] + 1 if at else same[-1] + 1
        steps.append((j % n_slots, len(same), at + 1, before))
    return steps


def project_to_residual(m, name, weight, layer, first):
    nc = m.nc
    w_in = semaphores(m, name, "w_in0 w_in1")
    product, added = semaphores(m, name, "product added")
    parts = [(CTX, TOK, 0)] + ([(0, CTX, 1)] if first == 0 else [])
    w = weight.rearrange("(k p) n -> p k n", p=P)
    with nc.Block() as block:

        @block.sync
        def _(sp):
            for s in range(2):
                sp.dma_start(slot(m, s).rearrange("p (k n) -> p k n", k=KD), w[:, :, s * BANK:(s + 1) * BANK]).then_inc(w_in[s], 16)

        @block.tensor
        def _(pe):
            for g in range(KD):
                pe.wait_ge(w_in[g // 4], 16)
                if g >= 4:
                    pe.wait_ge(added, (g - 3) * len(parts))
                ws = slot(m, g // 4).rearrange("p (k n) -> p k n", k=KD)
                for b, (t0, t1, _) in enumerate(parts):
                    for k in range(KD):
                        mm = nc.tensor.matmul(m.psum[2 * (g % 4) + b][:, 0:t1 - t0], ws[:, k, (g % 4) * P:(g % 4 + 1) * P],
                                              m.O[:, k, t0 - m.O_first:t1 - m.O_first], start=(k == 0), stop=(k == KD - 1))
                    mm.then_inc(product, 1)

        @block.vector
        def _(dve):
            for g in range(KD):
                for b, (t0, t1, v) in enumerate(parts):
                    dve.wait_ge(product, g * len(parts) + b + 1)
                    nc.vector.scalar_tensor_tensor(out=m.X[:, g, t0:t1], in0=m.psum[2 * (g % 4) + b][:, 0:t1 - t0],
                                                   scalar=m.MOD[:, layer, 2, g, v:v + 1], in1=m.X[:, g, t0:t1],
                                                   op0=ALU.mult, op1=ALU.add).then_inc(added, 1)


def swiglu(m):
    nc, dram = m.nc, m.dram
    FK = FFN // P
    CHUNKS = 2
    w_in = semaphores(m, "ffn", "w_in0 w_in1")
    out_in = semaphores(m, "ffn", "out_in0 out_in1 out_in2 out_in3")
    product, gated, silu_ok, out_product, added = semaphores(m, "ffn", "product gated silu_ok out_product added")
    G = cut(m, 0, FK * TOK).rearrange("p (k t) -> p k t", k=FK)
    sa = cut(m, FK * TOK, 2 * TOK).rearrange("p (s t) -> p s t", s=2)
    wi = dram["ffn_w_in"][0].rearrange("(k p) (s n) -> p s k n", p=P, s=2)
    wo = dram["ffn_w_out"][0].rearrange("(k p) n -> p k n", p=P)
    half = KD * P

    def in_slab(s):
        return slot(m, s)[:, 0:2 * half].rearrange("p (s k n) -> p s k n", s=2, k=KD)

    def out_slab(s):
        return slot(m, s)[:, 0:FK * P].rearrange("p (k n) -> p k n", k=FK)

    with nc.Block() as block:

        @block.sync
        def _(sp):
            for g in range(2):
                sp.dma_start(out_slab(2 + g), wo[:, :, g * P:(g + 1) * P]).then_inc(out_in[g], 16)
            with sp.Fori(0, FK // CHUNKS) as i:
                for c in range(CHUNKS):
                    sp.wait_ge(gated, i * (2 * CHUNKS) + 2 * c + 2)
                    for ab in range(2):
                        sp.dma_start(in_slab(c)[:, ab], wi[:, ab, :, bass.ds(i * (CHUNKS * P) + c * P, P)]).then_inc(w_in[c], 16)
            for g in range(2, KD):
                if g < 4:
                    sp.wait_ge(gated, 2 * CHUNKS + 2 * (FK + g - 3))
                else:
                    sp.wait_ge(out_product, (g - 3) * 2)
                sp.dma_start(out_slab((g + 2) % 4), wo[:, :, g * P:(g + 1) * P]).then_inc(out_in[g % 4], 16)

        @block.tensor
        def _(pe):
            pe.sem_inc(gated, 2 * CHUNKS)
            with pe.Fori(0, FK // CHUNKS) as i:
                for c in range(CHUNKS):
                    pe.wait_ge(w_in[c], i * 32 + 32)
                    pe.wait_ge(gated, i * (2 * CHUNKS) + 2 * c + 2)
                    w, bank = in_slab(c), 4 * c
                    for ab in range(2):
                        for k in range(KD):
                            mm = nc.tensor.matmul(m.psum[bank + ab][:, :], w[:, ab, k, :], m.H[:, k, CTX:TOK],
                                                  start=(k == 0), stop=(k == KD - 1))
                    mm.then_inc(product, 1)
                    for ab in range(2):
                        for k in range(KD):
                            mm = nc.tensor.matmul(m.psum[bank + 2 + ab][:, 0:CTX], w[:, ab, k, :], m.H[:, k, 0:CTX],
                                                  start=(k == 0), stop=(k == KD - 1))
                    mm.then_inc(product, 1)
            for g in range(KD):
                pe.wait_ge(out_in[g % 4], 16 * (g // 4 + 1))
                if g < 4:
                    pe.wait_ge(gated, 2 * FK + 2 * CHUNKS)
                else:
                    pe.wait_ge(added, (g - 3) * 2)
                for b, (t0, t1) in enumerate(((CTX, TOK), (0, CTX))):
                    for k in range(FK):
                        mm = nc.tensor.matmul(m.psum[2 * (g % 4) + b][:, 0:t1 - t0], out_slab((g + 2) % 4)[:, k, :], G[:, k, t0:t1],
                                              start=(k == 0), stop=(k == FK - 1))
                    mm.then_inc(out_product, 1)

        @block.scalar
        def _(act):
            with act.Fori(0, FK // CHUNKS) as i:
                for c in range(CHUNKS):
                    act.wait_ge(gated, i * (2 * CHUNKS) + 2 * c + 2)
                    for b, (t0, t1) in enumerate(((CTX, TOK), (0, CTX))):
                        act.wait_ge(product, i * (2 * CHUNKS) + 2 * c + b + 1)
                        nc.scalar.activation(sa[:, c, t0:t1], m.psum[4 * c + 2 * b][:, 0:t1 - t0], ACT.Silu).then_inc(silu_ok, 1)

        @block.vector
        def _(dve):
            with dve.Fori(0, FK // CHUNKS) as i:
                for c in range(CHUNKS):
                    for b, (t0, t1) in enumerate(((CTX, TOK), (0, CTX))):
                        dve.wait_ge(silu_ok, i * (2 * CHUNKS) + 2 * c + b + 1)
                        nc.vector.tensor_tensor(G[:, bass.ds(i * CHUNKS + c, 1), t0:t1], sa[:, c, t0:t1].unsqueeze(1),
                                                m.psum[4 * c + 2 * b + 1][:, 0:t1 - t0].unsqueeze(1), ALU.mult).then_inc(gated, 1)
            for g in range(KD):
                for b, (t0, t1) in enumerate(((CTX, TOK), (0, CTX))):
                    dve.wait_ge(out_product, 2 * g + b + 1)
                    nc.vector.scalar_tensor_tensor(out=m.X[:, g, t0:t1], in0=m.psum[2 * (g % 4) + b][:, 0:t1 - t0],
                                                   scalar=m.MOD[:, 0, 5, g, b:b + 1], in1=m.X[:, g, t0:t1],
                                                   op0=ALU.mult, op1=ALU.add).then_inc(added, 1)


def reorder(m):
    nc = m.nc
    copied, = semaphores(m, "reorder", "copied")
    back, = semaphores(m, "reorder", "back")
    tmp = cut(m, 0, KD * LAT).rearrange("p (k t) -> p k t", k=KD)
    with nc.Block() as block:

        @block.vector
        def _(dve):
            for k in range(KD):
                nc.vector.tensor_copy(tmp[:, k, :].rearrange("p (r c) -> p r c", c=GRID_C),
                                      m.X[:, k, CTX:TOK].rearrange("p (c r) -> p r c", r=GRID_R)).then_inc(copied, 1)

        @block.scalar
        def _(act):
            for k in range(KD):
                act.wait_ge(copied, k + 1)
                nc.scalar.copy(m.X[:, k, CTX:TOK], tmp[:, k, :]).then_inc(back, 1)


def experts(m):
    nc, dram = m.nc, m.dram
    EK = EFF // P
    w_in = semaphores(m, "moe", "w_in0 w_in1 w_in2 w_in3")
    out_in = semaphores(m, "moe", "out_in0 out_in1 out_in2 out_in3")
    (logits, logits_ok, top, weights, route_exp, routed, spread, spread_ok, used, out_used, product, silu_ok, weighted, gated,
     out_product, added) = semaphores(
        m, "moe", "logits logits_ok top weights route_exp routed spread spread_ok used out_used product silu_ok weighted gated "
                  "out_product added")
    at = [0]

    def area(cols):
        at[0] += cols
        return cut(m, at[0] - cols, cols)

    G = area(EK * LAT).rearrange("p (k t) -> p k t", k=EK)
    sa = area(2 * LAT).rearrange("p (s t) -> p s t", s=2)
    sg = area(2 * LAT).rearrange("p (s t) -> p s t", s=2)
    route = area(EXPERTS * LAT).rearrange("p (e t) -> p e t", e=EXPERTS)
    lg = area(4 * 8).rearrange("p (t e) -> p t e", t=4)
    top8 = area(4 * 8).rearrange("p (t e) -> p t e", t=4)
    idx = area(4 * 8).bitcast(U32).rearrange("p (t e) -> p t e", t=4)
    idxf = area(4 * 8).rearrange("p (t e) -> p t e", t=4)
    eq = area(2 * 4 * 8).rearrange("p (w t e) -> p w t e", w=2, t=4)
    gate = area(4 * 8).rearrange("p (t e) -> p t e", t=4)
    small = area(4 * 4).rearrange("p (w t) -> p w t", w=4)
    half = KD * P
    IN_SLOTS, OUT_SLOTS = 4, 4

    def in_slab(s):
        return m.ring[:, s * 2 * half:(s + 1) * 2 * half].rearrange("p (s k n) -> p s k n", s=2, k=KD)

    def out_slab(s):
        o = IN_SLOTS * 2 * half + s * EK * P
        return m.ring[:, o:o + EK * P].rearrange("p (k n) -> p k n", k=EK)

    wi = dram["moe_w_in"].rearrange("l e (k p) (s n) -> (l e) p s k n", p=P, s=2)
    wo = dram["moe_w_out"].rearrange("l e (k p) n -> (l e) p k n", p=P)
    in_steps, out_steps = ring_steps(EK, IN_SLOTS), ring_steps(KD, OUT_SLOTS)

    with nc.Block() as block:

        @block.sync
        def _(sp):
            with sp.Fori(0, EXPERTS) as e:
                for j, (s, _, _, before) in enumerate(in_steps):
                    sp.wait_ge(used, e * EK + before)
                    for ab in range(2):
                        sp.dma_start(in_slab(s)[:, ab], wi[bass.ds(e, 1), :, ab, :, j * P:(j + 1) * P].rearrange("o p k n -> (o p) k n"))\
                            .then_inc(w_in[s], 16)
                for j, (s, _, _, before) in enumerate(out_steps):
                    sp.wait_ge(out_used, e * KD + before)
                    sp.dma_start(out_slab(s), wo[bass.ds(e, 1), :, :, j * P:(j + 1) * P].rearrange("o p k n -> (o p) k n"))\
                        .then_inc(out_in[s], 16)

        @block.tensor
        def _(pe):
            pe.sem_inc(used, EK)
            pe.sem_inc(out_used, KD)
            pe.sem_inc(gated, EK)
            for t in range(4):
                for k in range(KD):
                    mm = nc.tensor.matmul(m.psum[6][:, 8 * t:8 * t + 8], m.H[:, k, CTX + t * P:CTX + (t + 1) * P],
                                          m.small[:, S_RT + 8 * k:S_RT + 8 * k + 8], start=(k == 0), stop=(k == KD - 1))
            mm.then_inc(logits, 1)
            pe.wait_ge(routed, 2)
            for e in range(EXPERTS):
                if e >= 2:
                    pe.wait_ge(spread_ok, e - 1)
                for t in range(4):
                    mm = nc.tensor.matmul(m.psum[e % 2][:, t * P:(t + 1) * P], gate[:, t, e:e + 1].to_broadcast([P, P]),
                                          const(m, C_IDENT), start=True, stop=True)
                mm.then_inc(spread, 1)
            pe.wait_ge(spread_ok, EXPERTS)
            with pe.Fori(0, EXPERTS) as e:
                for j, (s, per, upto, _) in enumerate(in_steps):
                    pe.wait_ge(w_in[s], e * (32 * per) + 32 * upto)
                    pe.wait_ge(gated, e * EK + EK + j - 1)
                    for ab in range(2):
                        for k in range(KD):
                            mm = nc.tensor.matmul(m.psum[2 * (j % 2) + ab][:, :], in_slab(s)[:, ab, k, :], m.H[:, k, CTX:TOK],
                                                  start=(k == 0), stop=(k == KD - 1))
                    mm.then_inc(used, 1)
                for j, (s, per, upto, _) in enumerate(out_steps):
                    pe.wait_ge(out_in[s], e * (16 * per) + 16 * upto)
                    pe.wait_ge(added, e * KD + 4 + j + 1)
                    for k in range(EK):
                        if j == 0 and k in (EK - 2, EK - 1):
                            pe.wait_ge(gated, e * EK + EK + k + 1)
                        mm = nc.tensor.matmul(m.psum[4 + j % 4][:, :], out_slab(s)[:, k, :], G[:, k, :],
                                              start=(k == 0), stop=(k == EK - 1))
                    mm.then_inc(out_used, 1)

        @block.scalar
        def _(act):
            act.wait_ge(weights, 1)
            nc.scalar.activation(small[:, 1, :], small[:, 0, :], ACT.Exp).then_inc(route_exp, 1)
            act.wait_ge(spread_ok, EXPERTS)
            act.sem_inc(weighted, 2)
            with act.Fori(0, EXPERTS) as e:
                for j in range(EK):
                    act.wait_ge(used, e * EK + EK + j + 1)
                    act.wait_ge(weighted, e * EK + j + 1)
                    nc.scalar.activation(sa[:, j % 2, :], m.psum[2 * (j % 2)][:, :], ACT.Silu).then_inc(silu_ok, 1)

        @block.vector
        def _(dve):
            n = 0
            dve.sem_inc(added, KD)
            dve.wait_ge(logits, 1)
            nc.vector.tensor_copy(lg, m.psum[6][:, 0:32].rearrange("p (t e) -> p t e", t=4)).then_inc(logits_ok, 1)
            dve.wait_ge(logits_ok, 1)
            for t in range(4):
                nc.vector.max(top8[:, t, :], lg[:, t, :]).then_inc(top, 1)
            dve.wait_ge(top, 4)
            for t in range(4):
                nc.vector.max_index(idx[:, t, :], top8[:, t, :], lg[:, t, :]).then_inc(top, 1)
            nc.vector.tensor_tensor(small[:, 0, :], top8[:, :, 1], top8[:, :, 0], ALU.subtract).then_inc(weights, 1)
            dve.wait_ge(top, 8)
            nc.vector.tensor_copy(idxf, idx).then_inc(top, 1)
            dve.wait_ge(top, 9)
            iota = const(m, C_IOTA, EXPERTS).unsqueeze(1).broadcast_to([P, 4, EXPERTS])
            for w in range(2):
                nc.vector.tensor_tensor(eq[:, w], idxf[:, :, w:w + 1].broadcast_to([P, 4, EXPERTS]), iota, ALU.is_equal).then_inc(top, 1)
            dve.wait_ge(route_exp, 1)
            nc.vector.tensor_scalar(small[:, 2, :], small[:, 1, :], 1.0, None, ALU.add).then_inc(weights, 1)
            dve.wait_ge(weights, 2)
            nc.vector.reciprocal(small[:, 2, :], small[:, 2, :]).then_inc(weights, 1)
            dve.wait_ge(weights, 3)
            nc.vector.tensor_tensor(small[:, 3, :], small[:, 1, :], small[:, 2, :], ALU.mult).then_inc(weights, 1)
            dve.wait_ge(weights, 4)
            dve.wait_ge(top, 11)
            for w in range(2):
                nc.vector.tensor_tensor(eq[:, w], eq[:, w], small[:, 2 + w, :].unsqueeze(2).broadcast_to([P, 4, EXPERTS]),
                                        ALU.mult).then_inc(top, 1)
            dve.wait_ge(top, 13)
            nc.vector.tensor_tensor(gate, eq[:, 0], eq[:, 1], ALU.add).then_inc(routed, 2)
            for e in range(EXPERTS):
                dve.wait_ge(spread, e + 1)
                nc.vector.tensor_copy(route[:, e, :], m.psum[e % 2][:, :]).then_inc(spread_ok, 1)
            with dve.Fori(0, EXPERTS) as e:
                for j in range(EK):
                    dve.wait_ge(silu_ok, e * EK + j + 1)
                    nc.vector.tensor_tensor(sg[:, j % 2, :].unsqueeze(1), sa[:, j % 2, :].unsqueeze(1), route[:, bass.ds(e, 1), :],
                                            ALU.mult).then_inc(weighted, 1)
                    dve.wait_ge(weighted, e * EK + j + 3)
                    dve.wait_ge(out_used, e * KD + KD)
                    nc.vector.tensor_tensor(G[:, j, :], sg[:, j % 2, :], m.psum[2 * (j % 2) + 1][:, :], ALU.mult).then_inc(gated, 1)
                for j in range(KD):
                    dve.wait_ge(out_used, e * KD + KD + j + 1)
                    nc.vector.scalar_tensor_tensor(out=m.X[:, j, CTX:TOK], in0=m.psum[4 + j % 4][:, :], scalar=m.MOD[:, 1, 5, j, 0:1],
                                                   in1=m.X[:, j, CTX:TOK], op0=ALU.mult, op1=ALU.add).then_inc(added, 1)


def store(m):
    nc = m.nc
    turned, even_out, odd_out, stored = semaphores(m, "store", "turned even_out odd_out stored")
    rows = cut(m, 0, 4 * D).rearrange("p (t d) -> p t d", t=4)
    with nc.Block() as block:

        @block.tensor
        def _(pe):
            for n in range(8):
                for k in range(4):
                    mm = nc.tensor.transpose(m.psum[n][:, k * P:(k + 1) * P],
                                             m.X[:, 4 * (n % 2) + k, CTX + (n // 2) * P:CTX + (n // 2 + 1) * P], const(m, C_IDENT))
                mm.then_inc(turned, 1)

        @block.vector
        def _(dve):
            for n in range(0, 8, 2):
                dve.wait_ge(turned, n + 1)
                nc.vector.tensor_copy(rows[:, n // 2, 0:BANK], m.psum[n][:, :]).then_inc(even_out, 1)

        @block.scalar
        def _(act):
            for n in range(1, 8, 2):
                act.wait_ge(turned, n + 1)
                nc.scalar.copy(rows[:, n // 2, BANK:D], m.psum[n][:, :]).then_inc(odd_out, 1)

        @block.sync
        def _(sp):
            for t in range(4):
                sp.wait_ge(even_out, t + 1)
                sp.wait_ge(odd_out, t + 1)
                sp.dma_start(m.out[0, t * P:(t + 1) * P, :], rows[:, t, :]).then_inc(stored, 16)
            sp.wait_ge(stored, 64)


class Steps:

    def __init__(self, sem, names):
        self.sem, self.names, self.next = sem, names, 0

    @property
    def credit(self):
        return len(self.names)

    def step(self, name):
        assert self.names[self.next] == name, (self.names[self.next], name)
        self.next += 1
        return 1

    def after(self, head, name):
        return head * len(self.names) + len(self.names) + self.names.index(name) + 1

    def before(self, head, name):
        return head * len(self.names) + self.names.index(name) + 1


LEVELS = 6
PROBLEMS = 12
RUNS = ((0, 4, 0, 0), (4, 8, 0, 1), (8, 10, 4, 0), (10, 12, 4, 1))


def scan_step(s, d):
    if s < 4:
        c = s if d == 0 else 3 - s
        return (8, 10)[d] + c // 2, c % 2
    c = s - 4 if d == 0 else 11 - s
    return (0, 4)[d] + c // 2, c % 2


def delta_net(m):
    nc, dram = m.nc, m.dram
    w_in, pre_pe, pre_act, pre_dve = semaphores(m, "gdn", "w_in pre_pe pre_act pre_dve")
    at = [0, SLOT]

    def area(cols):
        if at[0] + cols <= 19500:
            at[0] += cols
            return cut(m, at[0] - cols, cols)
        at[1] += cols
        assert at[1] <= SLOTS * SLOT
        return m.ring[:, at[1] - cols:at[1]]

    def tiles(n):
        return area(n * P).rearrange("p (n t) -> p n t", n=n)

    m.O = area(KD * LAT).rearrange("p (k t) -> p k t", k=KD)
    m.O_first = CTX
    uq, uk, uv = area(LAT), area(TOK), area(TOK)
    gate = area(LAT)
    sq = area(LAT + TOK)
    rs = area(LAT + TOK)
    K, V = tiles(6), tiles(6)
    vb, kb, kd = tiles(PROBLEMS), tiles(PROBLEMS), tiles(PROBLEMS)
    DM, EG = tiles(PROBLEMS), tiles(PROBLEMS)
    QE = tiles(8)
    A, T, U, AM, Y = (tiles(PROBLEMS) for _ in range(5))
    AT = tiles(8)
    state = tiles(2)
    cu, wt = A, AM
    coef = area(5 * GH * PROBLEMS).rearrange("p (c h n) -> p c h n", c=5, h=GH)
    hc = area(5 * PROBLEMS).rearrange("p (c n) -> p c n", c=5)
    cw = area(9).rearrange("p (g w) -> p g w", g=3)
    z = area(6 * 32).rearrange("p (t n) -> p t n", t=6)
    z2, z3 = (area(6 * 16).rearrange("p (t n) -> p t n", t=6) for _ in range(2))
    ea = area(16)
    G_, GC, BETA, BEG, EKD = range(5)
    ident = const(m, C_IDENT)
    small = m.small
    B = m.psum
    wq = dram["gdn_w_qkv"].rearrange("(k p) (s n) -> p s k n", p=P, s=3)
    wg = dram["gdn_w_gate"].rearrange("(k p) n -> p k n", p=P)
    W = slot(m, 0).rearrange("p (s k n) -> p s k n", s=4, k=KD)
    conv_w = small[:, S_CONV:S_CONV + 72].rearrange("p (g h w) -> p g h w", g=3, h=GH)
    cum = (const(m, C_CUMF), const(m, C_CUMB))
    lev = (C_LEVF, C_LEVB)

    def bank(b, n=4):
        return B[b][:, 0:n * P].rearrange("p (n t) -> p n t", n=n)

    def rows(c, n0, n1):
        return hc[:, c, n0:n1].unsqueeze(2).broadcast_to([P, n1 - n0, P])

    def same(mask, n):
        return mask.unsqueeze(1).broadcast_to([P, n, P])

    CONV = (("q", uq[:, 0:LAT], 0, 0, LAT, 0), ("k", uk[:, 0:LAT], 1, 0, LAT, 1), ("v", uv[:, 0:LAT], 2, 0, LAT, 2),
            ("kc", uk[:, LAT:TOK], 3, 0, CTX, 1), ("vc", uv[:, LAT:TOK], 3, CTX, CTX, 2))
    GROUPS = range(3)
    lv = [f"{l}.{x}" for l in range(1, LEVELS) for x in GROUPS]
    sd = [f"{s}.{d}" for s in range(12) for d in range(2)]
    pe_names = (["rows0", "rows1", "rows2", "q", "k", "v", "kvc", "gate", "v_turned", "ss_q", "ss_k", "ss_kc", "vc_turned", "k_turned", "kc_turned",
                 "kk", "kkc", "qk"] + [f"a_turned{x}" for x in GROUPS] + [f"t_turned{x}" for x in GROUPS])
    for l in range(1, LEVELS):
        pe_names += [f"y{l}.{x}" for x in GROUPS]
        pe_names += sum([([f"t{l}.{x}"] if l < LEVELS - 1 else []) + [f"u{l}.{x}"] for x in GROUPS], [])
    pe_names += [f"cu{x}" for x in GROUPS] + [f"wt{x}" for x in GROUPS]
    for s in range(12):
        pe_names += [f"ws{s}.{d}" for d in range(2)]
        if s < 11:
            pe_names += [f"kv{s}.{d}" for d in range(2)]
        if s >= 4:
            pe_names += [f"o{s}.{d}" for d in range(2)]
    pe_names += ["ss_o"]
    act_names = ([f"eg{x}" for x in GROUPS] + [f"tap_{c[0]}" for c in CONV] + ["gate"] + [f"dm{x}" for x in GROUPS]
                 + [f"silu_{c[0]}" for c in CONV] + ["sq_q", "sq_k", "sq_kc", "V", "root_q", "root_k", "root_kc", "Vc", "K", "Kc"]
                 + [f"U{x}" for x in GROUPS] + [f"Y{v_}" for v_ in lv] + [f"wt{x}" for x in GROUPS] + ["o_f", "sq_o", "root_o"])
    dve_names = (["head_coef", "head_conv"] + [f"dm{n}" for n in range(PROBLEMS)]
                 + sum([[f"left_{c[0]}", f"right_{c[0]}"] for c in CONV], [])
                 + ["inv_q", "q", "inv_k", "k"] + [f"vb{r}" for r in range(4)] + ["at0", "at1"] + [f"ad{r}" for r in range(4)]
                 + [f"a{x}" for x in GROUPS] + [f"T0.{x}" for x in GROUPS])
    for l in range(1, LEVELS):
        dve_names += sum([([f"T{l}.{x}"] if l < LEVELS - 1 else []) + [f"U{l}.{x}"] for x in GROUPS], [])
    dve_names += [f"cu{x}" for x in GROUPS]
    for s in range(12):
        dve_names += [f"vn{s}.{d}" for d in range(2)] + ([f"st{s}.{d}" for d in range(2)] if s < 11 else [])
    dve_names += ["o", "inv_o", "normed", "out"]
    pool_names = ([f"mask{r}" for r in range(4)] + ["zero", "qe0", "qe1"] + [f"kb{r}" for r in range(4)] + [f"kd{r}" for r in range(4)]
                  + [f"am0.{r}" for r in range(4)] + sum([[f"am{l}.{r}" for r in range(4)] for l in range(1, LEVELS)], []))
    pe_step, act_step, dve_step, pool_step = semaphores(m, "gdn", "pe_step act_step dve_step pool_step")
    TE, SC, VE, GP = Steps(pe_step, pe_names), Steps(act_step, act_names), Steps(dve_step, dve_names), Steps(pool_step, pool_names)
    run_of = {0: (0,), 1: (1,), 2: (2, 3)}

    with nc.Block() as block:

        @block.sync
        def _(sp):
            with sp.Fori(0, GH) as h:
                sp.wait_ge(pe_step, TE.before(h, "gate"))
                for s in range(3):
                    sp.dma_start(W[:, s], wq[:, s, :, bass.ds(h * P, P)]).then_inc(w_in, 16)
                sp.dma_start(W[:, 3], wg[:, :, bass.ds(h * P, P)]).then_inc(w_in, 16)

        @block.tensor
        def _(pe):
            pe.sem_inc(pe_step, TE.credit)
            for t in range(6):
                t0 = CTX + t * P if t < 4 else (t - 4) * P
                for k in range(KD):
                    mm = nc.tensor.matmul(B[0][:, 32 * t:32 * t + 32], m.H[:, k, t0:t0 + P], small[:, S_WBD + 32 * k:S_WBD + 32 * k + 32],
                                          start=(k == 0), stop=(k == KD - 1))
            mm.then_inc(pre_pe, 1)
            pe.wait_ge(pre_dve, 15)
            gc = B[1][:, 0:GH * PROBLEMS].rearrange("p (h n) -> p h n", h=GH)
            for n0, n1, _, d in RUNS:
                nc.tensor.matmul(gc[:, :, n0:n1], cum[d], coef[:, G_, :, n0:n1], start=True, stop=True)
            nc.tensor.matmul(B[2][:, 0:GH * PROBLEMS].rearrange("p (h n) -> p h n", h=GH), const(m, C_BLK), coef[:, G_], start=True,
                             stop=True).then_inc(pre_pe, 1)

            def project(b, c0, s, t0, t1):
                for k in range(KD):
                    mm = nc.tensor.matmul(B[b][:, c0:c0 + t1 - t0], W[:, s, k, :], m.H[:, k, t0:t1], start=(k == 0), stop=(k == KD - 1))
                return mm

            with pe.Fori(0, GH) as h:
                pe.wait_ge(dve_step, VE.after(h, "head_coef"))
                for x in GROUPS:
                    for n in range(4 * x, 4 * x + 4):
                        d = [r[3] for r in RUNS if r[0] <= n < r[1]][0]
                        mm = nc.tensor.matmul(B[5 + x][:, (n % 4) * P:(n % 4 + 1) * P], hc[:, G_, n:n + 1].to_broadcast([P, P]), cum[d],
                                              start=True, stop=True)
                    mm.then_inc(pe_step, TE.step(f"rows{x}"))
                pe.wait_ge(w_in, h * 64 + 64)
                project(0, 0, 0, CTX, TOK).then_inc(pe_step, TE.step("q"))
                project(1, 0, 1, CTX, TOK).then_inc(pe_step, TE.step("k"))
                project(2, 0, 2, CTX, TOK).then_inc(pe_step, TE.step("v"))
                project(3, 0, 1, 0, CTX)
                project(3, CTX, 2, 0, CTX).then_inc(pe_step, TE.step("kvc"))
                project(4, 0, 3, CTX, TOK).then_inc(pe_step, TE.step("gate"))
                pe.wait_ge(act_step, SC.after(h, "silu_v"))
                for t in range(4):
                    mm = nc.tensor.transpose(B[0][:, t * P:(t + 1) * P], uv[:, t * P:(t + 1) * P], ident)
                mm.then_inc(pe_step, TE.step("v_turned"))
                pe.wait_ge(dve_step, VE.after(h, "dm11"))
                pe.wait_ge(act_step, SC.after(h, "sq_q"))
                nc.tensor.matmul(B[5][:, :], const(m, C_ONES), sq[:, 0:LAT], start=True, stop=True).then_inc(pe_step, TE.step("ss_q"))
                pe.wait_ge(act_step, SC.after(h, "sq_k"))
                nc.tensor.matmul(B[6][:, :], const(m, C_ONES), sq[:, LAT:2 * LAT], start=True, stop=True).then_inc(pe_step, TE.step("ss_k"))
                pe.wait_ge(act_step, SC.after(h, "sq_kc"))
                nc.tensor.matmul(B[7][:, 0:CTX], const(m, C_ONES), sq[:, 2 * LAT:2 * LAT + CTX], start=True,
                                 stop=True).then_inc(pe_step, TE.step("ss_kc"))
                for t in range(2):
                    mm = nc.tensor.transpose(B[2][:, (2 + t) * P:(3 + t) * P], uv[:, LAT + t * P:LAT + (t + 1) * P], ident)
                mm.then_inc(pe_step, TE.step("vc_turned"))
                pe.wait_ge(dve_step, VE.after(h, "k"))
                for t in range(4):
                    mm = nc.tensor.transpose(B[1][:, t * P:(t + 1) * P], uk[:, t * P:(t + 1) * P], ident)
                mm.then_inc(pe_step, TE.step("k_turned"))
                pe.wait_ge(act_step, SC.after(h, "Vc"))
                for t in range(2):
                    mm = nc.tensor.transpose(B[2][:, t * P:(t + 1) * P], uk[:, LAT + t * P:LAT + (t + 1) * P], ident)
                mm.then_inc(pe_step, TE.step("kc_turned"))
                for t in range(6):
                    kt = uk[:, t * P:(t + 1) * P]
                    mm = nc.tensor.matmul(B[3 + t // 4][:, (t % 4) * P:(t % 4 + 1) * P], kt, kt, start=True, stop=True)
                    if t in (3, 5):
                        mm.then_inc(pe_step, TE.step("kk" if t == 3 else "kkc"))
                for t in range(4):
                    mm = nc.tensor.matmul(B[5][:, t * P:(t + 1) * P], uk[:, t * P:(t + 1) * P], uq[:, t * P:(t + 1) * P], start=True, stop=True)
                mm.then_inc(pe_step, TE.step("qk"))
                for x in GROUPS:
                    pe.wait_ge(dve_step, VE.after(h, ("ad0", "ad1", "ad3")[x]))
                    if x == 0:
                        pe.wait_ge(act_step, SC.after(h, "Kc"))
                    for n in range(4):
                        mm = nc.tensor.transpose(bank(x)[:, n, :], DM[:, 4 * x + n, :], ident)
                    mm.then_inc(pe_step, TE.step(f"a_turned{x}"))
                for x in GROUPS:
                    pe.wait_ge(dve_step, VE.after(h, f"T0.{x}"))
                    for n in range(4):
                        mm = nc.tensor.transpose(bank(3 + x)[:, n, :], T[:, 4 * x + n, :], ident)
                    mm.then_inc(pe_step, TE.step(f"t_turned{x}"))
                for l in range(1, LEVELS):
                    for x in GROUPS:
                        pe.wait_ge(pool_step, GP.after(h, f"am{l}.{run_of[x][-1]}"))
                        if l == 1:
                            pe.wait_ge(act_step, SC.after(h, f"U{x}"))
                        else:
                            pe.wait_ge(dve_step, VE.after(h, f"U{l - 1}.{x}"))
                        for n in range(4):
                            mm = nc.tensor.matmul(bank(x)[:, n, :], AM[:, 4 * x + n, :], U[:, 4 * x + n, :], start=True, stop=True)
                        mm.then_inc(pe_step, TE.step(f"y{l}.{x}"))
                    for x in GROUPS:
                        pe.wait_ge(act_step, SC.after(h, f"Y{l}.{x}"))
                        if l < LEVELS - 1:
                            for n in range(4):
                                mm = nc.tensor.matmul(bank(3 + x)[:, n, :], Y[:, 4 * x + n, :], T[:, 4 * x + n, :], start=True, stop=True)
                            mm.then_inc(pe_step, TE.step(f"t{l}.{x}"))
                        for n in range(4):
                            mm = nc.tensor.matmul(bank(x)[:, n, :], T[:, 4 * x + n, :], Y[:, 4 * x + n, :], start=True, stop=True)
                        mm.then_inc(pe_step, TE.step(f"u{l}.{x}"))
                for x in GROUPS:
                    pe.wait_ge(dve_step, VE.after(h, f"U{LEVELS - 1}.{x}"))
                    for n in range(4):
                        mm = nc.tensor.matmul(bank(3 + x)[:, n, :], U[:, 4 * x + n, :], vb[:, 4 * x + n, :], start=True, stop=True)
                    mm.then_inc(pe_step, TE.step(f"cu{x}"))
                for x in GROUPS:
                    pe.wait_ge(pool_step, GP.after(h, "kb3"))
                    for n in range(4):
                        mm = nc.tensor.matmul(bank(x)[:, n, :], kb[:, 4 * x + n, :], U[:, 4 * x + n, :], start=True, stop=True)
                    mm.then_inc(pe_step, TE.step(f"wt{x}"))
                pe.wait_ge(act_step, SC.after(h, "wt2"))
                pe.wait_ge(dve_step, VE.after(h, "cu2"))
                pe.wait_ge(pool_step, GP.after(h, "kd3"))
                for s in range(12):
                    for d in range(2):
                        n, half = scan_step(s, d)
                        c = slice(64 * half, 64 * half + 64)
                        if s:
                            pe.wait_ge(dve_step, VE.after(h, f"st{s - 1}.{d}"))
                        nc.tensor.matmul(B[6 + d][c, 0:P], wt[:, n, c], state[:, d, :], start=True, stop=True)\
                            .then_inc(pe_step, TE.step(f"ws{s}.{d}"))
                        if s >= 4:
                            o0 = (n % 4) * P + 64 * half
                            nc.tensor.matmul(B[2 + d][:, o0:o0 + 64], state[:, d, :], QE[:, n, c], start=True, stop=False)
                    for d in range(2):
                        n, half = scan_step(s, d)
                        c = slice(64 * half, 64 * half + 64)
                        pe.wait_ge(dve_step, VE.after(h, f"vn{s}.{d}"))
                        if s < 11:
                            nc.tensor.matmul(B[d][:, 0:P], kd[c, n, :], cu[c, n, :], start=True, stop=True)\
                                .then_inc(pe_step, TE.step(f"kv{s}.{d}"))
                    if s >= 4:
                        for d in range(2):
                            n, half = scan_step(s, d)
                            c = slice(64 * half, 64 * half + 64)
                            o0 = (n % 4) * P + 64 * half
                            nc.tensor.matmul(B[2 + d][:, o0:o0 + 64], cu[c, n, :], AT[c, n, c], start=False, stop=True)\
                                .then_inc(pe_step, TE.step(f"o{s}.{d}"))
                pe.wait_ge(act_step, SC.after(h, "sq_o"))
                nc.tensor.matmul(B[4][:, :], const(m, C_ONES), sq[:, 0:LAT], start=True, stop=True).then_inc(pe_step, TE.step("ss_o"))

        @block.scalar
        def _(act):
            act.sem_inc(act_step, SC.credit)
            act.wait_ge(pre_dve, 1)
            nc.scalar.activation(z[:, :, 0:16], z[:, :, 0:16], ACT.Sigmoid).then_inc(pre_act, 1)
            nc.scalar.activation(ea, small[:, S_ALOG:S_ALOG + 16], ACT.Exp).then_inc(pre_act, 1)
            act.wait_ge(pre_dve, 4)
            nc.scalar.activation(z3, z3, ACT.Exp).then_inc(pre_act, 1)
            act.wait_ge(pre_act, 3)
            nc.scalar.activation(z3, z3, ACT.Ln, bias=const(m, C_EPS + 2, 1)).then_inc(pre_act, 1)
            act.wait_ge(pre_dve, 17)
            nc.scalar.activation(coef[:, BEG], coef[:, GC], ACT.Exp).then_inc(pre_act, 1)
            nc.scalar.activation(coef[:, EKD], coef[:, EKD], ACT.Exp).then_inc(pre_act, 1)
            with act.Fori(0, GH) as h:
                act.wait_ge(dve_step, VE.before(h, "out"))
                for x in GROUPS:
                    act.wait_ge(pe_step, TE.after(h, f"rows{x}"))
                    nc.scalar.activation(EG[:, 4 * x:4 * x + 4, :], bank(5 + x), ACT.Exp).then_inc(act_step, SC.step(f"eg{x}"))
                for name, dst, b, c0, n, g in CONV:
                    act.wait_ge(pe_step, TE.after(h, {"q": "q", "k": "k", "v": "v"}.get(name, "kvc")))
                    act.wait_ge(dve_step, VE.after(h, "head_conv"))
                    nc.scalar.activation(dst, B[b][:, c0:c0 + n], ACT.Identity, scale=cw[:, g, 1:2]).then_inc(act_step, SC.step(f"tap_{name}"))
                act.wait_ge(pe_step, TE.after(h, "gate"))
                nc.scalar.activation(gate, B[4][:, :], ACT.Silu).then_inc(act_step, SC.step("gate"))
                for x in GROUPS:
                    act.wait_ge(dve_step, VE.after(h, f"dm{4 * x + 3}"))
                    nc.scalar.activation(DM[:, 4 * x:4 * x + 4, :], DM[:, 4 * x:4 * x + 4, :], ACT.Exp).then_inc(act_step, SC.step(f"dm{x}"))
                for name, dst, b, c0, n, g in CONV:
                    act.wait_ge(dve_step, VE.after(h, f"right_{name}"))
                    nc.scalar.activation(dst, dst, ACT.Silu).then_inc(act_step, SC.step(f"silu_{name}"))
                act.wait_ge(act_step, SC.after(h, "silu_kc"))
                nc.scalar.activation(sq[:, 0:LAT], uq, ACT.Square).then_inc(act_step, SC.step("sq_q"))
                nc.scalar.activation(sq[:, LAT:2 * LAT], uk[:, 0:LAT], ACT.Square).then_inc(act_step, SC.step("sq_k"))
                nc.scalar.activation(sq[:, 2 * LAT:2 * LAT + CTX], uk[:, LAT:TOK], ACT.Square).then_inc(act_step, SC.step("sq_kc"))
                act.wait_ge(pe_step, TE.after(h, "v_turned"))
                nc.scalar.copy(V[:, 0:4, :], bank(0)).then_inc(act_step, SC.step("V"))
                act.wait_ge(pe_step, TE.after(h, "ss_q"))
                nc.scalar.activation(rs[:, 0:LAT], B[5][:, :], ACT.Sqrt, bias=const(m, C_EPS + 3, 1), scale=float(GD))\
                    .then_inc(act_step, SC.step("root_q"))
                act.wait_ge(pe_step, TE.after(h, "ss_k"))
                nc.scalar.activation(rs[:, LAT:2 * LAT], B[6][:, :], ACT.Sqrt, bias=const(m, C_EPS, 1)).then_inc(act_step, SC.step("root_k"))
                act.wait_ge(pe_step, TE.after(h, "ss_kc"))
                nc.scalar.activation(rs[:, 2 * LAT:2 * LAT + CTX], B[7][:, 0:CTX], ACT.Sqrt, bias=const(m, C_EPS, 1))\
                    .then_inc(act_step, SC.step("root_kc"))
                act.wait_ge(pe_step, TE.after(h, "vc_turned"))
                nc.scalar.copy(V[:, 4:6, :], bank(2)[:, 2:4, :]).then_inc(act_step, SC.step("Vc"))
                act.wait_ge(pe_step, TE.after(h, "k_turned"))
                nc.scalar.copy(K[:, 0:4, :], bank(1)).then_inc(act_step, SC.step("K"))
                act.wait_ge(pe_step, TE.after(h, "kc_turned"))
                nc.scalar.copy(K[:, 4:6, :], bank(2)[:, 0:2, :]).then_inc(act_step, SC.step("Kc"))
                for x in GROUPS:
                    act.wait_ge(pe_step, TE.after(h, f"t_turned{x}"))
                    nc.scalar.copy(U[:, 4 * x:4 * x + 4, :], bank(3 + x)).then_inc(act_step, SC.step(f"U{x}"))
                for l in range(1, LEVELS):
                    for x in GROUPS:
                        act.wait_ge(pe_step, TE.after(h, f"y{l}.{x}"))
                        nc.scalar.copy(Y[:, 4 * x:4 * x + 4, :], bank(x)).then_inc(act_step, SC.step(f"Y{l}.{x}"))
                for x in GROUPS:
                    act.wait_ge(pe_step, TE.after(h, f"wt{x}"))
                    nc.scalar.copy(wt[:, 4 * x:4 * x + 4, :], bank(x)).then_inc(act_step, SC.step(f"wt{x}"))
                act.wait_ge(pe_step, TE.after(h, "o11.1"))
                nc.scalar.copy(rs[:, 0:LAT], B[2][:, :]).then_inc(act_step, SC.step("o_f"))
                act.wait_ge(dve_step, VE.after(h, "o"))
                nc.scalar.activation(sq[:, 0:LAT], uq, ACT.Square).then_inc(act_step, SC.step("sq_o"))
                act.wait_ge(pe_step, TE.after(h, "ss_o"))
                nc.scalar.activation(rs[:, LAT:2 * LAT], B[4][:, :], ACT.Sqrt, bias=const(m, C_EPS, 1), scale=1.0 / GD)\
                    .then_inc(act_step, SC.step("root_o"))

        @block.gpsimd
        def _(pool):
            pool.sem_inc(pool_step, GP.credit)
            with pool.Fori(0, GH) as h:
                pool.wait_ge(dve_step, VE.before(h, "out"))
                for r, (n0, n1, _, d) in enumerate(RUNS):
                    pool.wait_ge(act_step, SC.after(h, f"dm{(n1 - 1) // 4}"))
                    nc.gpsimd.tensor_tensor(DM[:, n0:n1, :], DM[:, n0:n1, :], same(cum[d], n1 - n0), ALU.mult)\
                        .then_inc(pool_step, GP.step(f"mask{r}"))
                nc.gpsimd.memset(state, 0.0).then_inc(pool_step, GP.step("zero"))
                pool.wait_ge(dve_step, VE.after(h, "q"))
                for d in range(2):
                    nc.gpsimd.tensor_tensor(QE[:, 4 * d:4 * d + 4, :], uq.rearrange("p (n t) -> p n t", n=4), EG[:, 4 * d:4 * d + 4, :], ALU.mult)\
                        .then_inc(pool_step, GP.step(f"qe{d}"))
                pool.wait_ge(act_step, SC.after(h, "Kc"))
                for dst, c, name in ((kb, BEG, "kb"), (kd, EKD, "kd")):
                    for r, (n0, n1, t0, d) in enumerate(RUNS):
                        nc.gpsimd.tensor_tensor(dst[:, n0:n1, :], K[:, t0:t0 + n1 - n0, :], rows(c, n0, n1), ALU.mult)\
                            .then_inc(pool_step, GP.step(f"{name}{r}"))
                for l in range(LEVELS):
                    for r, (n0, n1, _, d) in enumerate(RUNS):
                        x = min(r, 2)
                        if l == 0:
                            pool.wait_ge(dve_step, VE.after(h, f"a{x}"))
                        elif l == 1:
                            pool.wait_ge(dve_step, VE.after(h, f"T0.{x}"))
                        else:
                            pool.wait_ge(pe_step, TE.after(h, f"y{l - 1}.{x}"))
                        nc.gpsimd.tensor_tensor(AM[:, n0:n1, :], A[:, n0:n1, :], same(const(m, lev[d] + l * P), n1 - n0), ALU.mult)\
                            .then_inc(pool_step, GP.step(f"am{l}.{r}"))

        @block.vector
        def _(dve):
            dve.sem_inc(dve_step, VE.credit)
            dve.wait_ge(pre_pe, 1)
            nc.vector.tensor_copy(z, B[0][:, 0:192].rearrange("p (t n) -> p t n", t=6)).then_inc(pre_dve, 1)
            dve.wait_ge(pre_dve, 1)
            dtb = small[:, S_DTB:S_DTB + 16].unsqueeze(1).broadcast_to([P, 6, 16])
            nc.vector.tensor_tensor(z2, z[:, :, 16:32], dtb, ALU.add).then_inc(pre_dve, 1)
            dve.wait_ge(pre_dve, 2)
            nc.vector.tensor_scalar(z3, z2, -1.0, None, ALU.mult).then_inc(pre_dve, 1)
            dve.wait_ge(pre_dve, 3)
            nc.vector.tensor_tensor(z3, z3, z2, ALU.min).then_inc(pre_dve, 1)
            dve.wait_ge(pre_dve, 4)
            nc.vector.tensor_scalar(z2, z2, 0.0, None, ALU.max).then_inc(pre_dve, 1)
            dve.wait_ge(pre_dve, 5)
            dve.wait_ge(pre_act, 4)
            nc.vector.tensor_tensor(z2, z2, z3, ALU.add).then_inc(pre_dve, 1)
            dve.wait_ge(pre_dve, 6)
            nc.vector.tensor_tensor(z2, z2, ea.unsqueeze(1).broadcast_to([P, 6, 16]), ALU.mult).then_inc(pre_dve, 1)
            dve.wait_ge(pre_dve, 7)
            for n0, n1, t0, d in RUNS:
                for c, src, f in ((G_, z2, -1.0), (BETA, z, 1.0)):
                    nc.vector.tensor_scalar(coef[:, c, :, n0:n1], src[:, t0:t0 + n1 - n0, GH * d:GH * d + GH].rearrange("p t h -> p h t"),
                                            f, None, ALU.mult).then_inc(pre_dve, 1)
            dve.wait_ge(pre_pe, 2)
            nc.vector.tensor_copy(coef[:, GC], B[1][:, 0:GH * PROBLEMS].rearrange("p (h n) -> p h n", h=GH)).then_inc(pre_dve, 1)
            dve.wait_ge(pre_dve, 16)
            nc.vector.tensor_tensor(coef[:, EKD], B[2][:, 0:GH * PROBLEMS].rearrange("p (h n) -> p h n", h=GH), coef[:, GC],
                                    ALU.subtract).then_inc(pre_dve, 1)
            dve.wait_ge(pre_act, 6)
            nc.vector.tensor_tensor(coef[:, BEG], coef[:, BEG], coef[:, BETA], ALU.mult).then_inc(pre_dve, 1)
            dve.wait_ge(pre_dve, 18)
            with dve.Fori(0, GH) as h:
                dve.wait_ge(pe_step, TE.before(h, "ss_o"))
                dve.wait_ge(dve_step, VE.before(h, "out"))
                nc.vector.tensor_copy(hc.unsqueeze(2), coef[:, :, bass.ds(h, 1), :]).then_inc(dve_step, VE.step("head_coef"))
                nc.vector.tensor_copy(cw.unsqueeze(2), conv_w[:, :, bass.ds(h, 1), :]).then_inc(dve_step, VE.step("head_conv"))
                dve.wait_ge(dve_step, VE.after(h, "head_conv"))
                for n in range(PROBLEMS):
                    if n % 4 == 0:
                        dve.wait_ge(act_step, SC.after(h, f"eg{n // 4}"))
                    nc.vector.tensor_scalar(DM[:, n, :], bank(5 + n // 4)[:, n % 4, :], hc[:, GC, n:n + 1], 0.0, ALU.subtract, ALU.min)\
                        .then_inc(dve_step, VE.step(f"dm{n}"))
                for name, dst, b, c0, n, g in CONV:
                    dve.wait_ge(act_step, SC.after(h, "tap_vc" if b == 3 else f"tap_{name}"))
                    nc.vector.scalar_tensor_tensor(out=dst[:, 1:n], in0=B[b][:, c0:c0 + n - 1], scalar=cw[:, g, 0:1], in1=dst[:, 1:n],
                                                   op0=ALU.mult, op1=ALU.add).then_inc(dve_step, VE.step(f"left_{name}"))
                    dve.wait_ge(dve_step, VE.after(h, f"left_{name}"))
                    nc.vector.scalar_tensor_tensor(out=dst[:, 0:n - 1], in0=B[b][:, c0 + 1:c0 + n], scalar=cw[:, g, 2:3], in1=dst[:, 0:n - 1],
                                                   op0=ALU.mult, op1=ALU.add).then_inc(dve_step, VE.step(f"right_{name}"))
                dve.wait_ge(act_step, SC.after(h, "root_q"))
                nc.vector.reciprocal(rs[:, 0:LAT], rs[:, 0:LAT]).then_inc(dve_step, VE.step("inv_q"))
                dve.wait_ge(dve_step, VE.after(h, "inv_q"))
                nc.vector.tensor_tensor(uq, uq, rs[:, 0:LAT], ALU.mult).then_inc(dve_step, VE.step("q"))
                dve.wait_ge(act_step, SC.after(h, "root_kc"))
                nc.vector.reciprocal(rs[:, LAT:LAT + TOK], rs[:, LAT:LAT + TOK]).then_inc(dve_step, VE.step("inv_k"))
                dve.wait_ge(dve_step, VE.after(h, "inv_k"))
                nc.vector.tensor_tensor(uk, uk, rs[:, LAT:LAT + TOK], ALU.mult).then_inc(dve_step, VE.step("k"))
                for r, (n0, n1, t0, d) in enumerate(RUNS):
                    dve.wait_ge(act_step, SC.after(h, "Vc"))
                    nc.vector.tensor_tensor(vb[:, n0:n1, :], V[:, t0:t0 + n1 - n0, :], rows(BETA, n0, n1), ALU.mult)\
                        .then_inc(dve_step, VE.step(f"vb{r}"))
                for d in range(2):
                    dve.wait_ge(pe_step, TE.after(h, "qk"))
                    dve.wait_ge(pool_step, GP.after(h, "mask1"))
                    nc.vector.tensor_tensor(AT[:, 4 * d:4 * d + 4, :], bank(5), DM[:, 4 * d:4 * d + 4, :], ALU.mult)\
                        .then_inc(dve_step, VE.step(f"at{d}"))
                dve.wait_ge(pool_step, GP.after(h, "mask3"))
                dve.wait_ge(dve_step, VE.after(h, "at1"))
                for r, (n0, n1, t0, d) in enumerate(RUNS):
                    nc.vector.tensor_tensor(DM[:, n0:n1, :], bank(3 + (r > 1), n1 - n0), DM[:, n0:n1, :], ALU.mult)\
                        .then_inc(dve_step, VE.step(f"ad{r}"))
                for x in GROUPS:
                    dve.wait_ge(pe_step, TE.after(h, f"a_turned{x}"))
                    nc.vector.tensor_tensor(A[:, 4 * x:4 * x + 4, :], bank(x), rows(BETA, 4 * x, 4 * x + 4), ALU.mult)\
                        .then_inc(dve_step, VE.step(f"a{x}"))
                for x in GROUPS:
                    dve.wait_ge(pool_step, GP.after(h, f"am0.{run_of[x][-1]}"))
                    nc.vector.tensor_tensor(T[:, 4 * x:4 * x + 4, :], same(ident, 4), AM[:, 4 * x:4 * x + 4, :], ALU.subtract)\
                        .then_inc(dve_step, VE.step(f"T0.{x}"))
                for l in range(1, LEVELS):
                    for x in GROUPS:
                        g4 = slice(4 * x, 4 * x + 4)
                        dve.wait_ge(pe_step, TE.after(h, f"u{l}.{x}"))
                        if l < LEVELS - 1:
                            nc.vector.tensor_tensor(T[:, g4, :], T[:, g4, :], bank(3 + x), ALU.subtract).then_inc(dve_step, VE.step(f"T{l}.{x}"))
                        nc.vector.tensor_tensor(U[:, g4, :], U[:, g4, :], bank(x), ALU.subtract).then_inc(dve_step, VE.step(f"U{l}.{x}"))
                for x in GROUPS:
                    dve.wait_ge(pe_step, TE.after(h, f"cu{x}"))
                    nc.vector.tensor_copy(cu[:, 4 * x:4 * x + 4, :], bank(3 + x)).then_inc(dve_step, VE.step(f"cu{x}"))
                for s in range(12):
                    for d in range(2):
                        n, half = scan_step(s, d)
                        c = slice(64 * half, 64 * half + 64)
                        dve.wait_ge(pe_step, TE.after(h, f"ws{s}.{d}"))
                        if s == 0:
                            dve.wait_ge(dve_step, VE.after(h, "cu2"))
                        nc.vector.tensor_tensor(cu[c, n, :], cu[c, n, :], B[6 + d][c, 0:P], ALU.subtract).then_inc(dve_step, VE.step(f"vn{s}.{d}"))
                    if s < 11:
                        for d in range(2):
                            n, half = scan_step(s, d)
                            last = 64 * half + (63 if d == 0 else 0)
                            dve.wait_ge(pe_step, TE.after(h, f"kv{s}.{d}"))
                            nc.vector.scalar_tensor_tensor(out=state[:, d, :], in0=state[:, d, :], scalar=EG[:, n, last:last + 1], in1=B[d][:, 0:P],
                                                           op0=ALU.mult, op1=ALU.add).then_inc(dve_step, VE.step(f"st{s}.{d}"))
                dve.wait_ge(act_step, SC.after(h, "o_f"))
                nc.vector.tensor_tensor(uq, rs[:, 0:LAT], B[3][:, :], ALU.add).then_inc(dve_step, VE.step("o"))
                dve.wait_ge(act_step, SC.after(h, "root_o"))
                nc.vector.reciprocal(rs[:, LAT:2 * LAT], rs[:, LAT:2 * LAT]).then_inc(dve_step, VE.step("inv_o"))
                dve.wait_ge(dve_step, VE.after(h, "inv_o"))
                nc.vector.scalar_tensor_tensor(out=uq, in0=uq, scalar=small[:, S_ON:S_ON + 1], in1=rs[:, LAT:2 * LAT], op0=ALU.mult,
                                               op1=ALU.mult).then_inc(dve_step, VE.step("normed"))
                dve.wait_ge(dve_step, VE.after(h, "normed"))
                nc.vector.tensor_tensor(m.O[:, bass.ds(h, 1), :], uq.unsqueeze(1), gate.unsqueeze(1), ALU.mult)\
                    .then_inc(dve_step, VE.step("out"))
    for engine in (TE, SC, VE, GP):
        assert engine.next == len(engine.names), engine.names[engine.next]


def build(nc, dram, out):
    with ExitStack() as ctx:
        m = open_memory(nc, ctx, dram)
        m.out = out
        load_and_modulation(m)
        norm_modulate(m, "n0", 0, 0)
        neighbourhood_attention(m)
        project_to_residual(m, "no", dram["na_w_o"], 0, 0)
        norm_modulate(m, "n1", 0, 1)
        swiglu(m)
        reorder(m)
        norm_modulate(m, "n2", 1, 0)
        delta_net(m)
        project_to_residual(m, "go", dram["gdn_w_o"], 1, CTX)
        norm_modulate(m, "n3", 1, 1, first=CTX)
        experts(m)
        store(m)


_INS = ["x", "ctx", "ada_w", "na_w_qkv", "na_w_o", "gdn_w_qkv", "gdn_w_gate", "gdn_w_o", "ffn_w_in", "ffn_w_out",
        "moe_w_in", "moe_w_out"]


def kernel(**inputs):
    import concourse.bacc as bacc
    from concourse.bass_utils import run_bass_kernel_spmd

    nc = bacc.Bacc("TRN2", target_bir_lowering=False, num_devices=1)
    arrays = {n: np.ascontiguousarray(inputs[n]) for n in _INS}
    arrays["small"] = small_inputs(inputs)
    arrays["bias"] = bias_table(inputs["na_rpb"])
    arrays["const"] = constants()
    dram = {n: nc.dram_tensor(f"in_{n}", a.shape, mybir.dt.from_np(a.dtype), kind="ExternalInput").ap()
            for n, a in arrays.items()}
    out = nc.dram_tensor("out", (1, LAT, D), F32, kind="ExternalOutput").ap()
    build(nc, dram, out)
    r = run_bass_kernel_spmd(nc, [{f"in_{n}": a for n, a in arrays.items()}], core_ids=[0])
    return r.results[0]["out"]
```

```python
from contextlib import ExitStack

import numpy as np

import concourse.bass as bass
from concourse import mybir

F32 = mybir.dt.float32
U32 = mybir.dt.uint32
ALU = mybir.AluOpType
ACT = mybir.ActivationFunctionType
AX = mybir.AxisListType

P = 128
D = 1024
KD = D // P
CTX, LAT = 256, 512
TOK = CTX + LAT
GRID_R, GRID_C = 8, 64
BANK = 512
EPS = 1e-6
SLOT = 4096
SLOTS = 4

NA_HEADS, NA_HD = 16, 64
NA_PAIRS = NA_HEADS // 2
WIN_R, WIN_C = 8, 16
DR = 2 * WIN_R - 1
DC = 2 * WIN_C - 1
BIAS_DC = 2 * DC + 1
BIAS_RUN = 48 * DR
WIN = 256
WIN_START = (0, 64, 192, 256)
WIN_VARIANT = (0, 1, 1, 2)
WIN_SHIFT = (16, 8, 0)
MASKED = -1e30

FFN = 2816
EXPERTS = 8
EFF = 1408

GH, GD = 8, 128
CH = 64

C_IDENT = 0
C_MEAN = C_IDENT + P
C_HALF = C_MEAN + P
C_ONES = C_HALF + P
C_WMASK = C_ONES + P
C_CUMF = C_WMASK + 96
C_CUMB = C_CUMF + P
C_BLK = C_CUMB + P
C_BEFORE = C_BLK + P
C_LEVF = C_BEFORE + P
C_LEVB = C_LEVF + 6 * P
C_IOTA = C_LEVB + 6 * P
C_SLOT = C_IOTA + EXPERTS
C_EPS = C_SLOT + 2 * P
C_ALL = C_EPS + 4


def constants():
    c = np.zeros((P, C_ALL), np.float32)
    i = np.arange(P)
    row, col = i[:, None], i[None, :]
    same = row // CH == col // CH
    c[:, C_IDENT:C_IDENT + P] = row == col
    c[:, C_MEAN:C_MEAN + P] = 1.0 / D
    c[:, C_HALF:C_HALF + P] = (row // NA_HD == col // NA_HD) / NA_HD
    c[:, C_ONES:C_ONES + P] = 1.0
    for v, (block, start) in enumerate(((0, 0), (1, 8), (3, 32))):
        qcol = 16 * block + i // 8
        c0 = np.clip(qcol - WIN_C // 2, 0, GRID_C - WIN_C)[:, None]
        kcol = start + np.arange(32)[None, :]
        c[:, C_WMASK + 32 * v:C_WMASK + 32 * v + 32] = np.where((kcol >= c0) & (kcol < c0 + WIN_C), 0.0, MASKED)
    c[:, C_CUMF:C_CUMF + P] = same & (row <= col)
    c[:, C_CUMB:C_CUMB + P] = same & (row >= col)
    c[:, C_BLK:C_BLK + P] = same
    c[:, C_BEFORE:C_BEFORE + P] = row < col
    for n in range(6):
        s = 1 << n
        pair = (row // (2 * s) == col // (2 * s)) & (row // s != col // s)
        c[:, C_LEVF + n * P:C_LEVF + n * P + P] = pair & (row > col)
        c[:, C_LEVB + n * P:C_LEVB + n * P + P] = pair & (row < col)
    c[:, C_IOTA:C_IOTA + EXPERTS] = np.arange(EXPERTS)
    c[:, C_SLOT:C_SLOT + 2 * P] = np.arange(2 * P)
    c[:, C_EPS:C_EPS + 4] = (EPS, NA_HD * EPS, 1.0, GD * EPS)
    return c


S_C = 0
S_ADAB = S_C + 2 * KD
S_NORM = S_ADAB + 96
S_QN = S_NORM + 4 * KD
S_CONV = S_QN + 2
S_WBD = S_CONV + 72
S_ALOG = S_WBD + 32 * KD
S_DTB = S_ALOG + 2 * GH
S_ON = S_DTB + 2 * GH
S_RT = S_ON + 1
S_ALL = S_RT + EXPERTS * KD


def small_inputs(x):
    def groups(a):
        a = np.asarray(a)
        return np.moveaxis(a.reshape(a.shape[:-1] + (a.shape[-1] // P, P)), -1, 0)

    def rows(a):
        a = np.asarray(a)
        return a.reshape(a.shape[0] // P, P, a.shape[1]).transpose(1, 0, 2)

    gates = [x["gdn_w_beta"][0], x["gdn_w_beta"][1], x["gdn_w_decay"][0], x["gdn_w_decay"][1]]
    parts = [
        rows(np.stack([np.asarray(x["c"])[0], np.asarray(x["c_ctx"])], axis=1)),
        groups(x["ada_b"]), groups(x["norm_g"]),
        np.stack([np.tile(np.asarray(x["na_q_norm"]), 2), np.tile(np.asarray(x["na_k_norm"]), 2)], axis=1),
        groups(x["gdn_conv"]).transpose(0, 2, 1),
        rows(np.concatenate([np.asarray(g) for g in gates], axis=1)),
        np.broadcast_to(np.asarray(x["gdn_a_log"]).reshape(1, -1), (P, 2 * GH)),
        np.broadcast_to(np.asarray(x["gdn_dt_bias"]).reshape(1, -1), (P, 2 * GH)),
        np.asarray(x["gdn_out_norm"]).reshape(P, 1),
        rows(x["moe_router"][0]),
    ]
    return np.ascontiguousarray(np.concatenate([a.reshape(P, -1) for a in parts], axis=1))


def bias_table(rpb):
    rpb = np.asarray(rpb)
    t = np.zeros((NA_HEADS, BIAS_DC, DR), rpb.dtype)
    t[:, DC - 15:DC + 16, :] = rpb.transpose(0, 2, 1)[:, ::-1, ::-1]
    return np.concatenate([t.reshape(-1), np.zeros(BIAS_RUN, rpb.dtype)])


class Core:
    pass


def open_memory(nc, ctx, dram):
    m = Core()
    m.nc, m.ctx, m.dram = nc, ctx, dram

    def sb(name, cols):
        return ctx.enter_context(nc.sbuf_tensor(name, [P, cols], F32))

    m.xt = sb("residual", KD * TOK)
    m.ht = sb("hidden", KD * TOK)
    m.ring = sb("weight_ring", SLOTS * SLOT)
    m.work = sb("work", 19500)
    m.const = sb("constants", C_ALL)
    m.small = sb("small_inputs", S_ALL)
    m.mod = sb("modulation", 2 * 48 * 2)
    m.moda = sb("modulation_scale", 2 * 2 * KD * 2)
    m.psum = [ctx.enter_context(nc.psum_tensor(f"bank{i}", [P, BANK], F32)) for i in range(8)]
    m.X = m.xt[:, :].rearrange("p (k t) -> p k t", k=KD)
    m.H = m.ht[:, :].rearrange("p (k t) -> p k t", k=KD)
    m.MOD = m.mod[:, :].rearrange("p (l c k v) -> p l c k v", l=2, c=6, k=KD)
    m.MODA = m.moda[:, :].rearrange("p (l n k v) -> p l n k v", l=2, n=2, k=KD)
    return m


def cut(m, at, cols):
    return m.work[:, at:at + cols]


def const(m, at, cols=P):
    return m.const[:, at:at + cols]


def semaphores(m, phase, names):
    return [m.ctx.enter_context(m.nc.semaphore(f"{phase}_{n}")) for n in names.split()]


def slot(m, n):
    return m.ring[:, n * SLOT:(n + 1) * SLOT]


def load_and_modulation(m):
    nc, dram = m.nc, m.dram
    (small_in, tokens_in, turned, even_out, odd_out, silu_c, slab_used, mod_sum, mod_scale) = semaphores(
        m, "in", "small_in tokens_in turned even_out odd_out silu_c slab_used mod_sum mod_scale")
    slab_in = semaphores(m, "in", " ".join(f"slab_in{n}" for n in range(SLOTS)))
    raw = cut(m, 0, 6 * D).rearrange("p (t d) -> p t d", t=6)
    sig = cut(m, 6 * D, 2 * KD)
    sc = cut(m, 6 * D + 2 * KD, 2 * KD)
    ident = const(m, C_IDENT)
    lat = dram["x"][0].rearrange("(r c) d -> c r d", c=GRID_C)
    adaw = dram["ada_w"].rearrange("l (k p) n -> l p k n", p=P)
    slabs = 12

    with nc.Block() as block:

        @block.sync
        def _(sp):
            sp.dma_start(m.small[:, :], dram["small"]).then_inc(small_in, 16)
            sp.dma_start(m.const[:, :], dram["const"]).then_inc(small_in, 16)
            for t in range(6):
                src = dram["ctx"][0, t * P:(t + 1) * P, :] if t < 2 else lat[16 * (t - 2):16 * (t - 1)]
                sp.dma_start(raw[:, t, :], src).then_inc(tokens_in, 16)
            for l in range(2):
                with sp.Fori(0, slabs // SLOTS) as i:
                    for s in range(SLOTS):
                        sp.wait_ge(slab_used, i * SLOTS + (l * slabs + s + 1))
                        sp.dma_start(slot(m, s).rearrange("p (k n) -> p k n", k=KD),
                                     adaw[l][:, :, bass.ds(i * (SLOTS * BANK) + s * BANK, BANK)]).then_inc(slab_in[s], 16)

        @block.tensor
        def _(pe):
            pe.sem_inc(slab_used, SLOTS)
            pe.wait_ge(small_in, 32)
            pe.wait_ge(tokens_in, 96)
            for n in range(12):
                if n >= 6:
                    pe.wait_ge((even_out, odd_out)[n % 2], (n - 6) // 2 + 1)
                for k in range(4):
                    mm = nc.tensor.transpose(m.psum[n % 6][:, k * P:(k + 1) * P],
                                             raw[:, n // 2, (4 * (n % 2) + k) * P:(4 * (n % 2) + k + 1) * P], ident)
                mm.then_inc(turned, 1)
            pe.wait_ge(silu_c, 2)
            for l in range(2):
                with pe.Fori(0, slabs // SLOTS) as i:
                    for s in range(SLOTS):
                        pe.wait_ge(slab_in[s], i * 16 + (l * (slabs // SLOTS) * 16 + 16))
                        w = slot(m, s).rearrange("p (k n) -> p k n", k=KD)
                        for g in range(4):
                            for k in range(KD):
                                mm = nc.tensor.matmul(
                                    m.psum[6 + l][:, bass.ds(i * (8 * SLOTS) + (s * 4 + g) * 2, 2)],
                                    w[:, k, g * P:(g + 1) * P], sc[:, 2 * k:2 * k + 2], start=(k == 0), stop=(k == KD - 1))
                        mm.then_inc(slab_used, 1)

        @block.scalar
        def _(act):
            act.wait_ge(small_in, 32)
            nc.scalar.activation(sig, m.small[:, S_C:S_C + 2 * KD], ACT.Sigmoid).then_inc(silu_c, 1)
            for n in range(1, 12, 2):
                act.wait_ge(turned, n + 1)
                nc.scalar.copy(m.X[:, 4:8, (n // 2) * P:(n // 2 + 1) * P],
                               m.psum[n % 6][:, :].rearrange("p (k t) -> p k t", k=4)).then_inc(odd_out, 1)

        @block.vector
        def _(dve):
            dve.wait_ge(silu_c, 1)
            nc.vector.tensor_tensor(sc, sig, m.small[:, S_C:S_C + 2 * KD], ALU.mult).then_inc(silu_c, 1)
            for n in range(0, 12, 2):
                dve.wait_ge(turned, n + 1)
                nc.vector.tensor_copy(m.X[:, 0:4, (n // 2) * P:(n // 2 + 1) * P],
                                      m.psum[n % 6][:, :].rearrange("p (k t) -> p k t", k=4)).then_inc(even_out, 1)
            dve.wait_ge(slab_used, SLOTS + 2 * slabs)
            for l in range(2):
                b = m.small[:, S_ADAB + 48 * l:S_ADAB + 48 * l + 48].unsqueeze(2).broadcast_to([P, 48, 2])
                nc.vector.tensor_tensor(m.mod[:, 96 * l:96 * l + 96].rearrange("p (g v) -> p g v", v=2),
                                        m.psum[6 + l][:, 0:96].rearrange("p (g v) -> p g v", v=2), b, ALU.add).then_inc(mod_sum, 1)
            dve.wait_ge(mod_sum, 2)
            for l in range(2):
                for n in range(2):
                    g = m.small[:, S_NORM + (2 * l + n) * KD:S_NORM + (2 * l + n + 1) * KD]
                    nc.vector.scalar_tensor_tensor(
                        out=m.MODA[:, l, n], in0=m.MOD[:, l, 1 + 3 * n], scalar=1.0,
                        in1=g.unsqueeze(2).broadcast_to([P, KD, 2]), op0=ALU.add, op1=ALU.mult).then_inc(mod_scale, 1)


def norm_modulate(m, name, layer, norm, to_reference_order=False, first=0):
    nc = m.nc
    even_sq, odd_sq, summed, root, rstd_ok, scaled, hidden = semaphores(
        m, name, "even_sq odd_sq summed root rstd_ok scaled hidden")
    n_tok = TOK - first
    SQ = 4
    sq = cut(m, 0, SQ * TOK).rearrange("p (s t) -> p s t", s=SQ)
    rstd = cut(m, SQ * TOK, TOK)
    norm_x = cut(m, (SQ + 1) * TOK, KD * TOK).rearrange("p (k t) -> p k t", k=KD)
    parts = [(256, 768, 0)] + ([(0, 256, 1)] if first == 0 else [])
    with nc.Block() as block:

        @block.gpsimd
        def _(pool):
            for k in range(0, KD, 2):
                if k >= SQ:
                    pool.wait_ge(summed, k - SQ + 1)
                nc.gpsimd.tensor_tensor(sq[:, k % SQ, first:TOK], m.X[:, k, first:TOK], m.X[:, k, first:TOK],
                                        ALU.mult).then_inc(even_sq, 1)

        @block.tensor
        def _(pe):
            for k in range(KD):
                pe.wait_ge((even_sq, odd_sq)[k % 2], k // 2 + 1)
                for b, (t0, t1, _) in enumerate(parts):
                    mm = nc.tensor.matmul(m.psum[b][:, 0:t1 - t0], const(m, C_MEAN), sq[:, k % SQ, t0:t1],
                                          start=(k == 0), stop=(k == KD - 1))
                mm.then_inc(summed, 1)

        @block.scalar
        def _(act):
            for k in range(1, KD, 2):
                if k >= SQ:
                    act.wait_ge(summed, k - SQ + 1)
                nc.scalar.activation(sq[:, k % SQ, first:TOK], m.X[:, k, first:TOK], ACT.Square).then_inc(odd_sq, 1)
            act.wait_ge(summed, KD)
            for b, (t0, t1, _) in enumerate(parts):
                nc.scalar.activation(rstd[:, t0:t1], m.psum[b][:, 0:t1 - t0], ACT.Sqrt,
                                     bias=const(m, C_EPS, 1)).then_inc(root, 1)
            for k in range(KD):
                act.wait_ge(scaled, k + 1)
                for t0, t1, v in parts:
                    src, dst = norm_x[:, k, t0:t1], m.H[:, k, t0:t1]
                    if to_reference_order and v == 0:
                        src = src.rearrange("p (c r) -> p r c", r=GRID_R)
                        dst = dst.rearrange("p (r c) -> p r c", r=GRID_R)
                    nc.scalar.activation(dst, src, ACT.Identity, bias=m.MOD[:, layer, 3 * norm, k, v:v + 1],
                                         scale=m.MODA[:, layer, norm, k, v:v + 1]).then_inc(hidden, 1)

        @block.vector
        def _(dve):
            dve.wait_ge(root, len(parts))
            nc.vector.reciprocal(rstd[:, first:TOK], rstd[:, first:TOK]).then_inc(rstd_ok, 1)
            dve.wait_ge(rstd_ok, 1)
            for k in range(KD):
                nc.vector.tensor_tensor(norm_x[:, k, first:TOK], m.X[:, k, first:TOK], rstd[:, first:TOK],
                                        ALU.mult).then_inc(scaled, 1)


def neighbourhood_attention(m):
    nc, dram = m.nc, m.dram
    (projected, squared, stat, root, inv, qk_ready, v_ready, shifted, bias_ready, scored, biased, staged, maxed, exped, inverted, probs,
     turned, turned_out, weighted, out_copied, w_free, bias_free) = semaphores(
        m, "na", "projected squared stat root inv qk_ready v_ready shifted bias_ready scored biased staged maxed exped inverted probs "
                 "turned turned_out weighted out_copied w_free bias_free")
    w_in = semaphores(m, "na", "w_in0 w_in1")
    bias_in, = semaphores(m, "na", "bias_in")
    at = [0]

    def area(cols):
        at[0] += cols
        return cut(m, at[0] - cols, cols)

    m.O = area(KD * TOK).rearrange("p (k t) -> p k t", k=KD)
    m.O_first = 0
    q, k_, sq, rs = (area(TOK) for _ in range(4))
    sq2, rs2 = area(TOK), area(TOK)
    v = area(TOK).rearrange("p (t n) -> p t n", t=6)
    vs = area(3 * P).rearrange("p (t n) -> p t n", t=3)
    table = area(2 * BIAS_RUN).rearrange("p (h n) -> p h n", h=2)
    bm = area(6 * WIN).rearrange("p (h v n) -> p h v n", h=2, v=3)
    NS = 3
    S = area(NS * BANK).rearrange("p (s n) -> p s n", s=NS)
    PT = area(2 * BANK).rearrange("p (s n) -> p s n", s=2)
    stats = area(4 * NS)
    assert at[0] <= 19500
    ident = const(m, C_IDENT)
    wv = dram["na_w_qkv"].rearrange("(k p) (s n) -> p s k n", p=P, s=3)
    UNITS = [(h, j) for h in range(2) for j in range(6)]
    PAIRS_IN_BODY = 2

    def bias_source(pair, h):
        return bass.AP(tensor=dram["bias"].tensor, offset=(pair * 2 + h) * (BIAS_DC * DR),
                       ap=[[DR, 16], [1, 8], [1, BIAS_RUN]])

    with nc.Block() as block:

        @block.sync
        def _(sp):
            with sp.Fori(0, NA_PAIRS // PAIRS_IN_BODY) as i:
                for u in range(PAIRS_IN_BODY):
                    pair = i * PAIRS_IN_BODY + u
                    sp.wait_ge(w_free, pair + 1)
                    for s in range(3):
                        sp.dma_start(slot(m, u)[:, s * KD * P:(s + 1) * KD * P].rearrange("p (k n) -> p k n", k=KD),
                                     wv[:, s, :, bass.ds(pair * P, P)]).then_inc(w_in[u], 16)
                    sp.wait_ge(bias_free, pair + 1)
                    for h in range(2):
                        sp.dma_start(table[:, h, :], bias_source(pair, h)).then_inc(bias_in, 16)
                    sp.wait_ge(v_ready, pair * 2 + 2)
                    sp.wait_ge(weighted, pair * 12 + 1)
                    sp.dma_start(vs[0:64, :, :], v[64:128, 2:5, :]).then_inc(shifted, 16)
                    sp.dma_start(vs[64:128, :, :], v[0:64, 3:6, :]).then_inc(shifted, 16)

        @block.gpsimd
        def _(pool):
            pool.sem_inc(bias_free, 1)
            with pool.Fori(0, NA_PAIRS) as pair:
                pool.wait_ge(bias_in, pair * 32 + 32)
                pool.wait_ge(staged, pair * 12 + 1)
                for h in range(2):
                    for var in range(3):
                        src = table[:, h, :].rearrange("p (c r) -> p c r", r=DR)
                        last = 47 - WIN_SHIFT[var]
                        src = src[:, last - 31:last + 1, 0:WIN_R][:, ::-1, ::-1]
                        mask = const(m, C_WMASK + 32 * var, 32).unsqueeze(2).broadcast_to([P, 32, WIN_R])
                        op = nc.gpsimd.tensor_tensor(bm[:, h, var, :].rearrange("p (c r) -> p c r", r=WIN_R),
                                                     src, mask, ALU.add)
                        op.then_inc(bias_ready, 1)
                pool.wait_ge(bias_ready, pair * 6 + 6)
                pool.sem_inc(bias_free, 1)

        @block.tensor
        def _(pe):
            pe.sem_inc(weighted, 1)
            pe.sem_inc(stat, 1)

            def proj(bank, c0, w, t0, t1):
                for k in range(KD):
                    mm = nc.tensor.matmul(m.psum[bank][:, c0:c0 + t1 - t0], w[:, k, :], m.H[:, k, t0:t1],
                                          start=(k == 0), stop=(k == KD - 1))
                return mm

            with pe.Fori(0, NA_PAIRS // PAIRS_IN_BODY) as i:
                for u in range(PAIRS_IN_BODY):
                    pair = i * PAIRS_IN_BODY + u
                    w = [slot(m, u)[:, s * KD * P:(s + 1) * KD * P].rearrange("p (k n) -> p k n", k=KD) for s in range(3)]
                    pe.wait_ge(w_in[u], i * 48 + 48)
                    pe.wait_ge(out_copied, pair * 2 + 1)
                    proj(0, 0, w[0], CTX, TOK).then_inc(projected, 1)
                    proj(1, 0, w[1], CTX, TOK).then_inc(projected, 1)
                    proj(2, 0, w[0], 0, CTX)
                    proj(2, CTX, w[1], 0, CTX).then_inc(projected, 1)
                    for t in range(6):
                        for k in range(KD):
                            mm = nc.tensor.matmul(m.psum[3 + t // 4][:, (t % 4) * P:(t % 4 + 1) * P], m.H[:, k, t * P:(t + 1) * P],
                                                  w[2][:, k, :], start=(k == 0), stop=(k == KD - 1))
                        if t == 3:
                            mm.then_inc(projected, 1)
                    mm.then_inc(projected, 1)
                    for n, src in enumerate((sq[:, CTX:TOK], sq2[:, CTX:TOK], None)):
                        pe.wait_ge(squared, pair * 4 + (n + 1 if n < 2 else 4))
                        if n < 2:
                            nc.tensor.matmul(m.psum[5 + n][:, :], const(m, C_HALF), src, start=True, stop=True).then_inc(stat, 1)
                        else:
                            nc.tensor.matmul(m.psum[7][:, 0:CTX], const(m, C_HALF), sq[:, 0:CTX], start=True, stop=True)
                            nc.tensor.matmul(m.psum[7][:, CTX:2 * CTX], const(m, C_HALF), sq2[:, 0:CTX],
                                             start=True, stop=True).then_inc(stat, 1)

                    def scores(n):
                        h, j = UNITS[n]
                        at_h = slice(64 * h, 64 * h + 64)
                        if n >= 2:
                            pe.wait_ge(staged, pair * 12 + n)
                        out = m.psum[n % 2]
                        qs = q[at_h, CTX + j * P:CTX + (j + 1) * P] if j < 4 else q[at_h, (j - 4) * P:(j - 3) * P]
                        if j < 4:
                            k0 = CTX + WIN_START[j]
                            nc.tensor.matmul(out[:, 0:WIN], qs, k_[at_h, k0:k0 + WIN], start=True, stop=True)
                        nc.tensor.matmul(out[:, WIN:WIN + CTX], qs, k_[at_h, 0:CTX], start=True, stop=True).then_inc(scored, 1)

                    def turn(n):
                        pe.wait_ge(probs, pair * 12 + n + 1)
                        if n >= 2:
                            pe.wait_ge(turned_out, pair * 12 + n)
                        for c in range(0 if UNITS[n][1] < 4 else 2, 4):
                            mm = nc.tensor.transpose(m.psum[(5, 6)[n % 2]][:, c * P:(c + 1) * P], S[:, n % NS, c * P:(c + 1) * P], ident)
                        mm.then_inc(turned, 1)

                    def weigh(n):
                        h, j = UNITS[n]
                        pe.wait_ge(turned_out, pair * 12 + n + 2)
                        if j < 4:
                            near = [(v, 2), (vs, 0), (vs, 1), (v, 4)][j]
                            vals = [near[0][:, near[1], :], near[0][:, near[1] + 1, :], v[:, 0, :], v[:, 1, :]]
                            out = m.psum[3][64 * h:64 * h + 64, j * P:(j + 1) * P]
                            chunks = range(4)
                        else:
                            vals = [None, None, v[:, 0, :], v[:, 1, :]]
                            out = m.psum[4][64 * h:64 * h + 64, (j - 4) * P:(j - 3) * P]
                            chunks = range(2, 4)
                        for c in chunks:
                            mm = nc.tensor.matmul(out, vals[c][:, 64 * h:64 * h + 64], PT[:, n % 2, c * P:(c + 1) * P],
                                                  start=(c == chunks[0]), stop=(c == 3))
                        mm.then_inc(weighted, 1)

                    pe.wait_ge(qk_ready, pair * 4 + 4)
                    scores(0)
                    scores(1)
                    pe.wait_ge(v_ready, pair * 2 + 2)
                    pe.wait_ge(shifted, pair * 32 + 32)
                    for n in range(12):
                        turn(n)
                        if n + 2 < 12:
                            scores(n + 2)
                        if n:
                            weigh(n - 1)
                    weigh(11)

        @block.scalar
        def _(act):
            act.sem_inc(turned_out, 1)
            act.sem_inc(w_free, 2)
            with act.Fori(0, NA_PAIRS) as pair:
                act.wait_ge(projected, pair * 5 + 1)
                act.wait_ge(stat, pair * 3 + 1)
                nc.scalar.activation(sq[:, CTX:TOK], m.psum[0][:, :], ACT.Square).then_inc(squared, 1)
                act.wait_ge(projected, pair * 5 + 2)
                nc.scalar.activation(sq2[:, CTX:TOK], m.psum[1][:, :], ACT.Square).then_inc(squared, 1)
                act.wait_ge(projected, pair * 5 + 3)
                nc.scalar.activation(sq[:, 0:CTX], m.psum[2][:, 0:CTX], ACT.Square).then_inc(squared, 1)
                nc.scalar.activation(sq2[:, 0:CTX], m.psum[2][:, CTX:2 * CTX], ACT.Square).then_inc(squared, 1)
                act.wait_ge(weighted, pair * 12 + 1)
                act.wait_ge(projected, pair * 5 + 5)
                act.sem_inc(w_free, 1)
                nc.scalar.copy(v[:, 0:4, :], m.psum[3][:, :].rearrange("p (t n) -> p t n", t=4)).then_inc(v_ready, 1)
                nc.scalar.copy(v[:, 4:6, :], m.psum[4][:, 0:2 * P].rearrange("p (t n) -> p t n", t=2)).then_inc(v_ready, 1)
                e1, e64 = const(m, C_EPS, 1), const(m, C_EPS + 1, 1)
                for n, (dst, src, scale, eps) in enumerate((
                        (rs[:, CTX:TOK], m.psum[5][:, :], 64.0, e64), (rs2[:, CTX:TOK], m.psum[6][:, :], 1.0, e1),
                        (rs[:, 0:CTX], m.psum[7][:, 0:CTX], 64.0, e64), (rs2[:, 0:CTX], m.psum[7][:, CTX:2 * CTX], 1.0, e1))):
                    act.wait_ge(stat, pair * 3 + min(n, 2) + 2)
                    nc.scalar.activation(dst, src, ACT.Sqrt, bias=eps, scale=scale).then_inc(root, 1)

                def exp(n):
                    lo = 0 if UNITS[n][1] < 4 else WIN
                    b = 4 * (n % NS)
                    act.wait_ge(maxed, pair * 12 + n + 1)
                    nc.scalar.activation(S[:, n % NS, lo:BANK], S[:, n % NS, lo:BANK], ACT.Exp,
                                         bias=stats[:, b:b + 1], accum_out=stats[:, b + 2:b + 3]).then_inc(exped, 1)

                def copy_out(n):
                    lo = 0 if UNITS[n][1] < 4 else WIN
                    act.wait_ge(turned, pair * 12 + n + 1)
                    if n >= 2:
                        act.wait_ge(weighted, pair * 12 + n)
                    nc.scalar.copy(PT[:, n % 2, lo:BANK], m.psum[(5, 6)[n % 2]][:, lo:BANK]).then_inc(turned_out, 1)

                exp(0)
                for n in range(12):
                    if n + 1 < 12:
                        exp(n + 1)
                    copy_out(n)

        @block.vector
        def _(dve):
            dve.sem_inc(out_copied, 1)
            dve.sem_inc(staged, 1)
            with dve.Fori(0, NA_PAIRS) as pair:
                srcs = ((q, rs, CTX, TOK, m.psum[0][:, :], 0), (k_, rs2, CTX, TOK, m.psum[1][:, :], 1),
                        (q, rs, 0, CTX, m.psum[2][:, 0:CTX], 0), (k_, rs2, 0, CTX, m.psum[2][:, CTX:2 * CTX], 1))
                for n, (dst, r, t0, t1, src, g) in enumerate(srcs):
                    dve.wait_ge(root, pair * 4 + n + 1)
                    nc.vector.reciprocal(r[:, t0:t1], r[:, t0:t1]).then_inc(inv, 1)
                    dve.wait_ge(inv, pair * 4 + n + 1)
                    nc.vector.scalar_tensor_tensor(out=dst[:, t0:t1], in0=src, scalar=m.small[:, S_QN + g:S_QN + g + 1],
                                                   in1=r[:, t0:t1], op0=ALU.mult, op1=ALU.mult).then_inc(qk_ready, 1)

                def stage(n):
                    h, j = UNITS[n]
                    b = 4 * (n % NS)
                    lo = 0 if j < 4 else WIN
                    dve.wait_ge(scored, pair * 12 + n + 1)
                    if n >= NS:
                        dve.wait_ge(turned, pair * 12 + n - NS + 1)
                    if n == 0:
                        dve.wait_ge(bias_ready, pair * 6 + 6)
                    if j < 4:
                        nc.vector.tensor_tensor(S[:, n % NS, 0:WIN], m.psum[n % 2][:, 0:WIN], bm[:, h, WIN_VARIANT[j], :],
                                                ALU.add).then_inc(biased, 1)
                    nc.vector.tensor_copy(S[:, n % NS, WIN:BANK], m.psum[n % 2][:, WIN:BANK]).then_inc(staged, 1)
                    if j < 4:
                        dve.wait_ge(biased, pair * 8 + 4 * h + j + 1)
                    dve.wait_ge(staged, pair * 12 + n + 2)
                    nc.vector.tensor_reduce(stats[:, b:b + 1], S[:, n % NS, lo:BANK], AX.X, ALU.max, negate=True).then_inc(maxed, 1)

                def normalise(n):
                    b = 4 * (n % NS)
                    lo = 0 if UNITS[n][1] < 4 else WIN
                    dve.wait_ge(exped, pair * 12 + n + 1)
                    nc.vector.reciprocal(stats[:, b + 3:b + 4], stats[:, b + 2:b + 3]).then_inc(inverted, 1)
                    dve.wait_ge(inverted, pair * 12 + n + 1)
                    nc.vector.tensor_scalar(S[:, n % NS, lo:BANK], S[:, n % NS, lo:BANK], stats[:, b + 3:b + 4], None,
                                            ALU.mult).then_inc(probs, 1)

                order = [("s", 0)]
                for n in range(12):
                    order += ([("s", n + 1)] if n + 1 < 12 else []) + [("n", n)]
                for what, n in order:
                    (stage if what == "s" else normalise)(n)
                dve.wait_ge(weighted, pair * 12 + 13)
                nc.vector.tensor_copy(m.O[:, bass.ds(pair, 1), CTX:TOK], m.psum[3][:, :].unsqueeze(1)).then_inc(out_copied, 1)
                nc.vector.tensor_copy(m.O[:, bass.ds(pair, 1), 0:CTX], m.psum[4][:, 0:CTX].unsqueeze(1)).then_inc(out_copied, 1)


def ring_steps(n_slabs, n_slots):
    steps = []
    for j in range(n_slabs):
        same = [x for x in range(n_slabs) if x % n_slots == j % n_slots]
        at = same.index(j)
        before = n_slabs + same[at - 1] + 1 if at else same[-1] + 1
        steps.append((j % n_slots, len(same), at + 1, before))
    return steps


def project_to_residual(m, name, weight, layer, first):
    nc = m.nc
    w_in = semaphores(m, name, "w_in0 w_in1")
    product, added = semaphores(m, name, "product added")
    parts = [(CTX, TOK, 0)] + ([(0, CTX, 1)] if first == 0 else [])
    w = weight.rearrange("(k p) n -> p k n", p=P)
    with nc.Block() as block:

        @block.sync
        def _(sp):
            for s in range(2):
                sp.dma_start(slot(m, s).rearrange("p (k n) -> p k n", k=KD), w[:, :, s * BANK:(s + 1) * BANK]).then_inc(w_in[s], 16)

        @block.tensor
        def _(pe):
            for g in range(KD):
                pe.wait_ge(w_in[g // 4], 16)
                if g >= 4:
                    pe.wait_ge(added, (g - 3) * len(parts))
                ws = slot(m, g // 4).rearrange("p (k n) -> p k n", k=KD)
                for b, (t0, t1, _) in enumerate(parts):
                    for k in range(KD):
                        mm = nc.tensor.matmul(m.psum[2 * (g % 4) + b][:, 0:t1 - t0], ws[:, k, (g % 4) * P:(g % 4 + 1) * P],
                                              m.O[:, k, t0 - m.O_first:t1 - m.O_first], start=(k == 0), stop=(k == KD - 1))
                    mm.then_inc(product, 1)

        @block.vector
        def _(dve):
            for g in range(KD):
                for b, (t0, t1, v) in enumerate(parts):
                    dve.wait_ge(product, g * len(parts) + b + 1)
                    nc.vector.scalar_tensor_tensor(out=m.X[:, g, t0:t1], in0=m.psum[2 * (g % 4) + b][:, 0:t1 - t0],
                                                   scalar=m.MOD[:, layer, 2, g, v:v + 1], in1=m.X[:, g, t0:t1],
                                                   op0=ALU.mult, op1=ALU.add).then_inc(added, 1)


def swiglu(m):
    nc, dram = m.nc, m.dram
    FK = FFN // P
    CHUNKS = 2
    w_in = semaphores(m, "ffn", "w_in0 w_in1")
    out_in = semaphores(m, "ffn", "out_in0 out_in1 out_in2 out_in3")
    product, gated, silu_ok, out_product, added = semaphores(m, "ffn", "product gated silu_ok out_product added")
    G = cut(m, 0, FK * TOK).rearrange("p (k t) -> p k t", k=FK)
    sa = cut(m, FK * TOK, 2 * TOK).rearrange("p (s t) -> p s t", s=2)
    wi = dram["ffn_w_in"][0].rearrange("(k p) (s n) -> p s k n", p=P, s=2)
    wo = dram["ffn_w_out"][0].rearrange("(k p) n -> p k n", p=P)
    half = KD * P

    def in_slab(s):
        return slot(m, s)[:, 0:2 * half].rearrange("p (s k n) -> p s k n", s=2, k=KD)

    def out_slab(s):
        return slot(m, s)[:, 0:FK * P].rearrange("p (k n) -> p k n", k=FK)

    with nc.Block() as block:

        @block.sync
        def _(sp):
            for g in range(2):
                sp.dma_start(out_slab(2 + g), wo[:, :, g * P:(g + 1) * P]).then_inc(out_in[g], 16)
            with sp.Fori(0, FK // CHUNKS) as i:
                for c in range(CHUNKS):
                    sp.wait_ge(gated, i * (2 * CHUNKS) + 2 * c + 2)
                    for ab in range(2):
                        sp.dma_start(in_slab(c)[:, ab], wi[:, ab, :, bass.ds(i * (CHUNKS * P) + c * P, P)]).then_inc(w_in[c], 16)
            for g in range(2, KD):
                if g < 4:
                    sp.wait_ge(gated, 2 * CHUNKS + 2 * (FK + g - 3))
                else:
                    sp.wait_ge(out_product, (g - 3) * 2)
                sp.dma_start(out_slab((g + 2) % 4), wo[:, :, g * P:(g + 1) * P]).then_inc(out_in[g % 4], 16)

        @block.tensor
        def _(pe):
            pe.sem_inc(gated, 2 * CHUNKS)
            with pe.Fori(0, FK // CHUNKS) as i:
                for c in range(CHUNKS):
                    pe.wait_ge(w_in[c], i * 32 + 32)
                    pe.wait_ge(gated, i * (2 * CHUNKS) + 2 * c + 2)
                    w, bank = in_slab(c), 4 * c
                    for ab in range(2):
                        for k in range(KD):
                            mm = nc.tensor.matmul(m.psum[bank + ab][:, :], w[:, ab, k, :], m.H[:, k, CTX:TOK],
                                                  start=(k == 0), stop=(k == KD - 1))
                    mm.then_inc(product, 1)
                    for ab in range(2):
                        for k in range(KD):
                            mm = nc.tensor.matmul(m.psum[bank + 2 + ab][:, 0:CTX], w[:, ab, k, :], m.H[:, k, 0:CTX],
                                                  start=(k == 0), stop=(k == KD - 1))
                    mm.then_inc(product, 1)
            for g in range(KD):
                pe.wait_ge(out_in[g % 4], 16 * (g // 4 + 1))
                if g < 4:
                    pe.wait_ge(gated, 2 * FK + 2 * CHUNKS)
                else:
                    pe.wait_ge(added, (g - 3) * 2)
                for b, (t0, t1) in enumerate(((CTX, TOK), (0, CTX))):
                    for k in range(FK):
                        mm = nc.tensor.matmul(m.psum[2 * (g % 4) + b][:, 0:t1 - t0], out_slab((g + 2) % 4)[:, k, :], G[:, k, t0:t1],
                                              start=(k == 0), stop=(k == FK - 1))
                    mm.then_inc(out_product, 1)

        @block.scalar
        def _(act):
            with act.Fori(0, FK // CHUNKS) as i:
                for c in range(CHUNKS):
                    act.wait_ge(gated, i * (2 * CHUNKS) + 2 * c + 2)
                    for b, (t0, t1) in enumerate(((CTX, TOK), (0, CTX))):
                        act.wait_ge(product, i * (2 * CHUNKS) + 2 * c + b + 1)
                        nc.scalar.activation(sa[:, c, t0:t1], m.psum[4 * c + 2 * b][:, 0:t1 - t0], ACT.Silu).then_inc(silu_ok, 1)

        @block.vector
        def _(dve):
            with dve.Fori(0, FK // CHUNKS) as i:
                for c in range(CHUNKS):
                    for b, (t0, t1) in enumerate(((CTX, TOK), (0, CTX))):
                        dve.wait_ge(silu_ok, i * (2 * CHUNKS) + 2 * c + b + 1)
                        nc.vector.tensor_tensor(G[:, bass.ds(i * CHUNKS + c, 1), t0:t1], sa[:, c, t0:t1].unsqueeze(1),
                                                m.psum[4 * c + 2 * b + 1][:, 0:t1 - t0].unsqueeze(1), ALU.mult).then_inc(gated, 1)
            for g in range(KD):
                for b, (t0, t1) in enumerate(((CTX, TOK), (0, CTX))):
                    dve.wait_ge(out_product, 2 * g + b + 1)
                    nc.vector.scalar_tensor_tensor(out=m.X[:, g, t0:t1], in0=m.psum[2 * (g % 4) + b][:, 0:t1 - t0],
                                                   scalar=m.MOD[:, 0, 5, g, b:b + 1], in1=m.X[:, g, t0:t1],
                                                   op0=ALU.mult, op1=ALU.add).then_inc(added, 1)


def reorder(m):
    nc = m.nc
    copied, = semaphores(m, "reorder", "copied")
    back, = semaphores(m, "reorder", "back")
    tmp = cut(m, 0, KD * LAT).rearrange("p (k t) -> p k t", k=KD)
    with nc.Block() as block:

        @block.vector
        def _(dve):
            for k in range(KD):
                nc.vector.tensor_copy(tmp[:, k, :].rearrange("p (r c) -> p r c", c=GRID_C),
                                      m.X[:, k, CTX:TOK].rearrange("p (c r) -> p r c", r=GRID_R)).then_inc(copied, 1)

        @block.scalar
        def _(act):
            for k in range(KD):
                act.wait_ge(copied, k + 1)
                nc.scalar.copy(m.X[:, k, CTX:TOK], tmp[:, k, :]).then_inc(back, 1)


def experts(m):
    nc, dram = m.nc, m.dram
    EK = EFF // P
    SLABS = 6
    ROUND = EXPERTS
    TURNS = 2 * EXPERTS
    HALF = 2 * P
    I32 = mybir.dt.int32
    w_in = semaphores(m, "moe", "w_in0 w_in1 w_in2")
    out_in = semaphores(m, "moe", "out_in0 out_in1")
    (h_turned, h_even, h_odd, logits, logits_ok, top, weights, route_exp, routed, ranked, rank_ok, table_ok, built, gathered, gather_out,
     sel_turned, sel_out, product, silu_ok, gated, turned, turned_out, summed, sum_out, scattered, now_ok, added) = semaphores(
        m, "moe", "h_turned h_even h_odd logits logits_ok top weights route_exp routed ranked rank_ok table_ok built gathered gather_out "
                  "sel_turned sel_out product silu_ok gated turned turned_out summed sum_out scattered now_ok added")
    at = [0]

    def area(cols):
        at[0] += cols
        assert at[0] <= 19500
        return cut(m, at[0] - cols, cols)

    HT = area(4 * D).rearrange("p (t d) -> p t d", t=4)
    XG = area(KD * HALF).rearrange("p (k s) -> p k s", k=KD)
    sa = area(2 * HALF * 2).rearrange("p (u b n) -> p u b n", u=2, b=2)
    G = area(2 * EFF).rearrange("p (b n) -> p b n", b=2)
    GT = area(2 * EFF).rearrange("p (b k s) -> p b k s", b=2, k=EK)
    SEL = area(4 * HALF).rearrange("p (t s) -> p t s", t=4)
    SELG = area(4 * HALF).rearrange("p (t s) -> p t s", t=4)
    SELT = area(2 * LAT).rearrange("p (b t) -> p b t", b=2)
    lg, idxf = (area(4 * 8).rearrange("p (t e) -> p t e", t=4) for _ in range(2))
    top8 = area(4 * 8).rearrange("p (t e) -> p t e", t=4)
    idx = area(4 * 8).bitcast(U32).rearrange("p (t e) -> p t e", t=4)
    eq = area(2 * 4 * 8).rearrange("p (w t e) -> p w t e", w=2, t=4)
    small = area(4 * 4).rearrange("p (w t) -> p w t", w=4)
    table = area(3 * (TURNS + 1) * 4).rearrange("p (c e t) -> p c e t", c=3, e=TURNS + 1)
    count = area(EXPERTS + 1)
    county = area(EXPERTS + 1).bitcast(I32)
    now = area(3 * 4).rearrange("p (c t) -> p c t", c=3)
    IN = KD * BANK
    out_tail = area((EK - KD) * BANK)
    out_pieces = (((0, EK, m.ht[:, 0:EK * BANK]),), ((0, KD, m.ring[:, 3 * IN:4 * IN]), (KD, EK, out_tail)))

    def in_slab(s):
        return m.ring[:, s * IN:(s + 1) * IN]

    def SUM(k, b):
        return m.X[:, k, b * P:(b + 1) * P]

    def out_weights(half, k):
        for k0, k1, piece in out_pieces[half]:
            if k0 <= k < k1:
                return piece[:, (k - k0) * BANK:(k - k0 + 1) * BANK]

    wi = dram["moe_w_in"].rearrange("l e (k p) (s n) -> (l e) p s k n", p=P, s=2)
    wo = dram["moe_w_out"].rearrange("l e (k p) n -> (l e) p k n", p=P)
    steps = ring_steps(SLABS, 3)
    ident = const(m, C_IDENT)
    B = m.psum
    Y_BANKS = ((5, 6), (7, 5))

    def width(s):
        return HALF if s < SLABS - 1 else P

    def rounds(eng, turn):
        eng.wait_ge(table_ok, 2)
        most = eng.value_load(county[0:1, EXPERTS:EXPERTS + 1], min_val=0, max_val=LAT)
        with eng.Fori(0, EXPERTS) as e:
            mine = eng.value_load(county[0:1, bass.ds(e, 1)], min_val=0, max_val=LAT)
            with eng.If(mine > P):
                turn(e, 2)
            with eng.Else():
                turn(e, 1)
        with eng.If(most > HALF):
            with eng.Fori(EXPERTS, TURNS) as it:
                turn(it, 2)

    with nc.Block() as block:

        @block.sync
        def _(sp):
            def turn(it, e):
                for j, (s, _, _, before) in enumerate(steps):
                    sp.wait_ge(product, it * SLABS + before)
                    n = width(j)
                    dst = in_slab(s)[:, 0:KD * 2 * n].rearrange("p (k s n) -> p s k n", k=KD, s=2)
                    for ab in range(2):
                        sp.dma_start(dst[:, ab], wi[bass.ds(e, 1), :, ab, :, j * HALF:j * HALF + n].rearrange("o p k n -> (o p) k n"))\
                            .then_inc(w_in[s], 16)
                for j in range(2):
                    sp.wait_ge(summed, it * 2 + j + 1)
                    for k0, k1, piece in out_pieces[j]:
                        sp.dma_start(piece.rearrange("p (k n) -> p k n", k=k1 - k0),
                                     wo[bass.ds(e, 1), :, k0:k1, j * BANK:(j + 1) * BANK].rearrange("o p k n -> (o p) k n"))\
                            .then_inc(out_in[j], 16)

            with sp.Fori(0, EXPERTS) as e:
                turn(e, e)
            sp.wait_ge(table_ok, 2)
            most = sp.value_load(county[0:1, EXPERTS:EXPERTS + 1], min_val=0, max_val=LAT)
            with sp.If(most > HALF):
                with sp.Fori(0, EXPERTS) as e:
                    turn(e + EXPERTS, e)

        @block.tensor
        def _(pe):
            pe.sem_inc(product, SLABS)
            for n in range(8):
                if n >= 4:
                    pe.wait_ge((h_even, h_odd)[n % 2], (n - 4) // 2 + 1)
                for k in range(4):
                    mm = nc.tensor.transpose(B[n % 4][:, k * P:(k + 1) * P],
                                             m.H[:, 4 * (n % 2) + k, CTX + (n // 2) * P:CTX + (n // 2 + 1) * P], ident)
                mm.then_inc(h_turned, 1)
            for t in range(4):
                for k in range(KD):
                    mm = nc.tensor.matmul(B[6][:, 8 * t:8 * t + 8], m.H[:, k, CTX + t * P:CTX + (t + 1) * P],
                                          m.small[:, S_RT + 8 * k:S_RT + 8 * k + 8], start=(k == 0), stop=(k == KD - 1))
            mm.then_inc(logits, 1)
            pe.sem_inc(summed, 2)
            pe.wait_ge(routed, 2)
            for t in range(5):
                last = min(t, 3)
                for u in range(last + 1):
                    mm = nc.tensor.matmul(B[7][:, 8 * t:8 * t + 8], const(m, C_BEFORE if u == t else C_ONES), idxf[:, u, :],
                                          start=(u == 0), stop=(u == last))
            mm.then_inc(ranked, 1)

            def turn(it, nb):
                N = nb * P
                pe.wait_ge(built, it + 1)
                for j in range(4):
                    pe.wait_ge(added, it * KD + 4 + j + 1)
                    for k in range(2 * j, 2 * j + 2):
                        for t in range(4):
                            mm = nc.tensor.matmul(B[j][:, (k % 2) * N:(k % 2 + 1) * N], HT[:, t, k * P:(k + 1) * P], SEL[:, t, 0:N],
                                                  start=(t == 0), stop=(t == 3))
                    mm.then_inc(gathered, 1)
                for b in range(nb):
                    for t in range(4):
                        mm = nc.tensor.transpose(B[6 + b][:, t * P:(t + 1) * P], SELG[:, t, b * P:(b + 1) * P], ident)
                mm.then_inc(sel_turned, 1)

                def up(s):
                    slot_, per, upto, _ = steps[s]
                    n = 2 * width(s)
                    pe.wait_ge(w_in[slot_], it * (32 * per) + 32 * upto)
                    if s >= 2:
                        pe.wait_ge(gated, it * SLABS + s - 1)
                    else:
                        pe.wait_ge(gather_out, it * 4 + 4)
                    w = in_slab(slot_)[:, 0:KD * n].rearrange("p (k n) -> p k n", k=KD)
                    for b in range(nb):
                        for k in range(KD):
                            mm = nc.tensor.matmul(B[2 * (s % 2) + b][:, 0:n], XG[:, k, b * P:(b + 1) * P], w[:, k, :],
                                                  start=(k == 0), stop=(k == KD - 1))
                    mm.then_inc(product, 1)

                def turn_hidden(s):
                    pe.wait_ge(gated, it * SLABS + s + 1)
                    if s >= 1:
                        pe.wait_ge(turned_out, it * SLABS + s)
                    for b in range(nb):
                        for k in range(width(s) // P):
                            mm = nc.tensor.transpose(B[4][:, (2 * b + k) * P:(2 * b + k + 1) * P],
                                                     G[:, b, s * HALF + k * P:s * HALF + (k + 1) * P], ident)
                    mm.then_inc(turned, 1)

                for s in range(SLABS):
                    up(s)
                    if s:
                        turn_hidden(s - 1)
                for half in range(2):
                    pe.wait_ge(out_in[half], it * (16 * len(out_pieces[half])) + 16 * len(out_pieces[half]))
                    for b in range(nb):
                        bank = Y_BANKS[half][b]
                        if (half, b) == (0, 0):
                            pe.wait_ge(sel_out, it + 1)
                        if (half, b) == (1, 1):
                            pe.wait_ge(sum_out, it * 2 + 1)
                        for k in range(EK):
                            if (half, b) == (0, 0):
                                if k == 0:
                                    pe.wait_ge(turned_out, it * SLABS + 4)
                                if k == 6:
                                    turn_hidden(SLABS - 1)
                                if k == 8:
                                    pe.wait_ge(turned_out, it * SLABS + SLABS)
                            mm = nc.tensor.matmul(B[bank][:, :], GT[:, b, k, :], out_weights(half, k), start=(k == 0), stop=(k == EK - 1))
                    mm.then_inc(summed, 1)
                for k in range(KD):
                    if k == 0 or k == 4:
                        pe.wait_ge(sum_out, it * 2 + k // 4 + 1)
                    if k >= 4:
                        pe.wait_ge(added, it * KD + KD + k - 3)
                    for b in range(nb):
                        mm = nc.tensor.matmul(B[k % 4][:, :], SUM(k, b), SELT[:, b, :], start=(b == 0), stop=(b == nb - 1))
                    mm.then_inc(scattered, 1)

            rounds(pe, turn)

        @block.scalar
        def _(act):
            for n in range(1, 8, 2):
                act.wait_ge(h_turned, n + 1)
                nc.scalar.copy(HT[:, n // 2, BANK:D], B[n % 4][:, :]).then_inc(h_odd, 1)
            act.wait_ge(weights, 1)
            nc.scalar.activation(small[:, 1, :], small[:, 0, :], ACT.Exp).then_inc(route_exp, 1)

            def turn(it, nb):
                N = nb * P
                for j in range(4):
                    act.wait_ge(gathered, it * 4 + j + 1)
                    nc.scalar.copy(XG[:, 2 * j:2 * j + 2, 0:N], B[j][:, 0:2 * N].rearrange("p (k s) -> p k s", k=2)).then_inc(gather_out, 1)

                def silu(s):
                    n = width(s)
                    act.wait_ge(product, it * SLABS + SLABS + s + 1)
                    for b in range(nb):
                        op = nc.scalar.activation(sa[:, s % 2, b, 0:n], B[2 * (s % 2) + b][:, 0:n], ACT.Silu)
                    op.then_inc(silu_ok, 1)

                def copy_hidden(s):
                    k = width(s) // P
                    act.wait_ge(turned, it * SLABS + s + 1)
                    nc.scalar.copy(GT[:, 0:nb, 2 * s:2 * s + k, :],
                                   B[4][:, 0:nb * 2 * P].rearrange("p (b k s) -> p b k s", b=nb, k=2)[:, :, 0:k, :]).then_inc(turned_out, 1)

                silu(0)
                for s in range(1, SLABS):
                    silu(s)
                    copy_hidden(s - 1)
                copy_hidden(SLABS - 1)
                for half in range(2):
                    act.wait_ge(summed, it * 2 + 2 + half + 1)
                    for b in range(nb):
                        op = nc.scalar.copy(m.X[:, 4 * half:4 * half + 4, b * P:(b + 1) * P],
                                            B[Y_BANKS[half][b]][:, :].rearrange("p (k n) -> p k n", k=4))
                    op.then_inc(sum_out, 1)

            rounds(act, turn)

        @block.vector
        def _(dve):
            dve.sem_inc(added, KD)
            for n in range(0, 8, 2):
                dve.wait_ge(h_turned, n + 1)
                nc.vector.tensor_copy(HT[:, n // 2, 0:BANK], B[n % 4][:, :]).then_inc(h_even, 1)
            dve.wait_ge(logits, 1)
            nc.vector.tensor_copy(lg, B[6][:, 0:32].rearrange("p (t e) -> p t e", t=4)).then_inc(logits_ok, 1)
            dve.wait_ge(logits_ok, 1)
            for t in range(4):
                nc.vector.max(top8[:, t, :], lg[:, t, :]).then_inc(top, 1)
            dve.wait_ge(top, 4)
            for t in range(4):
                nc.vector.max_index(idx[:, t, :], top8[:, t, :], lg[:, t, :]).then_inc(top, 1)
            nc.vector.tensor_tensor(small[:, 0, :], top8[:, :, 1], top8[:, :, 0], ALU.subtract).then_inc(weights, 1)
            dve.wait_ge(top, 8)
            nc.vector.tensor_copy(idxf, idx).then_inc(top, 1)
            dve.wait_ge(top, 9)
            iota = const(m, C_IOTA, EXPERTS).unsqueeze(1).broadcast_to([P, 4, EXPERTS])
            for w in range(2):
                nc.vector.tensor_tensor(eq[:, w], idxf[:, :, w:w + 1].broadcast_to([P, 4, EXPERTS]), iota, ALU.is_equal).then_inc(top, 1)
            dve.wait_ge(top, 11)
            nc.vector.tensor_tensor(idxf, eq[:, 0], eq[:, 1], ALU.add).then_inc(routed, 2)
            dve.wait_ge(route_exp, 1)
            nc.vector.tensor_scalar(small[:, 2, :], small[:, 1, :], 1.0, None, ALU.add).then_inc(weights, 1)
            dve.wait_ge(weights, 2)
            nc.vector.reciprocal(small[:, 2, :], small[:, 2, :]).then_inc(weights, 1)
            dve.wait_ge(weights, 3)
            nc.vector.tensor_tensor(small[:, 3, :], small[:, 1, :], small[:, 2, :], ALU.mult).then_inc(weights, 1)
            dve.wait_ge(weights, 4)
            dve.wait_ge(routed, 2)
            for w in range(2):
                nc.vector.tensor_tensor(eq[:, w], eq[:, w], small[:, 2 + w, :].unsqueeze(2).broadcast_to([P, 4, EXPERTS]),
                                        ALU.mult).then_inc(top, 1)
            dve.wait_ge(top, 13)
            for r in range(2):
                def of(c):
                    return table[:, c, r * EXPERTS:(r + 1) * EXPERTS, :].rearrange("p e t -> p t e")
                nc.vector.tensor_tensor(of(0), eq[:, 0], eq[:, 1], ALU.add).then_inc(rank_ok, 1)
                nc.vector.tensor_copy(of(1), idxf).then_inc(rank_ok, 1)
            nc.vector.memset(table[:, :, TURNS, :], 0.0).then_inc(rank_ok, 1)
            dve.wait_ge(ranked, 1)
            ranks = B[7][:, 0:32].rearrange("p (t e) -> p t e", t=4)
            for r in range(2):
                nc.vector.tensor_scalar(table[:, 2, r * EXPERTS:(r + 1) * EXPERTS, :].rearrange("p e t -> p t e"), ranks, float(-HALF * r),
                                        None, ALU.add).then_inc(rank_ok, 1)
            nc.vector.tensor_copy(count[:, 0:EXPERTS], B[7][:, 32:40]).then_inc(rank_ok, 1)
            dve.wait_ge(rank_ok, 8)
            nc.vector.tensor_reduce(count[:, EXPERTS:EXPERTS + 1], count[:, 0:EXPERTS], AX.X, ALU.max).then_inc(table_ok, 1)
            dve.wait_ge(table_ok, 1)
            nc.vector.tensor_copy(county, count).then_inc(table_ok, 1)
            slots = const(m, C_SLOT, HALF)

            def one_hots():
                for dst, c in ((SEL, 1), (SELG, 0)):
                    for t in range(4):
                        op = nc.vector.tensor_scalar(dst[:, t, :], slots, now[:, 2, t:t + 1], now[:, c, t:t + 1], ALU.is_equal, ALU.mult)
                op.then_inc(built, 1)

            nc.vector.tensor_copy(now, table[:, :, 0, :]).then_inc(now_ok, 1)
            dve.wait_ge(now_ok, 1)
            one_hots()

            def turn(it, nb):
                dve.wait_ge(sel_turned, it + 1)
                for b in range(nb):
                    op = nc.vector.tensor_copy(SELT[:, b, :], B[6 + b][:, :])
                op.then_inc(sel_out, 1)
                for s in range(SLABS):
                    n = width(s)
                    dve.wait_ge(silu_ok, it * SLABS + s + 1)
                    for b in range(nb):
                        op = nc.vector.tensor_tensor(G[:, b, s * HALF:s * HALF + n], sa[:, s % 2, b, 0:n], B[2 * (s % 2) + b][:, n:2 * n], ALU.mult)
                    op.then_inc(gated, 1)
                    if s == 2:
                        nc.vector.tensor_copy(now.unsqueeze(2), table[:, :, bass.ds(it + 1, 1), :]).then_inc(now_ok, 1)
                        dve.wait_ge(now_ok, it + 2)
                        one_hots()
                for k in range(KD):
                    dve.wait_ge(scattered, it * KD + k + 1)
                    nc.vector.scalar_tensor_tensor(out=m.X[:, k, CTX:TOK], in0=B[k % 4][:, :], scalar=m.MOD[:, 1, 5, k, 0:1],
                                                   in1=m.X[:, k, CTX:TOK], op0=ALU.mult, op1=ALU.add).then_inc(added, 1)

            rounds(dve, turn)


def store(m):
    nc = m.nc
    turned, even_out, odd_out, stored = semaphores(m, "store", "turned even_out odd_out stored")
    rows = cut(m, 0, 4 * D).rearrange("p (t d) -> p t d", t=4)
    with nc.Block() as block:

        @block.tensor
        def _(pe):
            for n in range(8):
                for k in range(4):
                    mm = nc.tensor.transpose(m.psum[n][:, k * P:(k + 1) * P],
                                             m.X[:, 4 * (n % 2) + k, CTX + (n // 2) * P:CTX + (n // 2 + 1) * P], const(m, C_IDENT))
                mm.then_inc(turned, 1)

        @block.vector
        def _(dve):
            for n in range(0, 8, 2):
                dve.wait_ge(turned, n + 1)
                nc.vector.tensor_copy(rows[:, n // 2, 0:BANK], m.psum[n][:, :]).then_inc(even_out, 1)

        @block.scalar
        def _(act):
            for n in range(1, 8, 2):
                act.wait_ge(turned, n + 1)
                nc.scalar.copy(rows[:, n // 2, BANK:D], m.psum[n][:, :]).then_inc(odd_out, 1)

        @block.sync
        def _(sp):
            for t in range(4):
                sp.wait_ge(even_out, t + 1)
                sp.wait_ge(odd_out, t + 1)
                sp.dma_start(m.out[0, t * P:(t + 1) * P, :], rows[:, t, :]).then_inc(stored, 16)
            sp.wait_ge(stored, 64)


class Steps:

    def __init__(self, sem, names):
        self.sem, self.names, self.next = sem, names, 0

    @property
    def credit(self):
        return len(self.names)

    def step(self, name):
        assert self.names[self.next] == name, (self.names[self.next], name)
        self.next += 1
        return 1

    def after(self, head, name):
        return head * len(self.names) + len(self.names) + self.names.index(name) + 1

    def before(self, head, name):
        return head * len(self.names) + self.names.index(name) + 1


LEVELS = 6
PROBLEMS = 12
RUNS = ((0, 4, 0, 0), (4, 8, 0, 1), (8, 10, 4, 0), (10, 12, 4, 1))


def scan_step(s, d):
    if s < 4:
        c = s if d == 0 else 3 - s
        return (8, 10)[d] + c // 2, c % 2
    c = s - 4 if d == 0 else 11 - s
    return (0, 4)[d] + c // 2, c % 2


def delta_net(m):
    nc, dram = m.nc, m.dram
    w_in, pre_pe, pre_act, pre_dve = semaphores(m, "gdn", "w_in pre_pe pre_act pre_dve")
    at = [0, SLOT]

    def area(cols):
        if at[0] + cols <= 19500:
            at[0] += cols
            return cut(m, at[0] - cols, cols)
        at[1] += cols
        assert at[1] <= SLOTS * SLOT
        return m.ring[:, at[1] - cols:at[1]]

    def tiles(n):
        return area(n * P).rearrange("p (n t) -> p n t", n=n)

    m.O = area(KD * LAT).rearrange("p (k t) -> p k t", k=KD)
    m.O_first = CTX
    uq, uk, uv = area(LAT), area(TOK), area(TOK)
    gate = area(LAT)
    sq = area(LAT + TOK)
    rs = area(LAT + TOK)
    K, V = tiles(6), tiles(6)
    vb, kb, kd = tiles(PROBLEMS), tiles(PROBLEMS), tiles(PROBLEMS)
    DM, EG = tiles(PROBLEMS), tiles(PROBLEMS)
    QE = tiles(8)
    A, T, U, AM, Y = (tiles(PROBLEMS) for _ in range(5))
    AT = tiles(8)
    state = tiles(2)
    cu, wt = A, AM
    coef = area(5 * GH * PROBLEMS).rearrange("p (c h n) -> p c h n", c=5, h=GH)
    hc = area(5 * PROBLEMS).rearrange("p (c n) -> p c n", c=5)
    cw = area(9).rearrange("p (g w) -> p g w", g=3)
    z = area(6 * 32).rearrange("p (t n) -> p t n", t=6)
    z2, z3 = (area(6 * 16).rearrange("p (t n) -> p t n", t=6) for _ in range(2))
    ea = area(16)
    G_, GC, BETA, BEG, EKD = range(5)
    ident = const(m, C_IDENT)
    small = m.small
    B = m.psum
    wq = dram["gdn_w_qkv"].rearrange("(k p) (s n) -> p s k n", p=P, s=3)
    wg = dram["gdn_w_gate"].rearrange("(k p) n -> p k n", p=P)
    W = slot(m, 0).rearrange("p (s k n) -> p s k n", s=4, k=KD)
    conv_w = small[:, S_CONV:S_CONV + 72].rearrange("p (g h w) -> p g h w", g=3, h=GH)
    cum = (const(m, C_CUMF), const(m, C_CUMB))
    lev = (C_LEVF, C_LEVB)

    def bank(b, n=4):
        return B[b][:, 0:n * P].rearrange("p (n t) -> p n t", n=n)

    def rows(c, n0, n1):
        return hc[:, c, n0:n1].unsqueeze(2).broadcast_to([P, n1 - n0, P])

    def same(mask, n):
        return mask.unsqueeze(1).broadcast_to([P, n, P])

    CONV = (("q", uq[:, 0:LAT], 0, 0, LAT, 0), ("k", uk[:, 0:LAT], 1, 0, LAT, 1), ("v", uv[:, 0:LAT], 2, 0, LAT, 2),
            ("kc", uk[:, LAT:TOK], 3, 0, CTX, 1), ("vc", uv[:, LAT:TOK], 3, CTX, CTX, 2))
    GROUPS = range(3)
    lv = [f"{l}.{x}" for l in range(1, LEVELS) for x in GROUPS]
    sd = [f"{s}.{d}" for s in range(12) for d in range(2)]
    pe_names = (["rows0", "rows1", "rows2", "q", "k", "v", "kvc", "gate", "v_turned", "ss_q", "ss_k", "ss_kc", "vc_turned", "k_turned", "kc_turned",
                 "kk", "kkc", "qk"] + [f"a_turned{x}" for x in GROUPS] + [f"t_turned{x}" for x in GROUPS])
    for l in range(1, LEVELS):
        pe_names += [f"y{l}.{x}" for x in GROUPS]
        pe_names += sum([([f"t{l}.{x}"] if l < LEVELS - 1 else []) + [f"u{l}.{x}"] for x in GROUPS], [])
    pe_names += [f"cu{x}" for x in GROUPS] + [f"wt{x}" for x in GROUPS]
    for s in range(12):
        pe_names += [f"ws{s}.{d}" for d in range(2)]
        if s < 11:
            pe_names += [f"kv{s}.{d}" for d in range(2)]
        if s >= 4:
            pe_names += [f"o{s}.{d}" for d in range(2)]
    pe_names += ["ss_o"]
    act_names = ([f"eg{x}" for x in GROUPS] + [f"tap_{c[0]}" for c in CONV] + ["gate"] + [f"dm{x}" for x in GROUPS]
                 + [f"silu_{c[0]}" for c in CONV] + ["sq_q", "sq_k", "sq_kc", "V", "root_q", "root_k", "root_kc", "Vc", "K", "Kc"]
                 + [f"U{x}" for x in GROUPS] + [f"Y{v_}" for v_ in lv] + [f"wt{x}" for x in GROUPS] + ["o_f", "sq_o", "root_o"])
    dve_names = (["head_coef", "head_conv"] + [f"dm{n}" for n in range(PROBLEMS)]
                 + sum([[f"left_{c[0]}", f"right_{c[0]}"] for c in CONV], [])
                 + ["inv_q", "q", "inv_k", "k"] + [f"vb{r}" for r in range(4)] + ["at0", "at1"] + [f"ad{r}" for r in range(4)]
                 + [f"a{x}" for x in GROUPS] + [f"T0.{x}" for x in GROUPS])
    for l in range(1, LEVELS):
        dve_names += sum([([f"T{l}.{x}"] if l < LEVELS - 1 else []) + [f"U{l}.{x}"] for x in GROUPS], [])
    dve_names += [f"cu{x}" for x in GROUPS]
    for s in range(12):
        dve_names += [f"vn{s}.{d}" for d in range(2)] + ([f"st{s}.{d}" for d in range(2)] if s < 11 else [])
    dve_names += ["o", "inv_o", "normed", "out"]
    pool_names = ([f"mask{r}" for r in range(4)] + ["zero", "qe0", "qe1"] + [f"kb{r}" for r in range(4)] + [f"kd{r}" for r in range(4)]
                  + [f"am0.{r}" for r in range(4)] + sum([[f"am{l}.{r}" for r in range(4)] for l in range(1, LEVELS)], []))
    pe_step, act_step, dve_step, pool_step = semaphores(m, "gdn", "pe_step act_step dve_step pool_step")
    TE, SC, VE, GP = Steps(pe_step, pe_names), Steps(act_step, act_names), Steps(dve_step, dve_names), Steps(pool_step, pool_names)
    run_of = {0: (0,), 1: (1,), 2: (2, 3)}

    with nc.Block() as block:

        @block.sync
        def _(sp):
            with sp.Fori(0, GH) as h:
                sp.wait_ge(pe_step, TE.before(h, "gate"))
                for s in range(3):
                    sp.dma_start(W[:, s], wq[:, s, :, bass.ds(h * P, P)]).then_inc(w_in, 16)
                sp.dma_start(W[:, 3], wg[:, :, bass.ds(h * P, P)]).then_inc(w_in, 16)

        @block.tensor
        def _(pe):
            pe.sem_inc(pe_step, TE.credit)
            for t in range(6):
                t0 = CTX + t * P if t < 4 else (t - 4) * P
                for k in range(KD):
                    mm = nc.tensor.matmul(B[0][:, 32 * t:32 * t + 32], m.H[:, k, t0:t0 + P], small[:, S_WBD + 32 * k:S_WBD + 32 * k + 32],
                                          start=(k == 0), stop=(k == KD - 1))
            mm.then_inc(pre_pe, 1)
            pe.wait_ge(pre_dve, 15)
            gc = B[1][:, 0:GH * PROBLEMS].rearrange("p (h n) -> p h n", h=GH)
            for n0, n1, _, d in RUNS:
                nc.tensor.matmul(gc[:, :, n0:n1], cum[d], coef[:, G_, :, n0:n1], start=True, stop=True)
            nc.tensor.matmul(B[2][:, 0:GH * PROBLEMS].rearrange("p (h n) -> p h n", h=GH), const(m, C_BLK), coef[:, G_], start=True,
                             stop=True).then_inc(pre_pe, 1)

            def project(b, c0, s, t0, t1):
                for k in range(KD):
                    mm = nc.tensor.matmul(B[b][:, c0:c0 + t1 - t0], W[:, s, k, :], m.H[:, k, t0:t1], start=(k == 0), stop=(k == KD - 1))
                return mm

            with pe.Fori(0, GH) as h:
                pe.wait_ge(dve_step, VE.after(h, "head_coef"))
                for x in GROUPS:
                    for n in range(4 * x, 4 * x + 4):
                        d = [r[3] for r in RUNS if r[0] <= n < r[1]][0]
                        mm = nc.tensor.matmul(B[5 + x][:, (n % 4) * P:(n % 4 + 1) * P], hc[:, G_, n:n + 1].to_broadcast([P, P]), cum[d],
                                              start=True, stop=True)
                    mm.then_inc(pe_step, TE.step(f"rows{x}"))
                pe.wait_ge(w_in, h * 64 + 64)
                project(0, 0, 0, CTX, TOK).then_inc(pe_step, TE.step("q"))
                project(1, 0, 1, CTX, TOK).then_inc(pe_step, TE.step("k"))
                project(2, 0, 2, CTX, TOK).then_inc(pe_step, TE.step("v"))
                project(3, 0, 1, 0, CTX)
                project(3, CTX, 2, 0, CTX).then_inc(pe_step, TE.step("kvc"))
                project(4, 0, 3, CTX, TOK).then_inc(pe_step, TE.step("gate"))
                pe.wait_ge(act_step, SC.after(h, "silu_v"))
                for t in range(4):
                    mm = nc.tensor.transpose(B[0][:, t * P:(t + 1) * P], uv[:, t * P:(t + 1) * P], ident)
                mm.then_inc(pe_step, TE.step("v_turned"))
                pe.wait_ge(dve_step, VE.after(h, "dm11"))
                pe.wait_ge(act_step, SC.after(h, "sq_q"))
                nc.tensor.matmul(B[5][:, :], const(m, C_ONES), sq[:, 0:LAT], start=True, stop=True).then_inc(pe_step, TE.step("ss_q"))
                pe.wait_ge(act_step, SC.after(h, "sq_k"))
                nc.tensor.matmul(B[6][:, :], const(m, C_ONES), sq[:, LAT:2 * LAT], start=True, stop=True).then_inc(pe_step, TE.step("ss_k"))
                pe.wait_ge(act_step, SC.after(h, "sq_kc"))
                nc.tensor.matmul(B[7][:, 0:CTX], const(m, C_ONES), sq[:, 2 * LAT:2 * LAT + CTX], start=True,
                                 stop=True).then_inc(pe_step, TE.step("ss_kc"))
                for t in range(2):
                    mm = nc.tensor.transpose(B[2][:, (2 + t) * P:(3 + t) * P], uv[:, LAT + t * P:LAT + (t + 1) * P], ident)
                mm.then_inc(pe_step, TE.step("vc_turned"))
                pe.wait_ge(dve_step, VE.after(h, "k"))
                for t in range(4):
                    mm = nc.tensor.transpose(B[1][:, t * P:(t + 1) * P], uk[:, t * P:(t + 1) * P], ident)
                mm.then_inc(pe_step, TE.step("k_turned"))
                pe.wait_ge(act_step, SC.after(h, "Vc"))
                for t in range(2):
                    mm = nc.tensor.transpose(B[2][:, t * P:(t + 1) * P], uk[:, LAT + t * P:LAT + (t + 1) * P], ident)
                mm.then_inc(pe_step, TE.step("kc_turned"))
                for t in range(6):
                    kt = uk[:, t * P:(t + 1) * P]
                    mm = nc.tensor.matmul(B[3 + t // 4][:, (t % 4) * P:(t % 4 + 1) * P], kt, kt, start=True, stop=True)
                    if t in (3, 5):
                        mm.then_inc(pe_step, TE.step("kk" if t == 3 else "kkc"))
                for t in range(4):
                    mm = nc.tensor.matmul(B[5][:, t * P:(t + 1) * P], uk[:, t * P:(t + 1) * P], uq[:, t * P:(t + 1) * P], start=True, stop=True)
                mm.then_inc(pe_step, TE.step("qk"))
                for x in GROUPS:
                    pe.wait_ge(dve_step, VE.after(h, ("ad0", "ad1", "ad3")[x]))
                    if x == 0:
                        pe.wait_ge(act_step, SC.after(h, "Kc"))
                    for n in range(4):
                        mm = nc.tensor.transpose(bank(x)[:, n, :], DM[:, 4 * x + n, :], ident)
                    mm.then_inc(pe_step, TE.step(f"a_turned{x}"))
                for x in GROUPS:
                    pe.wait_ge(dve_step, VE.after(h, f"T0.{x}"))
                    for n in range(4):
                        mm = nc.tensor.transpose(bank(3 + x)[:, n, :], T[:, 4 * x + n, :], ident)
                    mm.then_inc(pe_step, TE.step(f"t_turned{x}"))
                for l in range(1, LEVELS):
                    for x in GROUPS:
                        pe.wait_ge(pool_step, GP.after(h, f"am{l}.{run_of[x][-1]}"))
                        if l == 1:
                            pe.wait_ge(act_step, SC.after(h, f"U{x}"))
                        else:
                            pe.wait_ge(dve_step, VE.after(h, f"U{l - 1}.{x}"))
                        for n in range(4):
                            mm = nc.tensor.matmul(bank(x)[:, n, :], AM[:, 4 * x + n, :], U[:, 4 * x + n, :], start=True, stop=True)
                        mm.then_inc(pe_step, TE.step(f"y{l}.{x}"))
                    for x in GROUPS:
                        pe.wait_ge(act_step, SC.after(h, f"Y{l}.{x}"))
                        if l < LEVELS - 1:
                            for n in range(4):
                                mm = nc.tensor.matmul(bank(3 + x)[:, n, :], Y[:, 4 * x + n, :], T[:, 4 * x + n, :], start=True, stop=True)
                            mm.then_inc(pe_step, TE.step(f"t{l}.{x}"))
                        for n in range(4):
                            mm = nc.tensor.matmul(bank(x)[:, n, :], T[:, 4 * x + n, :], Y[:, 4 * x + n, :], start=True, stop=True)
                        mm.then_inc(pe_step, TE.step(f"u{l}.{x}"))
                for x in GROUPS:
                    pe.wait_ge(dve_step, VE.after(h, f"U{LEVELS - 1}.{x}"))
                    for n in range(4):
                        mm = nc.tensor.matmul(bank(3 + x)[:, n, :], U[:, 4 * x + n, :], vb[:, 4 * x + n, :], start=True, stop=True)
                    mm.then_inc(pe_step, TE.step(f"cu{x}"))
                for x in GROUPS:
                    pe.wait_ge(pool_step, GP.after(h, "kb3"))
                    for n in range(4):
                        mm = nc.tensor.matmul(bank(x)[:, n, :], kb[:, 4 * x + n, :], U[:, 4 * x + n, :], start=True, stop=True)
                    mm.then_inc(pe_step, TE.step(f"wt{x}"))
                pe.wait_ge(act_step, SC.after(h, "wt2"))
                pe.wait_ge(dve_step, VE.after(h, "cu2"))
                pe.wait_ge(pool_step, GP.after(h, "kd3"))
                for s in range(12):
                    for d in range(2):
                        n, half = scan_step(s, d)
                        c = slice(64 * half, 64 * half + 64)
                        if s:
                            pe.wait_ge(dve_step, VE.after(h, f"st{s - 1}.{d}"))
                        nc.tensor.matmul(B[6 + d][c, 0:P], wt[:, n, c], state[:, d, :], start=True, stop=True)\
                            .then_inc(pe_step, TE.step(f"ws{s}.{d}"))
                        if s >= 4:
                            o0 = (n % 4) * P + 64 * half
                            nc.tensor.matmul(B[2 + d][:, o0:o0 + 64], state[:, d, :], QE[:, n, c], start=True, stop=False)
                    for d in range(2):
                        n, half = scan_step(s, d)
                        c = slice(64 * half, 64 * half + 64)
                        pe.wait_ge(dve_step, VE.after(h, f"vn{s}.{d}"))
                        if s < 11:
                            nc.tensor.matmul(B[d][:, 0:P], kd[c, n, :], cu[c, n, :], start=True, stop=True)\
                                .then_inc(pe_step, TE.step(f"kv{s}.{d}"))
                    if s >= 4:
                        for d in range(2):
                            n, half = scan_step(s, d)
                            c = slice(64 * half, 64 * half + 64)
                            o0 = (n % 4) * P + 64 * half
                            nc.tensor.matmul(B[2 + d][:, o0:o0 + 64], cu[c, n, :], AT[c, n, c], start=False, stop=True)\
                                .then_inc(pe_step, TE.step(f"o{s}.{d}"))
                pe.wait_ge(act_step, SC.after(h, "sq_o"))
                nc.tensor.matmul(B[4][:, :], const(m, C_ONES), sq[:, 0:LAT], start=True, stop=True).then_inc(pe_step, TE.step("ss_o"))

        @block.scalar
        def _(act):
            act.sem_inc(act_step, SC.credit)
            act.wait_ge(pre_dve, 1)
            nc.scalar.activation(z[:, :, 0:16], z[:, :, 0:16], ACT.Sigmoid).then_inc(pre_act, 1)
            nc.scalar.activation(ea, small[:, S_ALOG:S_ALOG + 16], ACT.Exp).then_inc(pre_act, 1)
            act.wait_ge(pre_dve, 4)
            nc.scalar.activation(z3, z3, ACT.Exp).then_inc(pre_act, 1)
            act.wait_ge(pre_act, 3)
            nc.scalar.activation(z3, z3, ACT.Ln, bias=const(m, C_EPS + 2, 1)).then_inc(pre_act, 1)
            act.wait_ge(pre_dve, 17)
            nc.scalar.activation(coef[:, BEG], coef[:, GC], ACT.Exp).then_inc(pre_act, 1)
            nc.scalar.activation(coef[:, EKD], coef[:, EKD], ACT.Exp).then_inc(pre_act, 1)
            with act.Fori(0, GH) as h:
                act.wait_ge(dve_step, VE.before(h, "out"))
                for x in GROUPS:
                    act.wait_ge(pe_step, TE.after(h, f"rows{x}"))
                    nc.scalar.activation(EG[:, 4 * x:4 * x + 4, :], bank(5 + x), ACT.Exp).then_inc(act_step, SC.step(f"eg{x}"))
                for name, dst, b, c0, n, g in CONV:
                    act.wait_ge(pe_step, TE.after(h, {"q": "q", "k": "k", "v": "v"}.get(name, "kvc")))
                    act.wait_ge(dve_step, VE.after(h, "head_conv"))
                    nc.scalar.activation(dst, B[b][:, c0:c0 + n], ACT.Identity, scale=cw[:, g, 1:2]).then_inc(act_step, SC.step(f"tap_{name}"))
                act.wait_ge(pe_step, TE.after(h, "gate"))
                nc.scalar.activation(gate, B[4][:, :], ACT.Silu).then_inc(act_step, SC.step("gate"))
                for x in GROUPS:
                    act.wait_ge(dve_step, VE.after(h, f"dm{4 * x + 3}"))
                    nc.scalar.activation(DM[:, 4 * x:4 * x + 4, :], DM[:, 4 * x:4 * x + 4, :], ACT.Exp).then_inc(act_step, SC.step(f"dm{x}"))
                for name, dst, b, c0, n, g in CONV:
                    act.wait_ge(dve_step, VE.after(h, f"right_{name}"))
                    nc.scalar.activation(dst, dst, ACT.Silu).then_inc(act_step, SC.step(f"silu_{name}"))
                act.wait_ge(act_step, SC.after(h, "silu_kc"))
                nc.scalar.activation(sq[:, 0:LAT], uq, ACT.Square).then_inc(act_step, SC.step("sq_q"))
                nc.scalar.activation(sq[:, LAT:2 * LAT], uk[:, 0:LAT], ACT.Square).then_inc(act_step, SC.step("sq_k"))
                nc.scalar.activation(sq[:, 2 * LAT:2 * LAT + CTX], uk[:, LAT:TOK], ACT.Square).then_inc(act_step, SC.step("sq_kc"))
                act.wait_ge(pe_step, TE.after(h, "v_turned"))
                nc.scalar.copy(V[:, 0:4, :], bank(0)).then_inc(act_step, SC.step("V"))
                act.wait_ge(pe_step, TE.after(h, "ss_q"))
                nc.scalar.activation(rs[:, 0:LAT], B[5][:, :], ACT.Sqrt, bias=const(m, C_EPS + 3, 1), scale=float(GD))\
                    .then_inc(act_step, SC.step("root_q"))
                act.wait_ge(pe_step, TE.after(h, "ss_k"))
                nc.scalar.activation(rs[:, LAT:2 * LAT], B[6][:, :], ACT.Sqrt, bias=const(m, C_EPS, 1)).then_inc(act_step, SC.step("root_k"))
                act.wait_ge(pe_step, TE.after(h, "ss_kc"))
                nc.scalar.activation(rs[:, 2 * LAT:2 * LAT + CTX], B[7][:, 0:CTX], ACT.Sqrt, bias=const(m, C_EPS, 1))\
                    .then_inc(act_step, SC.step("root_kc"))
                act.wait_ge(pe_step, TE.after(h, "vc_turned"))
                nc.scalar.copy(V[:, 4:6, :], bank(2)[:, 2:4, :]).then_inc(act_step, SC.step("Vc"))
                act.wait_ge(pe_step, TE.after(h, "k_turned"))
                nc.scalar.copy(K[:, 0:4, :], bank(1)).then_inc(act_step, SC.step("K"))
                act.wait_ge(pe_step, TE.after(h, "kc_turned"))
                nc.scalar.copy(K[:, 4:6, :], bank(2)[:, 0:2, :]).then_inc(act_step, SC.step("Kc"))
                for x in GROUPS:
                    act.wait_ge(pe_step, TE.after(h, f"t_turned{x}"))
                    nc.scalar.copy(U[:, 4 * x:4 * x + 4, :], bank(3 + x)).then_inc(act_step, SC.step(f"U{x}"))
                for l in range(1, LEVELS):
                    for x in GROUPS:
                        act.wait_ge(pe_step, TE.after(h, f"y{l}.{x}"))
                        nc.scalar.copy(Y[:, 4 * x:4 * x + 4, :], bank(x)).then_inc(act_step, SC.step(f"Y{l}.{x}"))
                for x in GROUPS:
                    act.wait_ge(pe_step, TE.after(h, f"wt{x}"))
                    nc.scalar.copy(wt[:, 4 * x:4 * x + 4, :], bank(x)).then_inc(act_step, SC.step(f"wt{x}"))
                act.wait_ge(pe_step, TE.after(h, "o11.1"))
                nc.scalar.copy(rs[:, 0:LAT], B[2][:, :]).then_inc(act_step, SC.step("o_f"))
                act.wait_ge(dve_step, VE.after(h, "o"))
                nc.scalar.activation(sq[:, 0:LAT], uq, ACT.Square).then_inc(act_step, SC.step("sq_o"))
                act.wait_ge(pe_step, TE.after(h, "ss_o"))
                nc.scalar.activation(rs[:, LAT:2 * LAT], B[4][:, :], ACT.Sqrt, bias=const(m, C_EPS, 1), scale=1.0 / GD)\
                    .then_inc(act_step, SC.step("root_o"))

        @block.gpsimd
        def _(pool):
            pool.sem_inc(pool_step, GP.credit)
            with pool.Fori(0, GH) as h:
                pool.wait_ge(dve_step, VE.before(h, "out"))
                for r, (n0, n1, _, d) in enumerate(RUNS):
                    pool.wait_ge(act_step, SC.after(h, f"dm{(n1 - 1) // 4}"))
                    nc.gpsimd.tensor_tensor(DM[:, n0:n1, :], DM[:, n0:n1, :], same(cum[d], n1 - n0), ALU.mult)\
                        .then_inc(pool_step, GP.step(f"mask{r}"))
                nc.gpsimd.memset(state, 0.0).then_inc(pool_step, GP.step("zero"))
                pool.wait_ge(dve_step, VE.after(h, "q"))
                for d in range(2):
                    nc.gpsimd.tensor_tensor(QE[:, 4 * d:4 * d + 4, :], uq.rearrange("p (n t) -> p n t", n=4), EG[:, 4 * d:4 * d + 4, :], ALU.mult)\
                        .then_inc(pool_step, GP.step(f"qe{d}"))
                pool.wait_ge(act_step, SC.after(h, "Kc"))
                for dst, c, name in ((kb, BEG, "kb"), (kd, EKD, "kd")):
                    for r, (n0, n1, t0, d) in enumerate(RUNS):
                        nc.gpsimd.tensor_tensor(dst[:, n0:n1, :], K[:, t0:t0 + n1 - n0, :], rows(c, n0, n1), ALU.mult)\
                            .then_inc(pool_step, GP.step(f"{name}{r}"))
                for l in range(LEVELS):
                    for r, (n0, n1, _, d) in enumerate(RUNS):
                        x = min(r, 2)
                        if l == 0:
                            pool.wait_ge(dve_step, VE.after(h, f"a{x}"))
                        elif l == 1:
                            pool.wait_ge(dve_step, VE.after(h, f"T0.{x}"))
                        else:
                            pool.wait_ge(pe_step, TE.after(h, f"y{l - 1}.{x}"))
                        nc.gpsimd.tensor_tensor(AM[:, n0:n1, :], A[:, n0:n1, :], same(const(m, lev[d] + l * P), n1 - n0), ALU.mult)\
                            .then_inc(pool_step, GP.step(f"am{l}.{r}"))

        @block.vector
        def _(dve):
            dve.sem_inc(dve_step, VE.credit)
            dve.wait_ge(pre_pe, 1)
            nc.vector.tensor_copy(z, B[0][:, 0:192].rearrange("p (t n) -> p t n", t=6)).then_inc(pre_dve, 1)
            dve.wait_ge(pre_dve, 1)
            dtb = small[:, S_DTB:S_DTB + 16].unsqueeze(1).broadcast_to([P, 6, 16])
            nc.vector.tensor_tensor(z2, z[:, :, 16:32], dtb, ALU.add).then_inc(pre_dve, 1)
            dve.wait_ge(pre_dve, 2)
            nc.vector.tensor_scalar(z3, z2, -1.0, None, ALU.mult).then_inc(pre_dve, 1)
            dve.wait_ge(pre_dve, 3)
            nc.vector.tensor_tensor(z3, z3, z2, ALU.min).then_inc(pre_dve, 1)
            dve.wait_ge(pre_dve, 4)
            nc.vector.tensor_scalar(z2, z2, 0.0, None, ALU.max).then_inc(pre_dve, 1)
            dve.wait_ge(pre_dve, 5)
            dve.wait_ge(pre_act, 4)
            nc.vector.tensor_tensor(z2, z2, z3, ALU.add).then_inc(pre_dve, 1)
            dve.wait_ge(pre_dve, 6)
            nc.vector.tensor_tensor(z2, z2, ea.unsqueeze(1).broadcast_to([P, 6, 16]), ALU.mult).then_inc(pre_dve, 1)
            dve.wait_ge(pre_dve, 7)
            for n0, n1, t0, d in RUNS:
                for c, src, f in ((G_, z2, -1.0), (BETA, z, 1.0)):
                    nc.vector.tensor_scalar(coef[:, c, :, n0:n1], src[:, t0:t0 + n1 - n0, GH * d:GH * d + GH].rearrange("p t h -> p h t"),
                                            f, None, ALU.mult).then_inc(pre_dve, 1)
            dve.wait_ge(pre_pe, 2)
            nc.vector.tensor_copy(coef[:, GC], B[1][:, 0:GH * PROBLEMS].rearrange("p (h n) -> p h n", h=GH)).then_inc(pre_dve, 1)
            dve.wait_ge(pre_dve, 16)
            nc.vector.tensor_tensor(coef[:, EKD], B[2][:, 0:GH * PROBLEMS].rearrange("p (h n) -> p h n", h=GH), coef[:, GC],
                                    ALU.subtract).then_inc(pre_dve, 1)
            dve.wait_ge(pre_act, 6)
            nc.vector.tensor_tensor(coef[:, BEG], coef[:, BEG], coef[:, BETA], ALU.mult).then_inc(pre_dve, 1)
            dve.wait_ge(pre_dve, 18)
            with dve.Fori(0, GH) as h:
                dve.wait_ge(pe_step, TE.before(h, "ss_o"))
                dve.wait_ge(dve_step, VE.before(h, "out"))
                nc.vector.tensor_copy(hc.unsqueeze(2), coef[:, :, bass.ds(h, 1), :]).then_inc(dve_step, VE.step("head_coef"))
                nc.vector.tensor_copy(cw.unsqueeze(2), conv_w[:, :, bass.ds(h, 1), :]).then_inc(dve_step, VE.step("head_conv"))
                dve.wait_ge(dve_step, VE.after(h, "head_conv"))
                for n in range(PROBLEMS):
                    if n % 4 == 0:
                        dve.wait_ge(act_step, SC.after(h, f"eg{n // 4}"))
                    nc.vector.tensor_scalar(DM[:, n, :], bank(5 + n // 4)[:, n % 4, :], hc[:, GC, n:n + 1], 0.0, ALU.subtract, ALU.min)\
                        .then_inc(dve_step, VE.step(f"dm{n}"))
                for name, dst, b, c0, n, g in CONV:
                    dve.wait_ge(act_step, SC.after(h, "tap_vc" if b == 3 else f"tap_{name}"))
                    nc.vector.scalar_tensor_tensor(out=dst[:, 1:n], in0=B[b][:, c0:c0 + n - 1], scalar=cw[:, g, 0:1], in1=dst[:, 1:n],
                                                   op0=ALU.mult, op1=ALU.add).then_inc(dve_step, VE.step(f"left_{name}"))
                    dve.wait_ge(dve_step, VE.after(h, f"left_{name}"))
                    nc.vector.scalar_tensor_tensor(out=dst[:, 0:n - 1], in0=B[b][:, c0 + 1:c0 + n], scalar=cw[:, g, 2:3], in1=dst[:, 0:n - 1],
                                                   op0=ALU.mult, op1=ALU.add).then_inc(dve_step, VE.step(f"right_{name}"))
                dve.wait_ge(act_step, SC.after(h, "root_q"))
                nc.vector.reciprocal(rs[:, 0:LAT], rs[:, 0:LAT]).then_inc(dve_step, VE.step("inv_q"))
                dve.wait_ge(dve_step, VE.after(h, "inv_q"))
                nc.vector.tensor_tensor(uq, uq, rs[:, 0:LAT], ALU.mult).then_inc(dve_step, VE.step("q"))
                dve.wait_ge(act_step, SC.after(h, "root_kc"))
                nc.vector.reciprocal(rs[:, LAT:LAT + TOK], rs[:, LAT:LAT + TOK]).then_inc(dve_step, VE.step("inv_k"))
                dve.wait_ge(dve_step, VE.after(h, "inv_k"))
                nc.vector.tensor_tensor(uk, uk, rs[:, LAT:LAT + TOK], ALU.mult).then_inc(dve_step, VE.step("k"))
                for r, (n0, n1, t0, d) in enumerate(RUNS):
                    dve.wait_ge(act_step, SC.after(h, "Vc"))
                    nc.vector.tensor_tensor(vb[:, n0:n1, :], V[:, t0:t0 + n1 - n0, :], rows(BETA, n0, n1), ALU.mult)\
                        .then_inc(dve_step, VE.step(f"vb{r}"))
                for d in range(2):
                    dve.wait_ge(pe_step, TE.after(h, "qk"))
                    dve.wait_ge(pool_step, GP.after(h, "mask1"))
                    nc.vector.tensor_tensor(AT[:, 4 * d:4 * d + 4, :], bank(5), DM[:, 4 * d:4 * d + 4, :], ALU.mult)\
                        .then_inc(dve_step, VE.step(f"at{d}"))
                dve.wait_ge(pool_step, GP.after(h, "mask3"))
                dve.wait_ge(dve_step, VE.after(h, "at1"))
                for r, (n0, n1, t0, d) in enumerate(RUNS):
                    nc.vector.tensor_tensor(DM[:, n0:n1, :], bank(3 + (r > 1), n1 - n0), DM[:, n0:n1, :], ALU.mult)\
                        .then_inc(dve_step, VE.step(f"ad{r}"))
                for x in GROUPS:
                    dve.wait_ge(pe_step, TE.after(h, f"a_turned{x}"))
                    nc.vector.tensor_tensor(A[:, 4 * x:4 * x + 4, :], bank(x), rows(BETA, 4 * x, 4 * x + 4), ALU.mult)\
                        .then_inc(dve_step, VE.step(f"a{x}"))
                for x in GROUPS:
                    dve.wait_ge(pool_step, GP.after(h, f"am0.{run_of[x][-1]}"))
                    nc.vector.tensor_tensor(T[:, 4 * x:4 * x + 4, :], same(ident, 4), AM[:, 4 * x:4 * x + 4, :], ALU.subtract)\
                        .then_inc(dve_step, VE.step(f"T0.{x}"))
                for l in range(1, LEVELS):
                    for x in GROUPS:
                        g4 = slice(4 * x, 4 * x + 4)
                        dve.wait_ge(pe_step, TE.after(h, f"u{l}.{x}"))
                        if l < LEVELS - 1:
                            nc.vector.tensor_tensor(T[:, g4, :], T[:, g4, :], bank(3 + x), ALU.subtract).then_inc(dve_step, VE.step(f"T{l}.{x}"))
                        nc.vector.tensor_tensor(U[:, g4, :], U[:, g4, :], bank(x), ALU.subtract).then_inc(dve_step, VE.step(f"U{l}.{x}"))
                for x in GROUPS:
                    dve.wait_ge(pe_step, TE.after(h, f"cu{x}"))
                    nc.vector.tensor_copy(cu[:, 4 * x:4 * x + 4, :], bank(3 + x)).then_inc(dve_step, VE.step(f"cu{x}"))
                for s in range(12):
                    for d in range(2):
                        n, half = scan_step(s, d)
                        c = slice(64 * half, 64 * half + 64)
                        dve.wait_ge(pe_step, TE.after(h, f"ws{s}.{d}"))
                        if s == 0:
                            dve.wait_ge(dve_step, VE.after(h, "cu2"))
                        nc.vector.tensor_tensor(cu[c, n, :], cu[c, n, :], B[6 + d][c, 0:P], ALU.subtract).then_inc(dve_step, VE.step(f"vn{s}.{d}"))
                    if s < 11:
                        for d in range(2):
                            n, half = scan_step(s, d)
                            last = 64 * half + (63 if d == 0 else 0)
                            dve.wait_ge(pe_step, TE.after(h, f"kv{s}.{d}"))
                            nc.vector.scalar_tensor_tensor(out=state[:, d, :], in0=state[:, d, :], scalar=EG[:, n, last:last + 1], in1=B[d][:, 0:P],
                                                           op0=ALU.mult, op1=ALU.add).then_inc(dve_step, VE.step(f"st{s}.{d}"))
                dve.wait_ge(act_step, SC.after(h, "o_f"))
                nc.vector.tensor_tensor(uq, rs[:, 0:LAT], B[3][:, :], ALU.add).then_inc(dve_step, VE.step("o"))
                dve.wait_ge(act_step, SC.after(h, "root_o"))
                nc.vector.reciprocal(rs[:, LAT:2 * LAT], rs[:, LAT:2 * LAT]).then_inc(dve_step, VE.step("inv_o"))
                dve.wait_ge(dve_step, VE.after(h, "inv_o"))
                nc.vector.scalar_tensor_tensor(out=uq, in0=uq, scalar=small[:, S_ON:S_ON + 1], in1=rs[:, LAT:2 * LAT], op0=ALU.mult,
                                               op1=ALU.mult).then_inc(dve_step, VE.step("normed"))
                dve.wait_ge(dve_step, VE.after(h, "normed"))
                nc.vector.tensor_tensor(m.O[:, bass.ds(h, 1), :], uq.unsqueeze(1), gate.unsqueeze(1), ALU.mult)\
                    .then_inc(dve_step, VE.step("out"))
    for engine in (TE, SC, VE, GP):
        assert engine.next == len(engine.names), engine.names[engine.next]


def build(nc, dram, out):
    with ExitStack() as ctx:
        m = open_memory(nc, ctx, dram)
        m.out = out
        load_and_modulation(m)
        norm_modulate(m, "n0", 0, 0)
        neighbourhood_attention(m)
        project_to_residual(m, "no", dram["na_w_o"], 0, 0)
        norm_modulate(m, "n1", 0, 1)
        swiglu(m)
        reorder(m)
        norm_modulate(m, "n2", 1, 0)
        delta_net(m)
        project_to_residual(m, "go", dram["gdn_w_o"], 1, CTX)
        norm_modulate(m, "n3", 1, 1, first=CTX)
        experts(m)
        store(m)


_INS = ["x", "ctx", "ada_w", "na_w_qkv", "na_w_o", "gdn_w_qkv", "gdn_w_gate", "gdn_w_o", "ffn_w_in", "ffn_w_out",
        "moe_w_in", "moe_w_out"]


def kernel(**inputs):
    import concourse.bacc as bacc
    from concourse.bass_utils import run_bass_kernel_spmd

    nc = bacc.Bacc("TRN2", target_bir_lowering=False, num_devices=1)
    arrays = {n: np.ascontiguousarray(inputs[n]) for n in _INS}
    arrays["small"] = small_inputs(inputs)
    arrays["bias"] = bias_table(inputs["na_rpb"])
    arrays["const"] = constants()
    dram = {n: nc.dram_tensor(f"in_{n}", a.shape, mybir.dt.from_np(a.dtype), kind="ExternalInput").ap()
            for n, a in arrays.items()}
    out = nc.dram_tensor("out", (1, LAT, D), F32, kind="ExternalOutput").ap()
    build(nc, dram, out)
    r = run_bass_kernel_spmd(nc, [{f"in_{n}": a for n, a in arrays.items()}], core_ids=[0])
    return r.results[0]["out"]
```

```python
from contextlib import ExitStack

import numpy as np

import concourse.bass as bass
from concourse import mybir

F32 = mybir.dt.float32
U32 = mybir.dt.uint32
ALU = mybir.AluOpType
ACT = mybir.ActivationFunctionType
AX = mybir.AxisListType

P = 128
D = 1024
KD = D // P
CTX, LAT = 256, 512
TOK = CTX + LAT
GRID_R, GRID_C = 8, 64
BANK = 512
EPS = 1e-6
SLOT = 4096
SLOTS = 4

NA_HEADS, NA_HD = 16, 64
NA_PAIRS = NA_HEADS // 2
WIN_R, WIN_C = 8, 16
DR = 2 * WIN_R - 1
DC = 2 * WIN_C - 1
BIAS_DC = 2 * DC + 1
BIAS_RUN = 48 * DR
WIN = 256
WIN_START = (0, 64, 192, 256)
WIN_VARIANT = (0, 1, 1, 2)
WIN_SHIFT = (16, 8, 0)
MASKED = -1e30

FFN = 2816
EXPERTS = 8
EFF = 1408

GH, GD = 8, 128
CH = 64

C_IDENT = 0
C_MEAN = C_IDENT + P
C_HALF = C_MEAN + P
C_ONES = C_HALF + P
C_WMASK = C_ONES + P
C_CUMF = C_WMASK + 96
C_CUMB = C_CUMF + P
C_BLK = C_CUMB + P
C_BEFORE = C_BLK + P
C_LEVF = C_BEFORE + P
C_LEVB = C_LEVF + 6 * P
C_IOTA = C_LEVB + 6 * P
C_SLOT = C_IOTA + EXPERTS
C_EPS = C_SLOT + 2 * P
C_ALL = C_EPS + 4


def constants():
    c = np.zeros((P, C_ALL), np.float32)
    i = np.arange(P)
    row, col = i[:, None], i[None, :]
    same = row // CH == col // CH
    c[:, C_IDENT:C_IDENT + P] = row == col
    c[:, C_MEAN:C_MEAN + P] = 1.0 / D
    c[:, C_HALF:C_HALF + P] = (row // NA_HD == col // NA_HD) / NA_HD
    c[:, C_ONES:C_ONES + P] = 1.0
    for v, (block, start) in enumerate(((0, 0), (1, 8), (3, 32))):
        qcol = 16 * block + i // 8
        c0 = np.clip(qcol - WIN_C // 2, 0, GRID_C - WIN_C)[:, None]
        kcol = start + np.arange(32)[None, :]
        c[:, C_WMASK + 32 * v:C_WMASK + 32 * v + 32] = np.where((kcol >= c0) & (kcol < c0 + WIN_C), 0.0, MASKED)
    c[:, C_CUMF:C_CUMF + P] = same & (row <= col)
    c[:, C_CUMB:C_CUMB + P] = same & (row >= col)
    c[:, C_BLK:C_BLK + P] = same
    c[:, C_BEFORE:C_BEFORE + P] = row < col
    for n in range(6):
        s = 1 << n
        pair = (row // (2 * s) == col // (2 * s)) & (row // s != col // s)
        c[:, C_LEVF + n * P:C_LEVF + n * P + P] = pair & (row > col)
        c[:, C_LEVB + n * P:C_LEVB + n * P + P] = pair & (row < col)
    c[:, C_IOTA:C_IOTA + EXPERTS] = np.arange(EXPERTS)
    c[:, C_SLOT:C_SLOT + 2 * P] = np.arange(2 * P)
    c[:, C_EPS:C_EPS + 4] = (EPS, NA_HD * EPS, 1.0, GD * EPS)
    return c


S_C = 0
S_ADAB = S_C + 2 * KD
S_NORM = S_ADAB + 96
S_QN = S_NORM + 4 * KD
S_CONV = S_QN + 2
S_WBD = S_CONV + 72
S_ALOG = S_WBD + 32 * KD
S_DTB = S_ALOG + 2 * GH
S_ON = S_DTB + 2 * GH
S_RT = S_ON + 1
S_ALL = S_RT + EXPERTS * KD


def small_inputs(x):
    def groups(a):
        a = np.asarray(a)
        return np.moveaxis(a.reshape(a.shape[:-1] + (a.shape[-1] // P, P)), -1, 0)

    def rows(a):
        a = np.asarray(a)
        return a.reshape(a.shape[0] // P, P, a.shape[1]).transpose(1, 0, 2)

    gates = [x["gdn_w_beta"][0], x["gdn_w_beta"][1], x["gdn_w_decay"][0], x["gdn_w_decay"][1]]
    parts = [
        rows(np.stack([np.asarray(x["c"])[0], np.asarray(x["c_ctx"])], axis=1)),
        groups(x["ada_b"]), groups(x["norm_g"]),
        np.stack([np.tile(np.asarray(x["na_q_norm"]), 2), np.tile(np.asarray(x["na_k_norm"]), 2)], axis=1),
        groups(x["gdn_conv"]).transpose(0, 2, 1),
        rows(np.concatenate([np.asarray(g) for g in gates], axis=1)),
        np.broadcast_to(np.asarray(x["gdn_a_log"]).reshape(1, -1), (P, 2 * GH)),
        np.broadcast_to(np.asarray(x["gdn_dt_bias"]).reshape(1, -1), (P, 2 * GH)),
        np.asarray(x["gdn_out_norm"]).reshape(P, 1),
        rows(x["moe_router"][0]),
    ]
    return np.ascontiguousarray(np.concatenate([a.reshape(P, -1) for a in parts], axis=1))


def bias_table(rpb):
    rpb = np.asarray(rpb)
    t = np.zeros((NA_HEADS, BIAS_DC, DR), rpb.dtype)
    t[:, DC - 15:DC + 16, :] = rpb.transpose(0, 2, 1)[:, ::-1, ::-1]
    return np.concatenate([t.reshape(-1), np.zeros(BIAS_RUN, rpb.dtype)])


class Core:
    pass


def open_memory(nc, ctx, dram):
    m = Core()
    m.nc, m.ctx, m.dram = nc, ctx, dram

    def sb(name, cols):
        return ctx.enter_context(nc.sbuf_tensor(name, [P, cols], F32))

    m.xt = sb("residual", KD * TOK)
    m.ht = sb("hidden", KD * TOK)
    m.ring = sb("weight_ring", SLOTS * SLOT)
    m.work = sb("work", 19500)
    m.const = sb("constants", C_ALL)
    m.small = sb("small_inputs", S_ALL)
    m.mod = sb("modulation", 2 * 48 * 2)
    m.moda = sb("modulation_scale", 2 * 2 * KD * 2)
    m.sc = sb("silu_c", 2 * KD)[:, :]
    m.psum = [ctx.enter_context(nc.psum_tensor(f"bank{i}", [P, BANK], F32)) for i in range(8)]
    m.X = m.xt[:, :].rearrange("p (k t) -> p k t", k=KD)
    m.H = m.ht[:, :].rearrange("p (k t) -> p k t", k=KD)
    m.MOD = m.mod[:, :].rearrange("p (l c k v) -> p l c k v", l=2, c=6, k=KD)
    m.MODA = m.moda[:, :].rearrange("p (l n k v) -> p l n k v", l=2, n=2, k=KD)
    return m


def cut(m, at, cols):
    return m.work[:, at:at + cols]


def const(m, at, cols=P):
    return m.const[:, at:at + cols]


def semaphores(m, phase, names):
    return [m.ctx.enter_context(m.nc.semaphore(f"{phase}_{n}")) for n in names.split()]


def slot(m, n):
    return m.ring[:, n * SLOT:(n + 1) * SLOT]


ADA_EARLY = BANK // P


def modulation_scale(m, l, norm):
    g = m.small[:, S_NORM + (2 * l + norm) * KD:S_NORM + (2 * l + norm + 1) * KD]
    return m.nc.vector.scalar_tensor_tensor(out=m.MODA[:, l, norm], in0=m.MOD[:, l, 1 + 3 * norm], scalar=1.0,
                                            in1=g.unsqueeze(2).broadcast_to([P, KD, 2]), op0=ALU.add, op1=ALU.mult)


def load_and_modulation(m):
    nc, dram = m.nc, m.dram
    (small_in, turned, even_out, odd_out, silu_c, acc_ok, modulated, mod_sum, mod_scale) = semaphores(
        m, "in", "small_in turned even_out odd_out silu_c acc_ok modulated mod_sum mod_scale")
    tile_in = semaphores(m, "in", " ".join(f"tile_in{t}" for t in range(6)))
    slab_in = semaphores(m, "in", " ".join(f"slab_in{n}" for n in range(SLOTS + 1)))
    raw = cut(m, 0, 6 * D).rearrange("p (t d) -> p t d", t=6)
    sig = cut(m, 6 * D, 2 * KD)
    VEC_SLABS = (0, 2, 4)
    acc = cut(m, 6 * D + 2 * KD, len(VEC_SLABS) * 2 * BANK).rearrange("p (s v n) -> p s v n", s=len(VEC_SLABS), v=2)
    ident = const(m, C_IDENT)
    lat = dram["x"][0].rearrange("(r c) d -> c r d", c=GRID_C)
    adaw = dram["ada_w"].rearrange("l (k p) n -> l p k n", p=P)

    def slab(s):
        return (slot(m, s) if s < SLOTS else m.ht[:, 0:SLOT]).rearrange("p (k n) -> p k n", k=KD)

    with nc.Block() as block:

        @block.sync
        def _(sp):
            sp.dma_start(m.small[:, :], dram["small"]).then_inc(small_in, 16)
            sp.dma_start(m.const[:, :], dram["const"]).then_inc(small_in, 16)
            for t in range(6):
                src = dram["ctx"][0, t * P:(t + 1) * P, :] if t < 2 else lat[16 * (t - 2):16 * (t - 1)]
                sp.dma_start(raw[:, t, :], src).then_inc(tile_in[t], 16)
            for s in range(SLOTS + 1):
                src = adaw[0][:, :, s * BANK:(s + 1) * BANK] if s < SLOTS else adaw[1][:, :, 0:BANK]
                sp.dma_start(slab(s), src).then_inc(slab_in[s], 16)

        @block.tensor
        def _(pe):
            pe.wait_ge(small_in, 32)
            for n in range(12):
                if n % 2 == 0:
                    pe.wait_ge(tile_in[n // 2], 16)
                if n >= 6:
                    pe.wait_ge((even_out, odd_out)[n % 2], (n - 6) // 2 + 1)
                for k in range(4):
                    mm = nc.tensor.transpose(m.psum[n % 6][:, k * P:(k + 1) * P],
                                             raw[:, n // 2, (4 * (n % 2) + k) * P:(4 * (n % 2) + k + 1) * P], ident)
                mm.then_inc(turned, 1)
            pe.wait_ge(silu_c, 2)
            for s in range(SLOTS + 1):
                if s in VEC_SLABS:
                    continue
                pe.wait_ge(slab_in[s], 16)
                for g in range(4):
                    for k in range(KD):
                        mm = nc.tensor.matmul(m.psum[6][:, 2 * (4 * s + g):2 * (4 * s + g) + 2], slab(s)[:, k, g * P:(g + 1) * P],
                                              m.sc[:, 2 * k:2 * k + 2], start=(k == 0), stop=(k == KD - 1))
            for j, s in enumerate(VEC_SLABS):
                pe.wait_ge(acc_ok, (j + 1) * 2 * KD)
                for g in range(4):
                    for vec in range(2):
                        c = 2 * (4 * s + g) + vec
                        mm = nc.tensor.matmul(m.psum[6][:, c:c + 1], acc[:, j, vec, g * P:(g + 1) * P], const(m, C_ONES, 1), start=True, stop=True)
            mm.then_inc(modulated, 1)

        @block.scalar
        def _(act):
            act.wait_ge(small_in, 32)
            nc.scalar.activation(sig, m.small[:, S_C:S_C + 2 * KD], ACT.Sigmoid).then_inc(silu_c, 1)
            for n in range(1, 12, 2):
                act.wait_ge(turned, n + 1)
                nc.scalar.copy(m.X[:, 4:8, (n // 2) * P:(n // 2 + 1) * P],
                               m.psum[n % 6][:, :].rearrange("p (k t) -> p k t", k=4)).then_inc(odd_out, 1)

        @block.vector
        def _(dve):
            dve.wait_ge(silu_c, 1)
            nc.vector.tensor_tensor(m.sc, sig, m.small[:, S_C:S_C + 2 * KD], ALU.mult).then_inc(silu_c, 1)
            for n in range(0, 12, 2):
                dve.wait_ge(turned, n + 1)
                nc.vector.tensor_copy(m.X[:, 0:4, (n // 2) * P:(n // 2 + 1) * P],
                                      m.psum[n % 6][:, :].rearrange("p (k t) -> p k t", k=4)).then_inc(even_out, 1)
            dve.wait_ge(silu_c, 2)
            for j, s in enumerate(VEC_SLABS):
                dve.wait_ge(slab_in[s], 16)
                for k in range(KD):
                    if k:
                        dve.wait_ge(acc_ok, (j * KD + k) * 2)
                    for vec in range(2):
                        out, x = acc[:, j, vec, :], m.sc[:, 2 * k + vec:2 * k + vec + 1]
                        if k == 0:
                            nc.vector.tensor_scalar(out, slab(s)[:, k, :], x, None, ALU.mult).then_inc(acc_ok, 1)
                        else:
                            nc.vector.scalar_tensor_tensor(out=out, in0=slab(s)[:, k, :], scalar=x, in1=out, op0=ALU.mult,
                                                           op1=ALU.add).then_inc(acc_ok, 1)
            dve.wait_ge(modulated, 1)
            for g0, first, groups in ((0, 0, 2 * KD), (2 * KD, 48, ADA_EARLY)):
                b = m.small[:, S_ADAB + first:S_ADAB + first + groups].unsqueeze(2).broadcast_to([P, groups, 2])
                nc.vector.tensor_tensor(m.mod[:, 2 * first:2 * (first + groups)].rearrange("p (g v) -> p g v", v=2),
                                        m.psum[6][:, 2 * g0:2 * (g0 + groups)].rearrange("p (g v) -> p g v", v=2), b, ALU.add).then_inc(mod_sum, 1)
            dve.wait_ge(mod_sum, 2)
            modulation_scale(m, 0, 0).then_inc(mod_scale, 1)


def norm_modulate(m, name, layer, norm, first=0, ahead=None):
    nc = m.nc
    even_sq, odd_sq, summed, root, rstd_ok, scaled, hidden = semaphores(
        m, name, "even_sq odd_sq summed root rstd_ok scaled hidden")
    n_tok = TOK - first
    SQ = 4
    sq = cut(m, 0, SQ * TOK).rearrange("p (s t) -> p s t", s=SQ)
    rstd = cut(m, SQ * TOK, TOK)
    norm_x = cut(m, (SQ + 1) * TOK, KD * TOK).rearrange("p (k t) -> p k t", k=KD)
    parts = [(256, 768, 0)] + ([(0, 256, 1)] if first == 0 else [])
    with nc.Block() as block:

        if ahead:
            @block.sync
            def _(sp):
                ahead(sp)

        @block.gpsimd
        def _(pool):
            for k in range(0, KD, 2):
                if k >= SQ:
                    pool.wait_ge(summed, k - SQ + 1)
                nc.gpsimd.tensor_tensor(sq[:, k % SQ, first:TOK], m.X[:, k, first:TOK], m.X[:, k, first:TOK],
                                        ALU.mult).then_inc(even_sq, 1)

        @block.tensor
        def _(pe):
            for k in range(KD):
                pe.wait_ge((even_sq, odd_sq)[k % 2], k // 2 + 1)
                for b, (t0, t1, _) in enumerate(parts):
                    mm = nc.tensor.matmul(m.psum[b][:, 0:t1 - t0], const(m, C_MEAN), sq[:, k % SQ, t0:t1],
                                          start=(k == 0), stop=(k == KD - 1))
                mm.then_inc(summed, 1)

        @block.scalar
        def _(act):
            for k in range(1, KD, 2):
                if k >= SQ:
                    act.wait_ge(summed, k - SQ + 1)
                nc.scalar.activation(sq[:, k % SQ, first:TOK], m.X[:, k, first:TOK], ACT.Square).then_inc(odd_sq, 1)
            act.wait_ge(summed, KD)
            for b, (t0, t1, _) in enumerate(parts):
                nc.scalar.activation(rstd[:, t0:t1], m.psum[b][:, 0:t1 - t0], ACT.Sqrt,
                                     bias=const(m, C_EPS, 1)).then_inc(root, 1)
            for k in range(KD):
                act.wait_ge(scaled, k + 1)
                for t0, t1, v in parts:
                    nc.scalar.activation(m.H[:, k, t0:t1], norm_x[:, k, t0:t1], ACT.Identity, bias=m.MOD[:, layer, 3 * norm, k, v:v + 1],
                                         scale=m.MODA[:, layer, norm, k, v:v + 1]).then_inc(hidden, 1)

        @block.vector
        def _(dve):
            dve.wait_ge(root, len(parts))
            nc.vector.reciprocal(rstd[:, first:TOK], rstd[:, first:TOK]).then_inc(rstd_ok, 1)
            dve.wait_ge(rstd_ok, 1)
            for k in range(KD):
                nc.vector.tensor_tensor(norm_x[:, k, first:TOK], m.X[:, k, first:TOK], rstd[:, first:TOK],
                                        ALU.mult).then_inc(scaled, 1)


def attention_weights(m, u):
    return slot(m, u)[:, 0:3 * KD * P].rearrange("p (k n) -> p k n", k=KD)


def attention_bias(m):
    return cut(m, 19500 - 2 * BIAS_RUN, 2 * BIAS_RUN).rearrange("p (h n) -> p h n", h=2)


def load_attention_weights(m, sp, u, pair):
    wv = m.dram["na_w_qkv"].rearrange("(k p) (s n) -> p s k n", p=P, s=3)
    for s in range(3):
        sp.dma_start(attention_weights(m, u)[:, :, s * P:(s + 1) * P], wv[:, s, :, bass.ds(pair * P, P)]).then_inc(m.na_w_in[u], 16)


def load_attention_bias(m, sp, pair):
    for h in range(2):
        src = bass.AP(tensor=m.dram["bias"].tensor, offset=(pair * 2 + h) * (BIAS_DC * DR), ap=[[DR, 16], [1, 8], [1, BIAS_RUN]])
        sp.dma_start(attention_bias(m)[:, h, :], src).then_inc(m.na_bias_in, 16)


def attention_ahead(m):
    m.na_w_in = semaphores(m, "na", "w_in0 w_in1")
    m.na_bias_in, = semaphores(m, "na", "bias_in")

    def ahead(sp):
        for u in range(2):
            load_attention_weights(m, sp, u, u)
        load_attention_bias(m, sp, 0)

    return ahead


def neighbourhood_attention(m, ahead):
    nc, dram = m.nc, m.dram
    (projected, raw_out, v_out, squared, summed, root, inv, scaled, flipped, qk_ready, qk_gain, shifted, bias_ready, scored, biased, staged,
     maxed, exped, inverted, probs, turned, turned_out, weighted, out_copied, bias_used, ada_used, mod_sum, mod_scale) = semaphores(
        m, "na", "projected raw_out v_out squared summed root inv scaled flipped qk_ready qk_gain shifted bias_ready scored biased staged "
                 "maxed exped inverted probs turned turned_out weighted out_copied bias_used ada_used mod_sum mod_scale")
    w_in, bias_in = m.na_w_in, m.na_bias_in
    ada_in = semaphores(m, "na", "ada_in0 ada_in1 ada_in2 ada_in3")
    at = [0]

    def area(cols):
        at[0] += cols
        assert at[0] <= 19500 - 2 * BIAS_RUN
        return cut(m, at[0] - cols, cols)

    m.O = area(KD * TOK).rearrange("p (k t) -> p k t", k=KD)
    m.O_first = 0
    q, k_ = (area(2 * TOK).rearrange("p (u t) -> p u t", u=2) for _ in range(2))
    v = area(2 * TOK).rearrange("p (u t n) -> p u t n", u=2, t=6)
    vs = area(3 * P).rearrange("p (t n) -> p t n", t=3)
    sq = area(2 * P)
    ss, rstd = (area(6 * 4).rearrange("p (t g) -> p t g", t=6) for _ in range(2))
    table = attention_bias(m)
    bm = area(2 * 6 * WIN).rearrange("p (u h v n) -> p u h v n", u=2, h=2, v=3)
    NS = 3
    S = area(NS * BANK).rearrange("p (s n) -> p s n", s=NS)
    PT = area(2 * BANK).rearrange("p (s n) -> p s n", s=2)
    stats = area(4 * NS)
    gain = area(1)
    ident = const(m, C_IDENT)
    adaw = dram["ada_w"].rearrange("l (k p) n -> l p k n", p=P)
    UNITS = [(h, j) for j in (4, 5, 0, 1, 2, 3) for h in range(2)]
    FIRST_LAT = 4
    N = len(UNITS)
    LAST = NA_PAIRS // 2 - 1
    HALVES = ((0, 1), (2,), (3, 4), (5,), (6,), (7,), (8,), (9,), (10,), (11,), (), ())
    DONE = {0: 0, 2: 1, 3: 2, 5: 3, 7: 4, 9: 5}
    BATCHES = ((0, 4), (4, 6))
    NORM = {6: 0, 10: 1}
    FLIP = {7: 0, 8: 1, 11: 2}
    ADA_SLABS = 2
    ADA_UNIT = {6: 0, 9: 1}
    ada_steps = ring_steps(2 * ADA_SLABS, 4)

    def ada_slab(s):
        return m.ring[:, 2 * SLOT + s * KD * WIN:2 * SLOT + (s + 1) * KD * WIN].rearrange("p (k n) -> p k n", k=KD)

    def raw(t):
        c = (t // 4) * SLOT + 3 * KD * P + (t % 4) * 2 * P
        return m.ring[:, c:c + 2 * P]

    def weights(u):
        return attention_weights(m, u)

    def pairs(eng, body):
        with eng.Fori(0, LAST) as i:
            for u in range(2):
                body(i, u, i * 2 + u, True)
        for u in range(2):
            body(LAST, u, LAST * 2 + u, u == 0)

    with nc.Block() as block:

        @block.sync
        def _(sp):
            def shift_v(u):
                sp.dma_start(vs[0:64, :, :], v[64:128, u, 2:5, :]).then_inc(shifted, 16)
                sp.dma_start(vs[64:128, :, :], v[0:64, u, 3:6, :]).then_inc(shifted, 16)

            sp.wait_ge(v_out, 6)
            shift_v(0)

            def body(i, u, pair, more):
                if more:
                    sp.wait_ge(bias_used, pair + 1)
                    load_attention_bias(m, sp, pair + 1)
                if not isinstance(i, int):
                    sp.wait_ge(projected, pair * 6 + 6)
                    load_attention_weights(m, sp, u, pair + 2)
                for j in range(ADA_SLABS):
                    s, _, _, before = ada_steps[u * ADA_SLABS + j]
                    sp.wait_ge(ada_used, i * (2 * ADA_SLABS) + before)
                    col = pair * (WIN * ADA_SLABS) + (2 * D + WIN * j)
                    sp.dma_start(ada_slab(s), adaw[0][:, :, bass.ds(col, WIN)]).then_inc(ada_in[s], 16)
                if not more:
                    sp.wait_ge(flipped, NA_PAIRS * 3)
                    ahead(sp)
                if more:
                    sp.wait_ge(v_out, pair * 6 + 12)
                    sp.wait_ge(weighted, pair * N + N)
                    shift_v(1 - u)

            pairs(sp, body)

        @block.gpsimd
        def _(pool):
            def square(t, pair):
                pool.wait_ge(raw_out, pair * 6 + (t + 1))
                if t or not isinstance(pair, int) or pair:
                    pool.wait_ge(summed, pair * 6 + t)
                nc.gpsimd.tensor_tensor(sq, raw(t), raw(t), ALU.mult).then_inc(squared, 1)

            def bias(n, u):
                h, var = divmod(n, 3)
                src = table[:, h, :].rearrange("p (c r) -> p c r", r=DR)
                last = 47 - WIN_SHIFT[var]
                src = src[:, last - 31:last + 1, 0:WIN_R][:, ::-1, ::-1]
                mask = const(m, C_WMASK + 32 * var, 32).unsqueeze(2).broadcast_to([P, 32, WIN_R])
                nc.gpsimd.tensor_tensor(bm[:, u, h, var, :].rearrange("p (c r) -> p c r", r=WIN_R), src, mask,
                                        ALU.add).then_inc(bias_ready, 1)

            for t in range(6):
                square(t, 0)
            pool.wait_ge(bias_in, 32)
            for t in range(6):
                bias(t, 0)
            pool.wait_ge(bias_ready, 6)
            pool.sem_inc(bias_used, 1)

            def body(i, u, pair, more):
                if not more:
                    return
                for t in range(6):
                    square(t, pair + 1)
                    if t == 0:
                        pool.wait_ge(bias_in, pair * 32 + 64)
                    bias(t, 1 - u)
                pool.wait_ge(bias_ready, pair * 6 + 12)
                pool.sem_inc(bias_used, 1)

            pairs(pool, body)

        @block.tensor
        def _(pe):
            pe.sem_inc(ada_used, 2 * ADA_SLABS)
            pe.sem_inc(weighted, 2)

            def half_tile(n, pair, u):
                t = n // 2
                if n % 2 == 0:
                    pe.wait_ge(v_out, pair * 6 + t)
                for k in range(4 * (n % 2), 4 * (n % 2) + 4):
                    mm = nc.tensor.matmul(m.psum[6][:, 0:3 * P], m.H[:, k, t * P:(t + 1) * P], weights(u)[:, k, :],
                                          start=(k == 0), stop=(k == KD - 1))
                if n % 2:
                    mm.then_inc(projected, 1)

            def flip(g, pair):
                pe.wait_ge(scaled, pair * 2 + (g // 2 + 1))
                if g or not isinstance(pair, int) or pair:
                    pe.wait_ge(qk_ready, pair * 3 + g)
                for s in range(2):
                    for t in range(2):
                        mm = nc.tensor.transpose(m.psum[7][:, (2 * s + t) * P:(2 * s + t + 1) * P],
                                                 raw(2 * g + t)[:, s * P:(s + 1) * P], ident)
                mm.then_inc(flipped, 1)

            def scores(n, pair, u):
                if n >= N:
                    u = 1 - u
                h, j = UNITS[n % N]
                at_h = slice(64 * h, 64 * h + 64)
                out = m.psum[n % 2]
                qs = q[at_h, u, CTX + j * P:CTX + (j + 1) * P] if j < 4 else q[at_h, u, (j - 4) * P:(j - 3) * P]
                if j < 4:
                    k0 = CTX + WIN_START[j]
                    nc.tensor.matmul(out[:, 0:WIN], qs, k_[at_h, u, k0:k0 + WIN], start=True, stop=True)
                nc.tensor.matmul(out[:, WIN:WIN + CTX], qs, k_[at_h, u, 0:CTX], start=True, stop=True).then_inc(scored, 1)

            pe.wait_ge(w_in[0], 48)
            for t in range(6):
                for n in (2 * t, 2 * t + 1):
                    if n:
                        half_tile(n, 0, 0)
                    else:
                        for k in range(4):
                            nc.tensor.matmul(m.psum[6][:, 0:3 * P], m.H[:, k, 0:P], weights(0)[:, k, :], start=(k == 0), stop=False)
            for g in range(3):
                flip(g, 0)
            pe.wait_ge(qk_ready, 3)
            scores(0, 0, 0)
            scores(1, 0, 0)

            def body(i, u, pair, more):
                for n in range(N):
                    h, j = UNITS[n]
                    lat = j < 4
                    pe.wait_ge(probs, pair * N + (n + 1))
                    pe.wait_ge(turned_out, pair * N + (n + 1))
                    for c in range(0 if lat else 2, 4):
                        mm = nc.tensor.transpose(m.psum[2 + n % 2][:, c * P:(c + 1) * P], S[:, n % NS, c * P:(c + 1) * P], ident)
                    mm.then_inc(turned, 1)
                    if more and n in FLIP:
                        flip(FLIP[n], pair + 1)
                    if n + 2 < N or more:
                        if n + 2 == N:
                            pe.wait_ge(qk_ready, pair * 3 + 4)
                        if n + 2 == FIRST_LAT:
                            pe.wait_ge(qk_ready, pair * 3 + 3)
                        pe.wait_ge(staged, pair * N + (n + 1))
                        scores(n + 2, pair, u)
                    if more:
                        for half in HALVES[n]:
                            if half == 0:
                                pe.wait_ge(w_in[1 - u], i * 48 + 48 * (1 + u))
                            half_tile(half, pair + 1, 1 - u)
                    if n in ADA_UNIT:
                        sl = ADA_UNIT[n]
                        s, per, upto, _ = ada_steps[u * ADA_SLABS + sl]
                        pe.wait_ge(ada_in[s], i * (16 * per) + 16 * upto)
                        for g in range(2):
                            for k in range(KD):
                                mm = nc.tensor.matmul(m.psum[5][:, CTX + 2 * (2 * sl + g):CTX + 2 * (2 * sl + g) + 2],
                                                      ada_slab(s)[:, k, g * P:(g + 1) * P], m.sc[:, 2 * k:2 * k + 2],
                                                      start=(k == 0), stop=(k == KD - 1))
                        mm.then_inc(ada_used, 1)
                    pe.wait_ge(turned_out, pair * N + (n + 3))
                    if n == 0:
                        pe.wait_ge(out_copied, pair * 2 + 1)
                    if n == FIRST_LAT:
                        pe.wait_ge(out_copied, pair * 2 + 2)
                    if j == 1 and h == 0:
                        pe.wait_ge(shifted, pair * 32 + 32)
                    if lat:
                        near = [(v[:, u], 2), (vs, 0), (vs, 1), (v[:, u], 4)][j]
                        vals = [near[0][:, near[1], :], near[0][:, near[1] + 1, :], v[:, u, 0, :], v[:, u, 1, :]]
                        out = m.psum[4][64 * h:64 * h + 64, j * P:(j + 1) * P]
                    else:
                        vals = [None, None, v[:, u, 0, :], v[:, u, 1, :]]
                        out = m.psum[5][64 * h:64 * h + 64, (j - 4) * P:(j - 3) * P]
                    chunks = range(0 if lat else 2, 4)
                    for c in chunks:
                        mm = nc.tensor.matmul(out, vals[c][:, 64 * h:64 * h + 64], PT[:, n % 2, c * P:(c + 1) * P],
                                              start=(c == chunks[0]), stop=(c == 3))
                    mm.then_inc(weighted, 1)

            pairs(pe, body)

        @block.scalar
        def _(act):
            act.sem_inc(turned_out, 2)
            e64 = const(m, C_EPS + 1, 1)

            def take_raw(t, pair, u):
                act.wait_ge(projected, pair * 6 + (t + 1))
                nc.scalar.copy(raw(t), m.psum[6][:, 0:2 * P]).then_inc(raw_out, 1)
                nc.scalar.copy(v[:, u, t, :], m.psum[6][:, 2 * P:3 * P]).then_inc(v_out, 1)

            def take_root(batch, pair):
                t0, t1 = BATCHES[batch]
                act.wait_ge(summed, pair * 6 + t1)
                nc.scalar.activation(rstd[:, t0:t1], ss[:, t0:t1], ACT.Sqrt, bias=e64).then_inc(root, 1)

            def take_flipped(g, pair, u):
                act.wait_ge(flipped, pair * 3 + (g + 1))
                nc.scalar.activation(q[:, u, 2 * g * P:2 * (g + 1) * P], m.psum[7][:, 0:2 * P], ACT.Identity, scale=gain)
                nc.scalar.copy(k_[:, u, 2 * g * P:2 * (g + 1) * P], m.psum[7][:, 2 * P:4 * P]).then_inc(qk_ready, 1)

            def exp(n, pair):
                lo = 0 if UNITS[n % N][1] < 4 else WIN
                b = 4 * (n % NS)
                act.wait_ge(maxed, pair * N + (n + 1))
                nc.scalar.activation(S[:, n % NS, lo:BANK], S[:, n % NS, lo:BANK], ACT.Exp,
                                     bias=stats[:, b:b + 1], accum_out=stats[:, b + 2:b + 3]).then_inc(exped, 1)

            act.wait_ge(qk_gain, 2)
            for t in range(6):
                take_raw(t, 0, 0)
                if t in (3, 5):
                    take_root(t // 4, 0)
            for g in range(3):
                take_flipped(g, 0, 0)
            exp(0, 0)
            exp(1, 0)

            def body(i, u, pair, more):
                for n in range(N):
                    lo = 0 if UNITS[n][1] < 4 else WIN
                    act.wait_ge(turned, pair * N + (n + 1))
                    act.wait_ge(weighted, pair * N + (n + 1))
                    nc.scalar.copy(PT[:, n % 2, lo:BANK], m.psum[2 + n % 2][:, lo:BANK]).then_inc(turned_out, 1)
                    if more and n in NORM:
                        take_root(NORM[n], pair + 1)
                    if more and n in FLIP:
                        take_flipped(FLIP[n], pair + 1, 1 - u)
                    if n + 2 < N or more:
                        exp(n + 2, pair)
                    if more and n in DONE:
                        take_raw(DONE[n], pair + 1, 1 - u)

            pairs(act, body)

        @block.vector
        def _(dve):
            dve.sem_inc(out_copied, 2)
            nc.vector.tensor_tensor(gain, m.small[:, S_QN:S_QN + 1], m.small[:, S_QN + 1:S_QN + 2], ALU.mult).then_inc(qk_gain, 1)
            dve.wait_ge(qk_gain, 1)
            nc.vector.tensor_scalar(gain, gain, float(NA_HD) ** 0.5, None, ALU.mult).then_inc(qk_gain, 1)

            def sums(t, pair):
                dve.wait_ge(squared, pair * 6 + (t + 1))
                nc.vector.tensor_reduce(ss[:, t], sq.rearrange("p (g n) -> p g n", g=4), AX.X, ALU.add).then_inc(summed, 1)

            def scale(batch, pair):
                t0, t1 = BATCHES[batch]
                dve.wait_ge(root, pair * 2 + (batch + 1))
                nc.vector.reciprocal(rstd[:, t0:t1], rstd[:, t0:t1]).then_inc(inv, 1)
                dve.wait_ge(inv, pair * 2 + (batch + 1))
                for t in range(t0, t1):
                    op = nc.vector.tensor_tensor(raw(t).rearrange("p (g n) -> p g n", g=4), raw(t).rearrange("p (g n) -> p g n", g=4),
                                                 rstd[:, t].unsqueeze(2).broadcast_to([P, 4, NA_HD]), ALU.mult)
                op.then_inc(scaled, 1)

            def stage(n, pair, u):
                if n >= N:
                    u = 1 - u
                h, j = UNITS[n % N]
                b = 4 * (n % NS)
                lo = 0 if j < 4 else WIN
                dve.wait_ge(scored, pair * N + (n + 1))
                if n == FIRST_LAT:
                    dve.wait_ge(bias_ready, pair * 6 + 6)
                if j < 4:
                    nc.vector.tensor_tensor(S[:, n % NS, 0:WIN], m.psum[n % 2][:, 0:WIN], bm[:, u, h, WIN_VARIANT[j], :],
                                            ALU.add).then_inc(biased, 1)
                nc.vector.tensor_copy(S[:, n % NS, WIN:BANK], m.psum[n % 2][:, WIN:BANK]).then_inc(staged, 1)
                if j < 4:
                    dve.wait_ge(biased, pair * (N - FIRST_LAT) + (n - FIRST_LAT + 1))
                dve.wait_ge(staged, pair * N + (n + 1))
                nc.vector.tensor_reduce(stats[:, b:b + 1], S[:, n % NS, lo:BANK], AX.X, ALU.max, negate=True).then_inc(maxed, 1)

            def normalise(n, pair):
                b = 4 * (n % NS)
                lo = 0 if UNITS[n % N][1] < 4 else WIN
                dve.wait_ge(exped, pair * N + (n + 1))
                nc.vector.reciprocal(stats[:, b + 3:b + 4], stats[:, b + 2:b + 3]).then_inc(inverted, 1)
                dve.wait_ge(inverted, pair * N + (n + 1))
                nc.vector.tensor_scalar(S[:, n % NS, lo:BANK], S[:, n % NS, lo:BANK], stats[:, b + 3:b + 4], None,
                                        ALU.mult).then_inc(probs, 1)

            for t in range(6):
                sums(t, 0)
                if t in (3, 5):
                    scale(t // 4, 0)
            for n in range(2):
                stage(n, 0, 0)
            for n in range(2):
                normalise(n, 0)

            def body(i, u, pair, more):
                for n in range(N):
                    if n == N - 2:
                        dve.wait_ge(weighted, pair * N + N)
                        dve.wait_ge(ada_used, i * (2 * ADA_SLABS) + (2 * ADA_SLABS + (u + 1) * ADA_SLABS))
                        nc.vector.tensor_copy(m.O[:, bass.ds(pair, 1), 0:CTX], m.psum[5][:, 0:CTX].unsqueeze(1))
                        groups, first = 2 * ADA_SLABS, 2 * KD
                        b = m.small[:, bass.ds(pair * groups + (S_ADAB + first), groups)].unsqueeze(2).broadcast_to([P, groups, 2])
                        nc.vector.tensor_tensor(
                            m.mod[:, bass.ds(pair * (2 * groups) + 2 * first, 2 * groups)].rearrange("p (g v) -> p g v", v=2),
                            m.psum[5][:, CTX:CTX + 2 * groups].rearrange("p (g v) -> p g v", v=2), b, ALU.add).then_inc(mod_sum, 1)
                        dve.wait_ge(mod_sum, pair + 1)
                        dve.sem_inc(out_copied, 1)
                    if n + 2 < N or more:
                        stage(n + 2, pair, u)
                    if more and n in NORM:
                        scale(NORM[n], pair + 1)
                    if n + 2 < N or more:
                        normalise(n + 2, pair)
                    if more and n in DONE:
                        sums(DONE[n], pair + 1)
                dve.wait_ge(weighted, pair * N + (N + 2))
                nc.vector.tensor_copy(m.O[:, bass.ds(pair, 1), CTX:TOK], m.psum[4][:, :].unsqueeze(1)).then_inc(out_copied, 1)

            pairs(dve, body)
            modulation_scale(m, 0, 1).then_inc(mod_scale, 1)




def ring_steps(n_slabs, n_slots):
    steps = []
    for j in range(n_slabs):
        same = [x for x in range(n_slabs) if x % n_slots == j % n_slots]
        at = same.index(j)
        before = n_slabs + same[at - 1] + 1 if at else same[-1] + 1
        steps.append((j % n_slots, len(same), at + 1, before))
    return steps


def projection_ahead(m, name, weight):
    m.w_o_in = semaphores(m, name, "w_in0 w_in1")
    w = weight.rearrange("(k p) n -> p k n", p=P)

    def ahead(sp):
        for s in range(2):
            sp.dma_start(slot(m, s).rearrange("p (k n) -> p k n", k=KD), w[:, :, s * BANK:(s + 1) * BANK]).then_inc(m.w_o_in[s], 16)

    return ahead


def project_to_residual(m, name, layer, first, load=None):
    nc = m.nc
    w_in = m.w_o_in
    product, added = semaphores(m, name, "product added")
    parts = [(CTX, TOK, 0)] + ([(0, CTX, 1)] if first == 0 else [])
    with nc.Block() as block:

        if load:
            @block.sync
            def _(sp):
                load(sp)

        @block.tensor
        def _(pe):
            for g in range(KD):
                pe.wait_ge(w_in[g // 4], 16)
                if g >= 4:
                    pe.wait_ge(added, (g - 3) * len(parts))
                ws = slot(m, g // 4).rearrange("p (k n) -> p k n", k=KD)
                for b, (t0, t1, _) in enumerate(parts):
                    for k in range(KD):
                        mm = nc.tensor.matmul(m.psum[2 * (g % 4) + b][:, 0:t1 - t0], ws[:, k, (g % 4) * P:(g % 4 + 1) * P],
                                              m.O[:, k, t0 - m.O_first:t1 - m.O_first], start=(k == 0), stop=(k == KD - 1))
                    mm.then_inc(product, 1)

        @block.vector
        def _(dve):
            for g in range(KD):
                for b, (t0, t1, v) in enumerate(parts):
                    dve.wait_ge(product, g * len(parts) + b + 1)
                    nc.vector.scalar_tensor_tensor(out=m.X[:, g, t0:t1], in0=m.psum[2 * (g % 4) + b][:, 0:t1 - t0],
                                                   scalar=m.MOD[:, layer, 2, g, v:v + 1], in1=m.X[:, g, t0:t1],
                                                   op0=ALU.mult, op1=ALU.add).then_inc(added, 1)


def swiglu_chunk(m, s):
    return slot(m, s)[:, 0:2 * KD * P].rearrange("p (s k n) -> p s k n", s=2, k=KD)


def load_swiglu_chunk(m, sp, c, column):
    wi = m.dram["ffn_w_in"][0].rearrange("(k p) (s n) -> p s k n", p=P, s=2)
    for ab in range(2):
        sp.dma_start(swiglu_chunk(m, c)[:, ab], wi[:, ab, :, column]).then_inc(m.ffn_w_in[c], 16)


def swiglu_ahead(m):
    m.ffn_w_in = semaphores(m, "ffn", "w_in0 w_in1")

    def ahead(sp):
        for c in range(2):
            load_swiglu_chunk(m, sp, c, slice(c * P, (c + 1) * P))

    return ahead


def swiglu(m):
    nc, dram = m.nc, m.dram
    FK = FFN // P
    CHUNKS = 2
    w_in = m.ffn_w_in
    out_in = semaphores(m, "ffn", "out_in0 out_in1 out_in2 out_in3")
    product, gated, silu_ok, out_product, added, acc_ok, mod_sum, mod_scale = semaphores(
        m, "ffn", "product gated silu_ok out_product added acc_ok mod_sum mod_scale")
    ada_in = semaphores(m, "ffn", "ada_in0 ada_in1")
    ADA = 2
    assert ADA_EARLY + ADA * FK == 48
    G = cut(m, 0, FK * TOK).rearrange("p (k t) -> p k t", k=FK)
    sa = cut(m, FK * TOK, 2 * TOK).rearrange("p (s t) -> p s t", s=2)
    acc = cut(m, (FK + 2) * TOK, 2 * ADA * P).rearrange("p (g v n) -> p g v n", g=ADA, v=2)
    adaw = dram["ada_w"][1].rearrange("(k p) n -> p k n", p=P)
    wo = dram["ffn_w_out"][0].rearrange("(k p) n -> p k n", p=P)

    def in_slab(s):
        return swiglu_chunk(m, s)

    def out_slab(s):
        return slot(m, s)[:, 0:FK * P].rearrange("p (k n) -> p k n", k=FK)

    def ada_slab(g):
        return slot(m, 2 + g)[:, FK * P:(FK + KD) * P].rearrange("p (k n) -> p k n", k=KD)

    with nc.Block() as block:

        @block.sync
        def _(sp):
            def body(i, c, first):
                if not first:
                    sp.wait_ge(gated, i * (2 * CHUNKS) + 2 * c + 2)
                    load_swiglu_chunk(m, sp, c, bass.ds(i * (CHUNKS * P) + c * P, P))
                for g in range(ADA):
                    sp.wait_ge(acc_ok, i * (CHUNKS * ADA * 2 * KD) + (c * ADA + g + 1) * 2 * KD)
                    sp.dma_start(ada_slab(g), adaw[:, :, bass.ds(i * (CHUNKS * ADA * P) + (ADA_EARLY + c * ADA + g) * P, P)])\
                        .then_inc(ada_in[g], 16)

            for c in range(CHUNKS):
                body(0, c, True)
            with sp.Fori(1, FK // CHUNKS) as i:
                for c in range(CHUNKS):
                    body(i, c, False)
            for g in range(2):
                sp.dma_start(out_slab(2 + g), wo[:, :, g * P:(g + 1) * P]).then_inc(out_in[g], 16)
            for g in range(2, KD):
                if g < 4:
                    sp.wait_ge(gated, 2 * CHUNKS + 2 * (FK + g - 3))
                else:
                    sp.wait_ge(out_product, (g - 3) * 2)
                sp.dma_start(out_slab((g + 2) % 4), wo[:, :, g * P:(g + 1) * P]).then_inc(out_in[g % 4], 16)

        @block.tensor
        def _(pe):
            pe.sem_inc(gated, 2 * CHUNKS)
            with pe.Fori(0, FK // CHUNKS) as i:
                for c in range(CHUNKS):
                    pe.wait_ge(w_in[c], i * 32 + 32)
                    pe.wait_ge(gated, i * (2 * CHUNKS) + 2 * c + 2)
                    w, bank = in_slab(c), 4 * c
                    for ab in range(2):
                        for k in range(KD):
                            mm = nc.tensor.matmul(m.psum[bank + ab][:, :], w[:, ab, k, :], m.H[:, k, CTX:TOK],
                                                  start=(k == 0), stop=(k == KD - 1))
                    mm.then_inc(product, 1)
                    for ab in range(2):
                        for k in range(KD):
                            mm = nc.tensor.matmul(m.psum[bank + 2 + ab][:, 0:CTX], w[:, ab, k, :], m.H[:, k, 0:CTX],
                                                  start=(k == 0), stop=(k == KD - 1))
                    pe.wait_ge(acc_ok, i * (CHUNKS * ADA * 2 * KD) + (c + 2) * ADA * 2 * KD)
                    for g in range(ADA):
                        for vec in range(2):
                            at = CTX + 2 * g + vec
                            mm = nc.tensor.matmul(m.psum[bank + 3][:, at:at + 1], acc[:, g, vec, :], const(m, C_ONES, 1), start=True, stop=True)
                    mm.then_inc(product, 1)
            for g in range(KD):
                pe.wait_ge(out_in[g % 4], 16 * (g // 4 + 1))
                if g < 4:
                    pe.wait_ge(gated, 2 * FK + 2 * CHUNKS)
                else:
                    pe.wait_ge(added, (g - 3) * 2)
                for b, (t0, t1) in enumerate(((CTX, TOK), (0, CTX))):
                    for k in range(FK):
                        mm = nc.tensor.matmul(m.psum[2 * (g % 4) + b][:, 0:t1 - t0], out_slab((g + 2) % 4)[:, k, :], G[:, k, t0:t1],
                                              start=(k == 0), stop=(k == FK - 1))
                    mm.then_inc(out_product, 1)

        @block.scalar
        def _(act):
            with act.Fori(0, FK // CHUNKS) as i:
                for c in range(CHUNKS):
                    act.wait_ge(gated, i * (2 * CHUNKS) + 2 * c + 2)
                    for b, (t0, t1) in enumerate(((CTX, TOK), (0, CTX))):
                        act.wait_ge(product, i * (2 * CHUNKS) + 2 * c + b + 1)
                        nc.scalar.activation(sa[:, c, t0:t1], m.psum[4 * c + 2 * b][:, 0:t1 - t0], ACT.Silu).then_inc(silu_ok, 1)

        @block.vector
        def _(dve):
            dve.sem_inc(acc_ok, ADA * 2 * KD)
            with dve.Fori(0, FK // CHUNKS) as i:
                for c in range(CHUNKS):
                    for g in range(ADA):
                        dve.wait_ge(ada_in[g], i * (16 * CHUNKS) + 16 * (c + 1))
                        for k in range(KD):
                            if k:
                                dve.wait_ge(acc_ok, i * (CHUNKS * ADA * 2 * KD) + (((c + 1) * ADA + g) * KD + k) * 2)
                            for vec in range(2):
                                out, x = acc[:, g, vec, :], m.sc[:, 2 * k + vec:2 * k + vec + 1]
                                if k == 0:
                                    nc.vector.tensor_scalar(out, ada_slab(g)[:, k, :], x, None, ALU.mult).then_inc(acc_ok, 1)
                                else:
                                    nc.vector.scalar_tensor_tensor(out=out, in0=ada_slab(g)[:, k, :], scalar=x, in1=out, op0=ALU.mult,
                                                                   op1=ALU.add).then_inc(acc_ok, 1)
                    for b, (t0, t1) in enumerate(((CTX, TOK), (0, CTX))):
                        dve.wait_ge(silu_ok, i * (2 * CHUNKS) + 2 * c + b + 1)
                        if b:
                            first = 48 + ADA_EARLY
                            bias = m.small[:, bass.ds(i * (CHUNKS * ADA) + (S_ADAB + first + c * ADA), ADA)].unsqueeze(2).broadcast_to([P, ADA, 2])
                            nc.vector.tensor_tensor(
                                m.mod[:, bass.ds(i * (2 * CHUNKS * ADA) + 2 * (first + c * ADA), 2 * ADA)].rearrange("p (g v) -> p g v", v=2),
                                m.psum[4 * c + 3][:, CTX:CTX + 2 * ADA].rearrange("p (g v) -> p g v", v=2), bias, ALU.add).then_inc(mod_sum, 1)
                        nc.vector.tensor_tensor(G[:, bass.ds(i * CHUNKS + c, 1), t0:t1], sa[:, c, t0:t1].unsqueeze(1),
                                                m.psum[4 * c + 2 * b + 1][:, 0:t1 - t0].unsqueeze(1), ALU.mult).then_inc(gated, 1)
            dve.wait_ge(mod_sum, FK)
            for norm in range(2):
                modulation_scale(m, 1, norm).then_inc(mod_scale, 1)
            for g in range(KD):
                for b, (t0, t1) in enumerate(((CTX, TOK), (0, CTX))):
                    dve.wait_ge(out_product, 2 * g + b + 1)
                    nc.vector.scalar_tensor_tensor(out=m.X[:, g, t0:t1], in0=m.psum[2 * (g % 4) + b][:, 0:t1 - t0],
                                                   scalar=m.MOD[:, 0, 5, g, b:b + 1], in1=m.X[:, g, t0:t1],
                                                   op0=ALU.mult, op1=ALU.add).then_inc(added, 1)


def reorder(m):
    nc = m.nc
    copied, = semaphores(m, "reorder", "copied")
    back, = semaphores(m, "reorder", "back")
    tmp = cut(m, 0, KD * LAT).rearrange("p (k t) -> p k t", k=KD)
    with nc.Block() as block:

        @block.vector
        def _(dve):
            for k in range(KD):
                nc.vector.tensor_copy(tmp[:, k, :].rearrange("p (r c) -> p r c", c=GRID_C),
                                      m.X[:, k, CTX:TOK].rearrange("p (c r) -> p r c", r=GRID_R)).then_inc(copied, 1)

        @block.scalar
        def _(act):
            for k in range(KD):
                act.wait_ge(copied, k + 1)
                nc.scalar.copy(m.X[:, k, CTX:TOK], tmp[:, k, :]).then_inc(back, 1)


def experts(m):
    nc, dram = m.nc, m.dram
    EK = EFF // P
    SLABS = 6
    ROUND = EXPERTS
    TURNS = 2 * EXPERTS
    HALF = 2 * P
    I32 = mybir.dt.int32
    w_in = semaphores(m, "moe", "w_in0 w_in1 w_in2")
    out_in = semaphores(m, "moe", "out_in0 out_in1")
    (h_turned, h_even, h_odd, logits, logits_ok, top, weights, route_exp, routed, ranked, rank_ok, table_ok, built, gathered, gather_out,
     sel_turned, sel_out, product, silu_ok, gated, turned, turned_out, summed, sum_out, scattered, now_ok, added) = semaphores(
        m, "moe", "h_turned h_even h_odd logits logits_ok top weights route_exp routed ranked rank_ok table_ok built gathered gather_out "
                  "sel_turned sel_out product silu_ok gated turned turned_out summed sum_out scattered now_ok added")
    at = [0]

    def area(cols):
        at[0] += cols
        assert at[0] <= 19500
        return cut(m, at[0] - cols, cols)

    HT = area(4 * D).rearrange("p (t d) -> p t d", t=4)
    XG = area(KD * HALF).rearrange("p (k s) -> p k s", k=KD)
    sa = area(2 * HALF * 2).rearrange("p (u b n) -> p u b n", u=2, b=2)
    G = area(2 * EFF).rearrange("p (b n) -> p b n", b=2)
    GT = area(2 * EFF).rearrange("p (b k s) -> p b k s", b=2, k=EK)
    SEL = area(4 * HALF).rearrange("p (t s) -> p t s", t=4)
    SELG = area(4 * HALF).rearrange("p (t s) -> p t s", t=4)
    SELT = area(2 * LAT).rearrange("p (b t) -> p b t", b=2)
    lg, idxf = (area(4 * 8).rearrange("p (t e) -> p t e", t=4) for _ in range(2))
    top8 = area(4 * 8).rearrange("p (t e) -> p t e", t=4)
    idx = area(4 * 8).bitcast(U32).rearrange("p (t e) -> p t e", t=4)
    eq = area(2 * 4 * 8).rearrange("p (w t e) -> p w t e", w=2, t=4)
    small = area(4 * 4).rearrange("p (w t) -> p w t", w=4)
    table = area(3 * (TURNS + 1) * 4).rearrange("p (c e t) -> p c e t", c=3, e=TURNS + 1)
    count = area(EXPERTS + 1)
    county = area(EXPERTS + 1).bitcast(I32)
    now = area(3 * 4).rearrange("p (c t) -> p c t", c=3)
    IN = KD * BANK
    out_tail = area((EK - KD) * BANK)
    out_pieces = (((0, EK, m.ht[:, 0:EK * BANK]),), ((0, KD, m.ring[:, 3 * IN:4 * IN]), (KD, EK, out_tail)))

    def in_slab(s):
        return m.ring[:, s * IN:(s + 1) * IN]

    def SUM(k, b):
        return m.X[:, k, b * P:(b + 1) * P]

    def out_weights(half, k):
        for k0, k1, piece in out_pieces[half]:
            if k0 <= k < k1:
                return piece[:, (k - k0) * BANK:(k - k0 + 1) * BANK]

    wi = dram["moe_w_in"].rearrange("l e (k p) (s n) -> (l e) p s k n", p=P, s=2)
    wo = dram["moe_w_out"].rearrange("l e (k p) n -> (l e) p k n", p=P)
    steps = ring_steps(SLABS, 3)
    ident = const(m, C_IDENT)
    B = m.psum
    Y_BANKS = ((5, 6), (7, 5))

    def width(s):
        return HALF if s < SLABS - 1 else P

    def rounds(eng, turn):
        eng.wait_ge(table_ok, 2)
        most = eng.value_load(county[0:1, EXPERTS:EXPERTS + 1], min_val=0, max_val=LAT)
        with eng.Fori(0, EXPERTS) as e:
            mine = eng.value_load(county[0:1, bass.ds(e, 1)], min_val=0, max_val=LAT)
            with eng.If(mine > P):
                turn(e, 2)
            with eng.Else():
                turn(e, 1)
        with eng.If(most > HALF):
            with eng.Fori(EXPERTS, TURNS) as it:
                turn(it, 2)

    with nc.Block() as block:

        @block.sync
        def _(sp):
            def turn(it, e):
                for j, (s, _, _, before) in enumerate(steps):
                    sp.wait_ge(product, it * SLABS + before)
                    n = width(j)
                    dst = in_slab(s)[:, 0:KD * 2 * n].rearrange("p (k s n) -> p s k n", k=KD, s=2)
                    for ab in range(2):
                        sp.dma_start(dst[:, ab], wi[bass.ds(e, 1), :, ab, :, j * HALF:j * HALF + n].rearrange("o p k n -> (o p) k n"))\
                            .then_inc(w_in[s], 16)
                for j in range(2):
                    sp.wait_ge(summed, it * 2 + j + 1)
                    for k0, k1, piece in out_pieces[j]:
                        sp.dma_start(piece.rearrange("p (k n) -> p k n", k=k1 - k0),
                                     wo[bass.ds(e, 1), :, k0:k1, j * BANK:(j + 1) * BANK].rearrange("o p k n -> (o p) k n"))\
                            .then_inc(out_in[j], 16)

            with sp.Fori(0, EXPERTS) as e:
                turn(e, e)
            sp.wait_ge(table_ok, 2)
            most = sp.value_load(county[0:1, EXPERTS:EXPERTS + 1], min_val=0, max_val=LAT)
            with sp.If(most > HALF):
                with sp.Fori(0, EXPERTS) as e:
                    turn(e + EXPERTS, e)

        @block.tensor
        def _(pe):
            pe.sem_inc(product, SLABS)
            for n in range(8):
                if n >= 4:
                    pe.wait_ge((h_even, h_odd)[n % 2], (n - 4) // 2 + 1)
                for k in range(4):
                    mm = nc.tensor.transpose(B[n % 4][:, k * P:(k + 1) * P],
                                             m.H[:, 4 * (n % 2) + k, CTX + (n // 2) * P:CTX + (n // 2 + 1) * P], ident)
                mm.then_inc(h_turned, 1)
            for t in range(4):
                for k in range(KD):
                    mm = nc.tensor.matmul(B[6][:, 8 * t:8 * t + 8], m.H[:, k, CTX + t * P:CTX + (t + 1) * P],
                                          m.small[:, S_RT + 8 * k:S_RT + 8 * k + 8], start=(k == 0), stop=(k == KD - 1))
            mm.then_inc(logits, 1)
            pe.sem_inc(summed, 2)
            pe.wait_ge(routed, 2)
            for t in range(5):
                last = min(t, 3)
                for u in range(last + 1):
                    mm = nc.tensor.matmul(B[7][:, 8 * t:8 * t + 8], const(m, C_BEFORE if u == t else C_ONES), idxf[:, u, :],
                                          start=(u == 0), stop=(u == last))
            mm.then_inc(ranked, 1)

            def turn(it, nb):
                N = nb * P
                pe.wait_ge(built, it + 1)
                for j in range(4):
                    pe.wait_ge(added, it * KD + 4 + j + 1)
                    for k in range(2 * j, 2 * j + 2):
                        for t in range(4):
                            mm = nc.tensor.matmul(B[j][:, (k % 2) * N:(k % 2 + 1) * N], HT[:, t, k * P:(k + 1) * P], SEL[:, t, 0:N],
                                                  start=(t == 0), stop=(t == 3))
                    mm.then_inc(gathered, 1)
                for b in range(nb):
                    for t in range(4):
                        mm = nc.tensor.transpose(B[6 + b][:, t * P:(t + 1) * P], SELG[:, t, b * P:(b + 1) * P], ident)
                mm.then_inc(sel_turned, 1)

                def up(s):
                    slot_, per, upto, _ = steps[s]
                    n = 2 * width(s)
                    pe.wait_ge(w_in[slot_], it * (32 * per) + 32 * upto)
                    if s >= 2:
                        pe.wait_ge(gated, it * SLABS + s - 1)
                    else:
                        pe.wait_ge(gather_out, it * 4 + 4)
                    w = in_slab(slot_)[:, 0:KD * n].rearrange("p (k n) -> p k n", k=KD)
                    for b in range(nb):
                        for k in range(KD):
                            mm = nc.tensor.matmul(B[2 * (s % 2) + b][:, 0:n], XG[:, k, b * P:(b + 1) * P], w[:, k, :],
                                                  start=(k == 0), stop=(k == KD - 1))
                    mm.then_inc(product, 1)

                def turn_hidden(s):
                    pe.wait_ge(gated, it * SLABS + s + 1)
                    if s >= 1:
                        pe.wait_ge(turned_out, it * SLABS + s)
                    for b in range(nb):
                        for k in range(width(s) // P):
                            mm = nc.tensor.transpose(B[4][:, (2 * b + k) * P:(2 * b + k + 1) * P],
                                                     G[:, b, s * HALF + k * P:s * HALF + (k + 1) * P], ident)
                    mm.then_inc(turned, 1)

                for s in range(SLABS):
                    up(s)
                    if s:
                        turn_hidden(s - 1)
                for half in range(2):
                    pe.wait_ge(out_in[half], it * (16 * len(out_pieces[half])) + 16 * len(out_pieces[half]))
                    for b in range(nb):
                        bank = Y_BANKS[half][b]
                        if (half, b) == (0, 0):
                            pe.wait_ge(sel_out, it + 1)
                        if (half, b) == (1, 1):
                            pe.wait_ge(sum_out, it * 2 + 1)
                        for k in range(EK):
                            if (half, b) == (0, 0):
                                if k == 0:
                                    pe.wait_ge(turned_out, it * SLABS + 4)
                                if k == 6:
                                    turn_hidden(SLABS - 1)
                                if k == 8:
                                    pe.wait_ge(turned_out, it * SLABS + SLABS)
                            mm = nc.tensor.matmul(B[bank][:, :], GT[:, b, k, :], out_weights(half, k), start=(k == 0), stop=(k == EK - 1))
                    mm.then_inc(summed, 1)
                for k in range(KD):
                    if k == 0 or k == 4:
                        pe.wait_ge(sum_out, it * 2 + k // 4 + 1)
                    if k >= 4:
                        pe.wait_ge(added, it * KD + KD + k - 3)
                    for b in range(nb):
                        mm = nc.tensor.matmul(B[k % 4][:, :], SUM(k, b), SELT[:, b, :], start=(b == 0), stop=(b == nb - 1))
                    mm.then_inc(scattered, 1)

            rounds(pe, turn)

        @block.scalar
        def _(act):
            for n in range(1, 8, 2):
                act.wait_ge(h_turned, n + 1)
                nc.scalar.copy(HT[:, n // 2, BANK:D], B[n % 4][:, :]).then_inc(h_odd, 1)
            act.wait_ge(weights, 1)
            nc.scalar.activation(small[:, 1, :], small[:, 0, :], ACT.Exp).then_inc(route_exp, 1)

            def turn(it, nb):
                N = nb * P
                for j in range(4):
                    act.wait_ge(gathered, it * 4 + j + 1)
                    nc.scalar.copy(XG[:, 2 * j:2 * j + 2, 0:N], B[j][:, 0:2 * N].rearrange("p (k s) -> p k s", k=2)).then_inc(gather_out, 1)

                def silu(s):
                    n = width(s)
                    act.wait_ge(product, it * SLABS + SLABS + s + 1)
                    for b in range(nb):
                        op = nc.scalar.activation(sa[:, s % 2, b, 0:n], B[2 * (s % 2) + b][:, 0:n], ACT.Silu)
                    op.then_inc(silu_ok, 1)

                def copy_hidden(s):
                    k = width(s) // P
                    act.wait_ge(turned, it * SLABS + s + 1)
                    nc.scalar.copy(GT[:, 0:nb, 2 * s:2 * s + k, :],
                                   B[4][:, 0:nb * 2 * P].rearrange("p (b k s) -> p b k s", b=nb, k=2)[:, :, 0:k, :]).then_inc(turned_out, 1)

                silu(0)
                for s in range(1, SLABS):
                    silu(s)
                    copy_hidden(s - 1)
                copy_hidden(SLABS - 1)
                for half in range(2):
                    act.wait_ge(summed, it * 2 + 2 + half + 1)
                    for b in range(nb):
                        op = nc.scalar.copy(m.X[:, 4 * half:4 * half + 4, b * P:(b + 1) * P],
                                            B[Y_BANKS[half][b]][:, :].rearrange("p (k n) -> p k n", k=4))
                    op.then_inc(sum_out, 1)

            rounds(act, turn)

        @block.vector
        def _(dve):
            dve.sem_inc(added, KD)
            for n in range(0, 8, 2):
                dve.wait_ge(h_turned, n + 1)
                nc.vector.tensor_copy(HT[:, n // 2, 0:BANK], B[n % 4][:, :]).then_inc(h_even, 1)
            dve.wait_ge(logits, 1)
            nc.vector.tensor_copy(lg, B[6][:, 0:32].rearrange("p (t e) -> p t e", t=4)).then_inc(logits_ok, 1)
            dve.wait_ge(logits_ok, 1)
            for t in range(4):
                nc.vector.max(top8[:, t, :], lg[:, t, :]).then_inc(top, 1)
            dve.wait_ge(top, 4)
            for t in range(4):
                nc.vector.max_index(idx[:, t, :], top8[:, t, :], lg[:, t, :]).then_inc(top, 1)
            nc.vector.tensor_tensor(small[:, 0, :], top8[:, :, 1], top8[:, :, 0], ALU.subtract).then_inc(weights, 1)
            dve.wait_ge(top, 8)
            nc.vector.tensor_copy(idxf, idx).then_inc(top, 1)
            dve.wait_ge(top, 9)
            iota = const(m, C_IOTA, EXPERTS).unsqueeze(1).broadcast_to([P, 4, EXPERTS])
            for w in range(2):
                nc.vector.tensor_tensor(eq[:, w], idxf[:, :, w:w + 1].broadcast_to([P, 4, EXPERTS]), iota, ALU.is_equal).then_inc(top, 1)
            dve.wait_ge(top, 11)
            nc.vector.tensor_tensor(idxf, eq[:, 0], eq[:, 1], ALU.add).then_inc(routed, 2)
            dve.wait_ge(route_exp, 1)
            nc.vector.tensor_scalar(small[:, 2, :], small[:, 1, :], 1.0, None, ALU.add).then_inc(weights, 1)
            dve.wait_ge(weights, 2)
            nc.vector.reciprocal(small[:, 2, :], small[:, 2, :]).then_inc(weights, 1)
            dve.wait_ge(weights, 3)
            nc.vector.tensor_tensor(small[:, 3, :], small[:, 1, :], small[:, 2, :], ALU.mult).then_inc(weights, 1)
            dve.wait_ge(weights, 4)
            dve.wait_ge(routed, 2)
            for w in range(2):
                nc.vector.tensor_tensor(eq[:, w], eq[:, w], small[:, 2 + w, :].unsqueeze(2).broadcast_to([P, 4, EXPERTS]),
                                        ALU.mult).then_inc(top, 1)
            dve.wait_ge(top, 13)
            for r in range(2):
                def of(c):
                    return table[:, c, r * EXPERTS:(r + 1) * EXPERTS, :].rearrange("p e t -> p t e")
                nc.vector.tensor_tensor(of(0), eq[:, 0], eq[:, 1], ALU.add).then_inc(rank_ok, 1)
                nc.vector.tensor_copy(of(1), idxf).then_inc(rank_ok, 1)
            nc.vector.memset(table[:, :, TURNS, :], 0.0).then_inc(rank_ok, 1)
            dve.wait_ge(ranked, 1)
            ranks = B[7][:, 0:32].rearrange("p (t e) -> p t e", t=4)
            for r in range(2):
                nc.vector.tensor_scalar(table[:, 2, r * EXPERTS:(r + 1) * EXPERTS, :].rearrange("p e t -> p t e"), ranks, float(-HALF * r),
                                        None, ALU.add).then_inc(rank_ok, 1)
            nc.vector.tensor_copy(count[:, 0:EXPERTS], B[7][:, 32:40]).then_inc(rank_ok, 1)
            dve.wait_ge(rank_ok, 8)
            nc.vector.tensor_reduce(count[:, EXPERTS:EXPERTS + 1], count[:, 0:EXPERTS], AX.X, ALU.max).then_inc(table_ok, 1)
            dve.wait_ge(table_ok, 1)
            nc.vector.tensor_copy(county, count).then_inc(table_ok, 1)
            slots = const(m, C_SLOT, HALF)

            def one_hots():
                for dst, c in ((SEL, 1), (SELG, 0)):
                    for t in range(4):
                        op = nc.vector.tensor_scalar(dst[:, t, :], slots, now[:, 2, t:t + 1], now[:, c, t:t + 1], ALU.is_equal, ALU.mult)
                op.then_inc(built, 1)

            nc.vector.tensor_copy(now, table[:, :, 0, :]).then_inc(now_ok, 1)
            dve.wait_ge(now_ok, 1)
            one_hots()

            def turn(it, nb):
                dve.wait_ge(sel_turned, it + 1)
                for b in range(nb):
                    op = nc.vector.tensor_copy(SELT[:, b, :], B[6 + b][:, :])
                op.then_inc(sel_out, 1)
                for s in range(SLABS):
                    n = width(s)
                    dve.wait_ge(silu_ok, it * SLABS + s + 1)
                    for b in range(nb):
                        op = nc.vector.tensor_tensor(G[:, b, s * HALF:s * HALF + n], sa[:, s % 2, b, 0:n], B[2 * (s % 2) + b][:, n:2 * n], ALU.mult)
                    op.then_inc(gated, 1)
                    if s == 2:
                        nc.vector.tensor_copy(now.unsqueeze(2), table[:, :, bass.ds(it + 1, 1), :]).then_inc(now_ok, 1)
                        dve.wait_ge(now_ok, it + 2)
                        one_hots()
                for k in range(KD):
                    dve.wait_ge(scattered, it * KD + k + 1)
                    nc.vector.scalar_tensor_tensor(out=m.X[:, k, CTX:TOK], in0=B[k % 4][:, :], scalar=m.MOD[:, 1, 5, k, 0:1],
                                                   in1=m.X[:, k, CTX:TOK], op0=ALU.mult, op1=ALU.add).then_inc(added, 1)

            rounds(dve, turn)


def store(m):
    nc = m.nc
    turned, even_out, odd_out, stored = semaphores(m, "store", "turned even_out odd_out stored")
    rows = cut(m, 0, 4 * D).rearrange("p (t d) -> p t d", t=4)
    with nc.Block() as block:

        @block.tensor
        def _(pe):
            for n in range(8):
                for k in range(4):
                    mm = nc.tensor.transpose(m.psum[n][:, k * P:(k + 1) * P],
                                             m.X[:, 4 * (n % 2) + k, CTX + (n // 2) * P:CTX + (n // 2 + 1) * P], const(m, C_IDENT))
                mm.then_inc(turned, 1)

        @block.vector
        def _(dve):
            for n in range(0, 8, 2):
                dve.wait_ge(turned, n + 1)
                nc.vector.tensor_copy(rows[:, n // 2, 0:BANK], m.psum[n][:, :]).then_inc(even_out, 1)

        @block.scalar
        def _(act):
            for n in range(1, 8, 2):
                act.wait_ge(turned, n + 1)
                nc.scalar.copy(rows[:, n // 2, BANK:D], m.psum[n][:, :]).then_inc(odd_out, 1)

        @block.sync
        def _(sp):
            for t in range(4):
                sp.wait_ge(even_out, t + 1)
                sp.wait_ge(odd_out, t + 1)
                sp.dma_start(m.out[0, t * P:(t + 1) * P, :], rows[:, t, :]).then_inc(stored, 16)
            sp.wait_ge(stored, 64)


class Steps:

    def __init__(self, sem, names):
        self.sem, self.names, self.next = sem, names, 0

    @property
    def credit(self):
        return len(self.names)

    def step(self, name):
        assert self.names[self.next] == name, (self.names[self.next], name)
        self.next = (self.next + 1) % len(self.names)
        return 1

    def after(self, head, name):
        return head * len(self.names) + len(self.names) + self.names.index(name) + 1

    def before(self, head, name):
        return head * len(self.names) + self.names.index(name) + 1


LEVELS = 6
PROBLEMS = 12
RUNS = ((0, 4, 0, 0), (4, 8, 0, 1), (8, 10, 4, 0), (10, 12, 4, 1))


def scan_step(s, d):
    if s < 4:
        c = s if d == 0 else 3 - s
        return (8, 10)[d] + c // 2, c % 2
    c = s - 4 if d == 0 else 11 - s
    return (0, 4)[d] + c // 2, c % 2


def load_head_weights(m, sp, h):
    wq = m.dram["gdn_w_qkv"].rearrange("(k p) (s n) -> p s k n", p=P, s=3)
    W = slot(m, 0).rearrange("p (s k n) -> p s k n", s=4, k=KD)
    for s in range(3):
        sp.dma_start(W[:, s], wq[:, s, :, bass.ds(h * P, P)]).then_inc(m.gdn_w_in, 16)


def delta_net_ahead(m):
    m.gdn_w_in, = semaphores(m, "gdn", "w_in")
    return lambda sp: load_head_weights(m, sp, 0)


def delta_net(m):
    nc, dram = m.nc, m.dram
    w_in = m.gdn_w_in
    gate_in, pre_pe, pre_act, pre_dve = semaphores(m, "gdn", "gate_in pre_pe pre_act pre_dve")
    at = [0, SLOT]

    def area(cols):
        if at[0] + cols <= 19500:
            at[0] += cols
            return cut(m, at[0] - cols, cols)
        at[1] += cols
        assert at[1] <= SLOTS * SLOT
        return m.ring[:, at[1] - cols:at[1]]

    def tiles(n):
        return area(n * P).rearrange("p (n t) -> p n t", n=n)

    m.O = area(KD * LAT).rearrange("p (k t) -> p k t", k=KD)
    m.O_first = CTX
    uq, uk, uv = area(LAT), area(TOK), area(TOK)
    gate = area(LAT)
    sq = area(LAT + TOK)
    o_sum, o_f = area(LAT), area(LAT)
    K, V = tiles(6), tiles(6)
    vb, kb, kd = tiles(PROBLEMS), tiles(PROBLEMS), tiles(PROBLEMS)
    DM, EG = tiles(PROBLEMS), tiles(PROBLEMS)
    QE = tiles(8)
    A, T, U, AM, Y = (tiles(PROBLEMS) for _ in range(5))
    AT = tiles(8)
    state = tiles(2)
    cu, wt = A, AM
    coef = area(5 * GH * PROBLEMS).rearrange("p (c h n) -> p c h n", c=5, h=GH)
    hc = area(5 * PROBLEMS).rearrange("p (c n) -> p c n", c=5)
    cw = area(9).rearrange("p (g w) -> p g w", g=3)
    z = area(6 * 32).rearrange("p (t n) -> p t n", t=6)
    z2, z3 = (area(6 * 16).rearrange("p (t n) -> p t n", t=6) for _ in range(2))
    ea = area(16)
    rstd = area(10)
    rstd_o = area(4)
    chunk_eg = area(2 * PROBLEMS).rearrange("p (n c) -> p n c", n=PROBLEMS)
    G_, GC, BETA, BEG, EKD = range(5)
    ident = const(m, C_IDENT)
    small = m.small
    B = m.psum
    wg = dram["gdn_w_gate"].rearrange("(k p) n -> p k n", p=P)
    W = slot(m, 0).rearrange("p (s k n) -> p s k n", s=4, k=KD)
    conv_w = small[:, S_CONV:S_CONV + 72].rearrange("p (g h w) -> p g h w", g=3, h=GH)
    cum = (const(m, C_CUMF), const(m, C_CUMB))
    lev = (C_LEVF, C_LEVB)

    def bank(b, n=4):
        return B[b][:, 0:n * P].rearrange("p (n t) -> p n t", n=n)

    def rows(c, n0, n1):
        return hc[:, c, n0:n1].unsqueeze(2).broadcast_to([P, n1 - n0, P])

    def same(mask, n):
        return mask.unsqueeze(1).broadcast_to([P, n, P])

    CONV = (("kc", uk[:, LAT:TOK], 3, 0, CTX, 1), ("vc", uv[:, LAT:TOK], 3, CTX, CTX, 2), ("k", uk[:, 0:LAT], 0, 0, LAT, 1),
            ("v", uv[:, 0:LAT], 1, 0, LAT, 2), ("q", uq[:, 0:LAT], 2, 0, LAT, 0))
    CONV_OF = {c[0]: c for c in CONV}
    GROUPS = range(3)
    FIRST, SECOND = (3, 0, 2), (4, 5, 1)
    SCAN, OUT = 4, 6
    STEPS = 12
    lv = [f"{l}.{x}" for l in range(1, LEVELS) for x in GROUPS]
    pe_names = (["rows0", "rows1", "rows2", "kvc", "k", "v", "q", "v_turned", "ss", "vc_turned", "bc_k", "bc_kc", "bc_q", "k_turned",
                 "kc_turned", "kk", "kkc", "qk"] + [f"a_turned{x}" for x in GROUPS] + [f"t_turned{x}" for x in GROUPS])
    for l in range(1, LEVELS):
        pe_names += [f"y{l}.{x}" for x in GROUPS]
        pe_names += sum([([f"t{l}.{x}"] if l < LEVELS - 1 else []) + [f"u{l}.{x}"] for x in GROUPS], [])
    pe_names += [f"cu{x}" for x in GROUPS] + [f"wt{x}" for x in GROUPS]
    pe_scan = []
    for s in range(STEPS):
        pe_scan += [f"ws{s}.{d}" for d in range(2)] + (["gate"] if s == 3 else [])
        if s < 11:
            pe_scan += [f"kv{s}.{d}" for d in range(2)]
        if s >= 4:
            pe_scan += [f"o{s}.{d}" for d in range(2)]
    pe_scan += ["ss_o", "bc_o"]
    act_names = ([f"eg{x}" for x in GROUPS] + [f"dm{x}" for x in GROUPS] +
                 ["tap_kc", "tap_vc", "tap_k", "silu_kc", "silu_vc", "sq_kc", "tap_v", "silu_k", "sq_k", "tap_q", "silu_v", "silu_q",
                  "sq_q", "V", "root_q", "root_k", "Vc", "K", "Kc"]
                 + [f"U{x}" for x in GROUPS] + [f"Y{v_}" for v_ in lv] + [f"wt{x}" for x in GROUPS])
    act_scan = ["gate", "o_f", "sq_o", "root_o"]
    dve_names = (["head_coef", "head_conv"] + [f"dm{n}" for n in range(PROBLEMS)]
                 + sum([[f"left_{c[0]}", f"right_{c[0]}"] for c in CONV], [])
                 + ["inv", "k", "kc", "q"] + [f"ad{r}" for r in range(4)]
                 + [f"a{x}" for x in GROUPS] + ["at0", "at1", "T0.0", "T0.1", "T0.2"])
    for l in range(1, LEVELS):
        dve_names += sum([([f"T{l}.{x}"] if l < LEVELS - 1 else []) + [f"U{l}.{x}"] for x in GROUPS], []) + ([f"vb{l - 1}"] if l < 5 else [])
    dve_names += [f"ce{r}" for r in range(4)] + [f"cu{x}" for x in GROUPS]
    dve_scan = []
    for s in range(STEPS):
        dve_scan += [f"vn{s}.{d}" for d in range(2)] + ([f"st{s}.{d}" for d in range(2)] if s < 11 else [])
    dve_scan += ["o", "inv_o", "normed", "out"]
    pool_names = ([f"mask{r}" for r in range(4)] + [f"kb{r}" for r in range(4)] + [f"am0.{r}" for r in range(4)]
                  + [f"am1.{r}" for r in range(4)] + ["qe0", "qe1", "zero"]
                  + sum([[f"am{l}.{r}" for r in range(4)] + [f"kd{l - 2}"] for l in range(2, LEVELS)], []))
    (pe_step, act_step, dve_step, pool_step, pe_scan_step, act_scan_step, dve_scan_step) = semaphores(
        m, "gdn", "pe_step act_step dve_step pool_step pe_scan_step act_scan_step dve_scan_step")
    TE, SC, VE, GP = Steps(pe_step, pe_names), Steps(act_step, act_names), Steps(dve_step, dve_names), Steps(pool_step, pool_names)
    TS, SS, VS = Steps(pe_scan_step, pe_scan), Steps(act_scan_step, act_scan), Steps(dve_scan_step, dve_scan)
    run_of = {0: (0,), 1: (1,), 2: (2, 3)}

    def turns(eng, body):
        body(0, True, False)
        with eng.Fori(1, GH) as h:
            body(h, True, True)
        body(GH, False, True)

    with nc.Block() as block:

        @block.sync
        def _(sp):
            def body(h, prep, scan):
                if prep and scan:
                    sp.wait_ge(pe_step, TE.before(h, "q"))
                    load_head_weights(m, sp, h)
                if scan:
                    sp.wait_ge(pe_scan_step, TS.before(h - 1, "gate"))
                    sp.dma_start(W[:, 3], wg[:, :, bass.ds((h - 1) * P, P)]).then_inc(gate_in, 16)

            turns(sp, body)

        @block.tensor
        def _(pe):
            pe.sem_inc(pe_step, TE.credit)
            pe.sem_inc(pe_scan_step, TS.credit)
            for t in range(6):
                t0 = CTX + t * P if t < 4 else (t - 4) * P
                for k in range(KD):
                    mm = nc.tensor.matmul(B[0][:, 32 * t:32 * t + 32], m.H[:, k, t0:t0 + P], small[:, S_WBD + 32 * k:S_WBD + 32 * k + 32],
                                          start=(k == 0), stop=(k == KD - 1))
            mm.then_inc(pre_pe, 1)
            pe.wait_ge(pre_dve, 15)
            gc = B[1][:, 0:GH * PROBLEMS].rearrange("p (h n) -> p h n", h=GH)
            for n0, n1, _, d in RUNS:
                nc.tensor.matmul(gc[:, :, n0:n1], cum[d], coef[:, G_, :, n0:n1], start=True, stop=True)
            nc.tensor.matmul(B[2][:, 0:GH * PROBLEMS].rearrange("p (h n) -> p h n", h=GH), const(m, C_BLK), coef[:, G_], start=True,
                             stop=True).then_inc(pre_pe, 1)

            def project(b, c0, s, t0, t1, k0=0, k1=KD):
                for k in range(k0, k1):
                    mm = nc.tensor.matmul(B[b][:, c0:c0 + t1 - t0], W[:, s, k, :], m.H[:, k, t0:t1], start=(k == 0), stop=(k == KD - 1))
                return mm

            def body(h, prep, scan):
                def ws(s):
                    if s == 0:
                        pe.wait_ge(act_step, SC.before(h, "wt2"))
                        pe.wait_ge(dve_step, VE.before(h, "cu2"))
                        pe.wait_ge(pool_step, GP.before(h, "kd3"))
                    for d in range(2):
                        n, half = scan_step(s, d)
                        c = slice(64 * half, 64 * half + 64)
                        if s:
                            pe.wait_ge(dve_scan_step, VS.before(h, f"st{s - 1}.{d}"))
                        nc.tensor.matmul(B[SCAN + d][c, 0:P], wt[:, n, c], state[:, d, :], start=True, stop=True)\
                            .then_inc(pe_scan_step, TS.step(f"ws{s}.{d}"))
                        if s >= 4:
                            o0 = (n % 4) * P + 64 * half
                            nc.tensor.matmul(B[OUT + d][:, o0:o0 + 64], state[:, d, :], QE[:, n, c], start=True, stop=False)

                def kv(s):
                    for d in range(2):
                        n, half = scan_step(s, d)
                        c = slice(64 * half, 64 * half + 64)
                        pe.wait_ge(dve_scan_step, VS.before(h, f"vn{s}.{d}"))
                        if s < 11:
                            nc.tensor.matmul(B[SCAN + d][:, P:2 * P], kd[c, n, :], cu[c, n, :], start=True, stop=True)\
                                .then_inc(pe_scan_step, TS.step(f"kv{s}.{d}"))
                    if s >= 4:
                        for d in range(2):
                            n, half = scan_step(s, d)
                            c = slice(64 * half, 64 * half + 64)
                            o0 = (n % 4) * P + 64 * half
                            nc.tensor.matmul(B[OUT + d][:, o0:o0 + 64], cu[c, n, :], AT[c, n, c], start=False, stop=True)\
                                .then_inc(pe_scan_step, TS.step(f"o{s}.{d}"))

                if prep:
                    pe.wait_ge(dve_step, VE.after(h, "head_coef"))
                    pe.wait_ge(act_step, SC.before(h, "wt2"))
                    for x in GROUPS:
                        for n in range(4 * x, 4 * x + 4):
                            d = [r[3] for r in RUNS if r[0] <= n < r[1]][0]
                            mm = nc.tensor.matmul(B[x][:, (n % 4) * P:(n % 4 + 1) * P], hc[:, G_, n:n + 1].to_broadcast([P, P]), cum[d],
                                                  start=True, stop=True)
                        mm.then_inc(pe_step, TE.step(f"rows{x}"))
                    pe.wait_ge(w_in, h * 48 + 48)
                    project(3, 0, 1, 0, CTX)
                    project(3, CTX, 2, 0, CTX).then_inc(pe_step, TE.step("kvc"))
                    pe.wait_ge(dve_step, VE.after(h, "dm3"))
                    project(0, 0, 1, CTX, TOK).then_inc(pe_step, TE.step("k"))
                    pe.wait_ge(dve_step, VE.after(h, "dm7"))
                    project(1, 0, 2, CTX, TOK).then_inc(pe_step, TE.step("v"))
                if scan:
                    ws(0)
                if prep:
                    pe.wait_ge(dve_step, VE.after(h, "dm11"))
                    project(2, 0, 0, CTX, TOK, 0, 4)
                if scan:
                    kv(0)
                    ws(1)
                if prep:
                    project(2, 0, 0, CTX, TOK, 4, 8).then_inc(pe_step, TE.step("q"))
                if scan:
                    kv(1)
                    ws(2)
                    pe.wait_ge(gate_in, h * 16)
                    if prep:
                        pe.wait_ge(dve_step, VE.after(h, "right_vc"))
                    project(3, 0, 3, CTX, TOK, 0, 4)
                    kv(2)
                    ws(3)
                    project(3, 0, 3, CTX, TOK, 4, 8).then_inc(pe_scan_step, TS.step("gate"))
                    kv(3)
                if prep:
                    pe.wait_ge(act_step, SC.after(h, "silu_v"))
                    for t in range(4):
                        mm = nc.tensor.transpose(B[1][:, t * P:(t + 1) * P], uv[:, t * P:(t + 1) * P], ident)
                    mm.then_inc(pe_step, TE.step("v_turned"))
                if scan:
                    ws(4)
                if prep:
                    pe.wait_ge(act_step, SC.after(h, "sq_q"))
                    for t in range(10):
                        mm = nc.tensor.matmul(B[0][:, t:t + 1], sq[:, t * P:(t + 1) * P], const(m, C_ONES, 1), start=True, stop=True)
                    mm.then_inc(pe_step, TE.step("ss"))
                if scan:
                    kv(4)
                    ws(5)
                if prep:
                    pe.wait_ge(act_step, SC.after(h, "V"))
                    for t in range(2):
                        mm = nc.tensor.transpose(B[1][:, t * P:(t + 1) * P], uv[:, LAT + t * P:LAT + (t + 1) * P], ident)
                    mm.then_inc(pe_step, TE.step("vc_turned"))
                if scan:
                    kv(5)
                    ws(6)
                if prep:
                    pe.wait_ge(dve_step, VE.after(h, "inv"))
                    for name, b, t0, n in (("bc_k", 0, 4, 4), ("bc_kc", 3, 8, 2), ("bc_q", 2, 0, 4)):
                        if b == 3:
                            pe.wait_ge(act_scan_step, SS.before(h, "gate"))
                        for t in range(n):
                            mm = nc.tensor.matmul(B[b][:, t * P:(t + 1) * P], rstd[:, t0 + t:t0 + t + 1].to_broadcast([P, P]), ident,
                                                  start=True, stop=True)
                        mm.then_inc(pe_step, TE.step(name))
                if scan:
                    kv(6)
                    ws(7)
                if prep:
                    pe.wait_ge(dve_step, VE.after(h, "k"))
                    pe.wait_ge(act_step, SC.after(h, "Vc"))
                    for t in range(4):
                        mm = nc.tensor.transpose(B[1][:, t * P:(t + 1) * P], uk[:, t * P:(t + 1) * P], ident)
                    mm.then_inc(pe_step, TE.step("k_turned"))
                    pe.wait_ge(dve_step, VE.after(h, "kc"))
                    for t in range(2):
                        mm = nc.tensor.transpose(B[3][:, t * P:(t + 1) * P], uk[:, LAT + t * P:LAT + (t + 1) * P], ident)
                    mm.then_inc(pe_step, TE.step("kc_turned"))
                if scan:
                    kv(7)
                    ws(8)
                if prep:
                    pe.wait_ge(dve_step, VE.after(h, "q"))
                    for t in range(6):
                        kt = uk[:, t * P:(t + 1) * P]
                        mm = nc.tensor.matmul(B[(0, 2)[t // 4]][:, (t % 4) * P:(t % 4 + 1) * P], kt, kt, start=True, stop=True)
                        if t in (3, 5):
                            mm.then_inc(pe_step, TE.step("kk" if t == 3 else "kkc"))
                if scan:
                    kv(8)
                    ws(9)
                if prep:
                    pe.wait_ge(act_step, SC.after(h, "K"))
                    for t in range(4):
                        mm = nc.tensor.matmul(B[1][:, t * P:(t + 1) * P], uk[:, t * P:(t + 1) * P], uq[:, t * P:(t + 1) * P],
                                              start=True, stop=True)
                    mm.then_inc(pe_step, TE.step("qk"))
                if scan:
                    kv(9)
                    ws(10)

                def a_turned(x):
                    pe.wait_ge(dve_step, VE.after(h, ("ad0", "ad1", "ad3")[x]))
                    if x == 0:
                        pe.wait_ge(act_step, SC.after(h, "Kc"))
                    for n in range(4):
                        mm = nc.tensor.transpose(bank(FIRST[x])[:, n, :], T[:, 4 * x + n, :], ident)
                    mm.then_inc(pe_step, TE.step(f"a_turned{x}"))

                if prep:
                    a_turned(0)
                if scan:
                    kv(10)
                    ws(11)
                if prep:
                    a_turned(1)
                    a_turned(2)
                if scan:
                    kv(11)

                def norm_sums():
                    pe.wait_ge(act_scan_step, SS.before(h, "sq_o"))
                    for t in range(4):
                        mm = nc.tensor.matmul(B[OUT][:, t:t + 1], sq[:, t * P:(t + 1) * P], const(m, C_ONES, 1), start=True, stop=True)
                    mm.then_inc(pe_scan_step, TS.step("ss_o"))

                def norm_rows():
                    pe.wait_ge(dve_scan_step, VS.before(h, "inv_o"))
                    for t in range(4):
                        mm = nc.tensor.matmul(B[OUT + 1][:, t * P:(t + 1) * P], rstd_o[:, t:t + 1].to_broadcast([P, P]), ident,
                                              start=True, stop=True)
                    mm.then_inc(pe_scan_step, TS.step("bc_o"))

                if not prep:
                    norm_sums()
                    norm_rows()
                    return
                for x in GROUPS:
                    pe.wait_ge(dve_step, VE.after(h, f"T0.{x}"))
                    for n in range(4):
                        mm = nc.tensor.transpose(bank(SECOND[x])[:, n, :], T[:, 4 * x + n, :], ident)
                    mm.then_inc(pe_step, TE.step(f"t_turned{x}"))

                def level(l):
                    for x in GROUPS:
                        pe.wait_ge(pool_step, GP.after(h, f"am{l}.{run_of[x][-1]}"))
                        if l == 1:
                            pe.wait_ge(act_step, SC.after(h, f"U{x}"))
                        else:
                            pe.wait_ge(dve_step, VE.after(h, f"U{l - 1}.{x}"))
                        for n in range(4):
                            mm = nc.tensor.matmul(bank(FIRST[x])[:, n, :], AM[:, 4 * x + n, :], U[:, 4 * x + n, :], start=True, stop=True)
                        mm.then_inc(pe_step, TE.step(f"y{l}.{x}"))
                    for x in GROUPS:
                        pe.wait_ge(act_step, SC.after(h, f"Y{l}.{x}"))
                        if l < LEVELS - 1:
                            for n in range(4):
                                mm = nc.tensor.matmul(bank(SECOND[x])[:, n, :], Y[:, 4 * x + n, :], T[:, 4 * x + n, :], start=True, stop=True)
                            mm.then_inc(pe_step, TE.step(f"t{l}.{x}"))
                        for n in range(4):
                            mm = nc.tensor.matmul(bank(FIRST[x])[:, n, :], T[:, 4 * x + n, :], Y[:, 4 * x + n, :], start=True, stop=True)
                        mm.then_inc(pe_step, TE.step(f"u{l}.{x}"))

                for l in range(1, LEVELS):
                    level(l)
                    if scan and l == 2:
                        norm_sums()
                    if scan and l == 4:
                        norm_rows()
                for x in GROUPS:
                    pe.wait_ge(dve_step, VE.after(h, f"U{LEVELS - 1}.{x}"))
                    for n in range(4):
                        mm = nc.tensor.matmul(bank(SECOND[x])[:, n, :], U[:, 4 * x + n, :], vb[:, 4 * x + n, :], start=True, stop=True)
                    mm.then_inc(pe_step, TE.step(f"cu{x}"))
                for x in GROUPS:
                    pe.wait_ge(pool_step, GP.after(h, "kb3"))
                    for n in range(4):
                        mm = nc.tensor.matmul(bank(FIRST[x])[:, n, :], kb[:, 4 * x + n, :], U[:, 4 * x + n, :], start=True, stop=True)
                    mm.then_inc(pe_step, TE.step(f"wt{x}"))

            turns(pe, body)

        @block.scalar
        def _(act):
            act.sem_inc(act_step, SC.credit)
            act.sem_inc(act_scan_step, SS.credit)
            act.wait_ge(pre_dve, 1)
            nc.scalar.activation(z[:, :, 0:16], z[:, :, 0:16], ACT.Sigmoid).then_inc(pre_act, 1)
            nc.scalar.activation(ea, small[:, S_ALOG:S_ALOG + 16], ACT.Exp).then_inc(pre_act, 1)
            act.wait_ge(pre_dve, 4)
            nc.scalar.activation(z3, z3, ACT.Exp).then_inc(pre_act, 1)
            act.wait_ge(pre_act, 3)
            nc.scalar.activation(z3, z3, ACT.Ln, bias=const(m, C_EPS + 2, 1)).then_inc(pre_act, 1)
            act.wait_ge(pre_dve, 17)
            nc.scalar.activation(coef[:, BEG], coef[:, GC], ACT.Exp).then_inc(pre_act, 1)
            nc.scalar.activation(coef[:, EKD], coef[:, EKD], ACT.Exp).then_inc(pre_act, 1)

            def body(h, prep, scan):
                def take_o():
                    act.wait_ge(pe_scan_step, TS.before(h, "o11.1"))
                    nc.scalar.copy(o_f, B[OUT][:, :]).then_inc(act_scan_step, SS.step("o_f"))

                def square_o():
                    act.wait_ge(dve_scan_step, VS.before(h, "o"))
                    nc.scalar.activation(sq[:, 0:LAT], o_sum, ACT.Square).then_inc(act_scan_step, SS.step("sq_o"))

                def root_o():
                    act.wait_ge(pe_scan_step, TS.before(h, "ss_o"))
                    nc.scalar.activation(rstd_o, B[OUT][:, 0:4], ACT.Sqrt, bias=const(m, C_EPS, 1), scale=1.0 / GD)\
                        .then_inc(act_scan_step, SS.step("root_o"))

                def take_gate():
                    act.wait_ge(pe_scan_step, TS.before(h, "gate"))
                    nc.scalar.activation(gate, B[3][:, :], ACT.Silu).then_inc(act_scan_step, SS.step("gate"))

                if not prep:
                    take_gate()
                    take_o()
                    square_o()
                    root_o()
                    return

                def tap(name):
                    _, dst, b, c0, n, g = CONV_OF[name]
                    act.wait_ge(pe_step, TE.after(h, {"kc": "kvc", "vc": "kvc"}.get(name, name)))
                    nc.scalar.activation(dst, B[b][:, c0:c0 + n], ACT.Identity, scale=cw[:, g, 1:2]).then_inc(act_step, SC.step(f"tap_{name}"))

                def silu(name):
                    dst = CONV_OF[name][1]
                    act.wait_ge(dve_step, VE.after(h, f"right_{name}"))
                    nc.scalar.activation(dst, dst, ACT.Silu).then_inc(act_step, SC.step(f"silu_{name}"))

                def square(name):
                    at_ = {"q": 0, "k": LAT, "kc": 2 * LAT}[name]
                    dst = CONV_OF[name][1]
                    act.wait_ge(act_step, SC.after(h, f"silu_{name}"))
                    nc.scalar.activation(sq[:, at_:at_ + (CTX if name == "kc" else LAT)], dst, ACT.Square).then_inc(act_step, SC.step(f"sq_{name}"))

                act.wait_ge(pool_step, GP.before(h, "kd3"))
                act.wait_ge(dve_step, VE.after(h, "head_conv"))
                for x in GROUPS:
                    act.wait_ge(pe_step, TE.after(h, f"rows{x}"))
                    nc.scalar.activation(EG[:, 4 * x:4 * x + 4, :], bank(x), ACT.Exp).then_inc(act_step, SC.step(f"eg{x}"))
                for x in GROUPS:
                    act.wait_ge(dve_step, VE.after(h, f"dm{4 * x + 3}"))
                    nc.scalar.activation(DM[:, 4 * x:4 * x + 4, :], DM[:, 4 * x:4 * x + 4, :], ACT.Exp).then_inc(act_step, SC.step(f"dm{x}"))
                tap("kc")
                tap("vc")
                tap("k")
                silu("kc")
                silu("vc")
                square("kc")
                tap("v")
                silu("k")
                square("k")
                tap("q")
                silu("v")
                silu("q")
                square("q")
                if scan:
                    take_gate()
                act.wait_ge(pe_step, TE.after(h, "v_turned"))
                nc.scalar.copy(V[:, 0:4, :], bank(1)).then_inc(act_step, SC.step("V"))
                act.wait_ge(pe_step, TE.after(h, "ss"))
                nc.scalar.activation(rstd[:, 0:4], B[0][:, 0:4], ACT.Sqrt, bias=const(m, C_EPS + 3, 1), scale=float(GD))\
                    .then_inc(act_step, SC.step("root_q"))
                nc.scalar.activation(rstd[:, 4:10], B[0][:, 4:10], ACT.Sqrt, bias=const(m, C_EPS, 1)).then_inc(act_step, SC.step("root_k"))
                act.wait_ge(pe_step, TE.after(h, "vc_turned"))
                nc.scalar.copy(V[:, 4:6, :], bank(1, 2)).then_inc(act_step, SC.step("Vc"))
                act.wait_ge(pe_step, TE.after(h, "k_turned"))
                nc.scalar.copy(K[:, 0:4, :], bank(1)).then_inc(act_step, SC.step("K"))
                act.wait_ge(pe_step, TE.after(h, "kc_turned"))
                nc.scalar.copy(K[:, 4:6, :], bank(3, 2)).then_inc(act_step, SC.step("Kc"))
                for x in GROUPS:
                    act.wait_ge(pe_step, TE.after(h, f"t_turned{x}"))
                    nc.scalar.copy(U[:, 4 * x:4 * x + 4, :], bank(SECOND[x])).then_inc(act_step, SC.step(f"U{x}"))
                if scan:
                    take_o()
                for l in range(1, LEVELS):
                    for x in GROUPS:
                        act.wait_ge(pe_step, TE.after(h, f"y{l}.{x}"))
                        nc.scalar.copy(Y[:, 4 * x:4 * x + 4, :], bank(FIRST[x])).then_inc(act_step, SC.step(f"Y{l}.{x}"))
                    if scan and l == 1:
                        square_o()
                    if scan and l == 3:
                        root_o()
                for x in GROUPS:
                    act.wait_ge(pe_step, TE.after(h, f"wt{x}"))
                    nc.scalar.copy(wt[:, 4 * x:4 * x + 4, :], bank(FIRST[x])).then_inc(act_step, SC.step(f"wt{x}"))

            turns(act, body)

        @block.gpsimd
        def _(pool):
            pool.sem_inc(pool_step, GP.credit)

            def body(h, prep, scan):
                if not prep:
                    return
                for r, (n0, n1, _, d) in enumerate(RUNS):
                    pool.wait_ge(act_step, SC.after(h, f"dm{(n1 - 1) // 4}"))
                    nc.gpsimd.tensor_tensor(DM[:, n0:n1, :], DM[:, n0:n1, :], same(cum[d], n1 - n0), ALU.mult)\
                        .then_inc(pool_step, GP.step(f"mask{r}"))

                def scaled_keys(dst, c, name, r):
                    n0, n1, t0, d = RUNS[r]
                    nc.gpsimd.tensor_tensor(dst[:, n0:n1, :], K[:, t0:t0 + n1 - n0, :], rows(c, n0, n1), ALU.mult)\
                        .then_inc(pool_step, GP.step(f"{name}{r}"))

                pool.wait_ge(act_step, SC.after(h, "Kc"))
                for r in range(4):
                    scaled_keys(kb, BEG, "kb", r)
                for l in range(LEVELS):
                    for r, (n0, n1, _, d) in enumerate(RUNS):
                        x = min(r, 2)
                        if l == 0:
                            pool.wait_ge(dve_step, VE.after(h, f"a{x}"))
                        elif l == 1:
                            pool.wait_ge(dve_step, VE.after(h, f"T0.{x}"))
                        else:
                            pool.wait_ge(pe_step, TE.after(h, f"y{l - 1}.{x}"))
                        nc.gpsimd.tensor_tensor(AM[:, n0:n1, :], A[:, n0:n1, :], same(const(m, lev[d] + l * P), n1 - n0), ALU.mult)\
                            .then_inc(pool_step, GP.step(f"am{l}.{r}"))
                    if l == 1:
                        pool.wait_ge(dve_step, VE.after(h, "q"))
                        pool.wait_ge(pe_scan_step, TS.before(h, "o11.1"))
                        for d in range(2):
                            nc.gpsimd.tensor_tensor(QE[:, 4 * d:4 * d + 4, :], uq.rearrange("p (n t) -> p n t", n=4), EG[:, 4 * d:4 * d + 4, :],
                                                    ALU.mult).then_inc(pool_step, GP.step(f"qe{d}"))
                        nc.gpsimd.memset(state, 0.0).then_inc(pool_step, GP.step("zero"))
                    if l >= 2:
                        scaled_keys(kd, EKD, "kd", l - 2)

            turns(pool, body)

        @block.vector
        def _(dve):
            dve.sem_inc(dve_step, VE.credit)
            dve.sem_inc(dve_scan_step, VS.credit)
            dve.wait_ge(pre_pe, 1)
            nc.vector.tensor_copy(z, B[0][:, 0:192].rearrange("p (t n) -> p t n", t=6)).then_inc(pre_dve, 1)
            dve.wait_ge(pre_dve, 1)
            dtb = small[:, S_DTB:S_DTB + 16].unsqueeze(1).broadcast_to([P, 6, 16])
            nc.vector.tensor_tensor(z2, z[:, :, 16:32], dtb, ALU.add).then_inc(pre_dve, 1)
            dve.wait_ge(pre_dve, 2)
            nc.vector.tensor_scalar(z3, z2, -1.0, None, ALU.mult).then_inc(pre_dve, 1)
            dve.wait_ge(pre_dve, 3)
            nc.vector.tensor_tensor(z3, z3, z2, ALU.min).then_inc(pre_dve, 1)
            dve.wait_ge(pre_dve, 4)
            nc.vector.tensor_scalar(z2, z2, 0.0, None, ALU.max).then_inc(pre_dve, 1)
            dve.wait_ge(pre_dve, 5)
            dve.wait_ge(pre_act, 4)
            nc.vector.tensor_tensor(z2, z2, z3, ALU.add).then_inc(pre_dve, 1)
            dve.wait_ge(pre_dve, 6)
            nc.vector.tensor_tensor(z2, z2, ea.unsqueeze(1).broadcast_to([P, 6, 16]), ALU.mult).then_inc(pre_dve, 1)
            dve.wait_ge(pre_dve, 7)
            for n0, n1, t0, d in RUNS:
                for c, src, f in ((G_, z2, -1.0), (BETA, z, 1.0)):
                    nc.vector.tensor_scalar(coef[:, c, :, n0:n1], src[:, t0:t0 + n1 - n0, GH * d:GH * d + GH].rearrange("p t h -> p h t"),
                                            f, None, ALU.mult).then_inc(pre_dve, 1)
            dve.wait_ge(pre_pe, 2)
            nc.vector.tensor_copy(coef[:, GC], B[1][:, 0:GH * PROBLEMS].rearrange("p (h n) -> p h n", h=GH)).then_inc(pre_dve, 1)
            dve.wait_ge(pre_dve, 16)
            nc.vector.tensor_tensor(coef[:, EKD], B[2][:, 0:GH * PROBLEMS].rearrange("p (h n) -> p h n", h=GH), coef[:, GC],
                                    ALU.subtract).then_inc(pre_dve, 1)
            dve.wait_ge(pre_act, 6)
            nc.vector.tensor_tensor(coef[:, BEG], coef[:, BEG], coef[:, BETA], ALU.mult).then_inc(pre_dve, 1)
            dve.wait_ge(pre_dve, 18)

            def body(h, prep, scan):
                def vn(s):
                    for d in range(2):
                        n, half = scan_step(s, d)
                        c = slice(64 * half, 64 * half + 64)
                        dve.wait_ge(pe_scan_step, TS.before(h, f"ws{s}.{d}"))
                        if s == 0:
                            dve.wait_ge(dve_step, VE.before(h, "cu2"))
                        nc.vector.tensor_tensor(cu[c, n, :], cu[c, n, :], B[SCAN + d][c, 0:P], ALU.subtract)\
                            .then_inc(dve_scan_step, VS.step(f"vn{s}.{d}"))

                def st(s):
                    for d in range(2):
                        n, half = scan_step(s, d)
                        dve.wait_ge(pe_scan_step, TS.before(h, f"kv{s}.{d}"))
                        nc.vector.scalar_tensor_tensor(out=state[:, d, :], in0=state[:, d, :], scalar=chunk_eg[:, n, half:half + 1],
                                                       in1=B[SCAN + d][:, P:2 * P], op0=ALU.mult, op1=ALU.add)\
                            .then_inc(dve_scan_step, VS.step(f"st{s}.{d}"))

                def conv(name):
                    _, dst, b, c0, n, g = CONV_OF[name]
                    dve.wait_ge(act_step, SC.after(h, "tap_vc" if b == 3 else f"tap_{name}"))
                    nc.vector.scalar_tensor_tensor(out=dst[:, 1:n], in0=B[b][:, c0:c0 + n - 1], scalar=cw[:, g, 0:1], in1=dst[:, 1:n],
                                                   op0=ALU.mult, op1=ALU.add).then_inc(dve_step, VE.step(f"left_{name}"))
                    dve.wait_ge(dve_step, VE.after(h, f"left_{name}"))
                    nc.vector.scalar_tensor_tensor(out=dst[:, 0:n - 1], in0=B[b][:, c0 + 1:c0 + n], scalar=cw[:, g, 2:3], in1=dst[:, 0:n - 1],
                                                   op0=ALU.mult, op1=ALU.add).then_inc(dve_step, VE.step(f"right_{name}"))

                def value_rows(r):
                    n0, n1, t0, d = RUNS[r]
                    dve.wait_ge(act_step, SC.after(h, "Vc"))
                    nc.vector.tensor_tensor(vb[:, n0:n1, :], V[:, t0:t0 + n1 - n0, :], rows(BETA, n0, n1), ALU.mult)\
                        .then_inc(dve_step, VE.step(f"vb{r}"))

                def masked(r):
                    n0, n1, t0, d = RUNS[r]
                    dve.wait_ge(pe_step, TE.after(h, "kk" if r < 2 else "kkc"))
                    dve.wait_ge(pool_step, GP.after(h, f"mask{r}"))
                    nc.vector.tensor_tensor(T[:, n0:n1, :], bank((0, 2)[r > 1], n1 - n0), DM[:, n0:n1, :], ALU.mult)\
                        .then_inc(dve_step, VE.step(f"ad{r}"))

                def sum_o():
                    dve.wait_ge(act_scan_step, SS.before(h, "o_f"))
                    nc.vector.tensor_tensor(o_sum, o_f, B[OUT + 1][:, :], ALU.add).then_inc(dve_scan_step, VS.step("o"))

                def inv_o():
                    dve.wait_ge(act_scan_step, SS.before(h, "root_o"))
                    nc.vector.reciprocal(rstd_o, rstd_o).then_inc(dve_scan_step, VS.step("inv_o"))

                def out_o():
                    dve.wait_ge(pe_scan_step, TS.before(h, "bc_o"))
                    nc.vector.scalar_tensor_tensor(out=o_sum, in0=o_sum, scalar=small[:, S_ON:S_ON + 1], in1=B[OUT + 1][:, :], op0=ALU.mult,
                                                   op1=ALU.mult).then_inc(dve_scan_step, VS.step("normed"))
                    dve.wait_ge(dve_scan_step, VS.before(h, "normed"))
                    nc.vector.tensor_tensor(m.O[:, bass.ds(h - 1, 1), :], o_sum.unsqueeze(1), gate.unsqueeze(1), ALU.mult)\
                        .then_inc(dve_scan_step, VS.step("out"))

                if not prep:
                    for s in range(STEPS):
                        vn(s)
                        if s < STEPS - 1:
                            st(s)
                    sum_o()
                    inv_o()
                    out_o()
                    return
                dve.wait_ge(pool_step, GP.before(h, "kd3"))
                dve.wait_ge(act_step, SC.before(h, "wt2"))
                nc.vector.tensor_copy(hc.unsqueeze(2), coef[:, :, bass.ds(h, 1), :]).then_inc(dve_step, VE.step("head_coef"))
                nc.vector.tensor_copy(cw.unsqueeze(2), conv_w[:, :, bass.ds(h, 1), :]).then_inc(dve_step, VE.step("head_conv"))
                dve.wait_ge(dve_step, VE.after(h, "head_conv"))
                for n in range(PROBLEMS):
                    if n % 4 == 0:
                        dve.wait_ge(act_step, SC.after(h, f"eg{n // 4}"))
                    nc.vector.tensor_scalar(DM[:, n, :], bank(n // 4)[:, n % 4, :], hc[:, GC, n:n + 1], 0.0, ALU.subtract, ALU.min)\
                        .then_inc(dve_step, VE.step(f"dm{n}"))
                conv("kc")
                conv("vc")
                conv("k")
                if scan:
                    vn(0)
                conv("v")
                if scan:
                    st(0)
                    vn(1)
                    st(1)
                    vn(2)
                conv("q")
                if scan:
                    st(2)
                    vn(3)
                    st(3)
                    vn(4)
                    st(4)
                    vn(5)
                dve.wait_ge(act_step, SC.after(h, "root_k"))
                nc.vector.reciprocal(rstd, rstd).then_inc(dve_step, VE.step("inv"))
                if scan:
                    st(5)
                    vn(6)
                for name, dst, b, n in (("k", uk[:, 0:LAT], 0, LAT), ("kc", uk[:, LAT:TOK], 3, CTX), ("q", uq, 2, LAT)):
                    dve.wait_ge(pe_step, TE.after(h, f"bc_{name}"))
                    nc.vector.tensor_tensor(dst, dst, B[b][:, 0:n], ALU.mult).then_inc(dve_step, VE.step(name))
                if scan:
                    st(6)
                    vn(7)
                    st(7)
                    vn(8)
                    st(8)
                masked(0)
                masked(1)
                if scan:
                    vn(9)
                masked(2)
                masked(3)
                if scan:
                    st(9)
                    vn(10)
                    st(10)
                    vn(11)
                dve.wait_ge(pe_scan_step, TS.before(h, "o11.1"))
                for x in GROUPS:
                    dve.wait_ge(pe_step, TE.after(h, f"a_turned{x}"))
                    nc.vector.tensor_tensor(A[:, 4 * x:4 * x + 4, :], bank(FIRST[x]), rows(BETA, 4 * x, 4 * x + 4), ALU.mult)\
                        .then_inc(dve_step, VE.step(f"a{x}"))
                for d in range(2):
                    dve.wait_ge(pe_step, TE.after(h, "qk"))
                    nc.vector.tensor_tensor(AT[:, 4 * d:4 * d + 4, :], bank(1), DM[:, 4 * d:4 * d + 4, :], ALU.mult)\
                        .then_inc(dve_step, VE.step(f"at{d}"))
                for x in GROUPS:
                    dve.wait_ge(pool_step, GP.after(h, f"am0.{run_of[x][-1]}"))
                    nc.vector.tensor_tensor(T[:, 4 * x:4 * x + 4, :], same(ident, 4), AM[:, 4 * x:4 * x + 4, :], ALU.subtract)\
                        .then_inc(dve_step, VE.step(f"T0.{x}"))
                if scan:
                    sum_o()
                for l in range(1, LEVELS):
                    for x in GROUPS:
                        g4 = slice(4 * x, 4 * x + 4)
                        dve.wait_ge(pe_step, TE.after(h, f"u{l}.{x}"))
                        if l < LEVELS - 1:
                            nc.vector.tensor_tensor(T[:, g4, :], T[:, g4, :], bank(SECOND[x]), ALU.subtract).then_inc(dve_step, VE.step(f"T{l}.{x}"))
                        nc.vector.tensor_tensor(U[:, g4, :], U[:, g4, :], bank(FIRST[x]), ALU.subtract).then_inc(dve_step, VE.step(f"U{l}.{x}"))
                    if l < 5:
                        value_rows(l - 1)
                    if scan and l == 3:
                        inv_o()
                    if scan and l == 4:
                        out_o()
                for r, (n0, n1, _, d) in enumerate(RUNS):
                    nc.vector.tensor_copy(chunk_eg[:, n0:n1, :], EG[:, n0:n1, (63, 0)[d]:P:64]).then_inc(dve_step, VE.step(f"ce{r}"))
                for x in GROUPS:
                    dve.wait_ge(pe_step, TE.after(h, f"cu{x}"))
                    nc.vector.tensor_copy(cu[:, 4 * x:4 * x + 4, :], bank(SECOND[x])).then_inc(dve_step, VE.step(f"cu{x}"))

            turns(dve, body)
    for engine in (TE, SC, VE, GP, TS, SS, VS):
        assert engine.next == 0, engine.names[engine.next]


def build(nc, dram, out):
    with ExitStack() as ctx:
        m = open_memory(nc, ctx, dram)
        m.out = out
        load_and_modulation(m)
        norm_modulate(m, "n0", 0, 0, ahead=attention_ahead(m))
        neighbourhood_attention(m, ahead=projection_ahead(m, "no", dram["na_w_o"]))
        project_to_residual(m, "no", 0, 0)
        norm_modulate(m, "n1", 0, 1, ahead=swiglu_ahead(m))
        swiglu(m)
        reorder(m)
        norm_modulate(m, "n2", 1, 0, ahead=delta_net_ahead(m))
        delta_net(m)
        project_to_residual(m, "go", 1, CTX, load=projection_ahead(m, "go", dram["gdn_w_o"]))
        norm_modulate(m, "n3", 1, 1, first=CTX)
        experts(m)
        store(m)


_INS = ["x", "ctx", "ada_w", "na_w_qkv", "na_w_o", "gdn_w_qkv", "gdn_w_gate", "gdn_w_o", "ffn_w_in", "ffn_w_out",
        "moe_w_in", "moe_w_out"]


def kernel(**inputs):
    import concourse.bacc as bacc
    from concourse.bass_utils import run_bass_kernel_spmd

    nc = bacc.Bacc("TRN2", target_bir_lowering=False, num_devices=1)
    arrays = {n: np.ascontiguousarray(inputs[n]) for n in _INS}
    arrays["small"] = small_inputs(inputs)
    arrays["bias"] = bias_table(inputs["na_rpb"])
    arrays["const"] = constants()
    dram = {n: nc.dram_tensor(f"in_{n}", a.shape, mybir.dt.from_np(a.dtype), kind="ExternalInput").ap()
            for n, a in arrays.items()}
    out = nc.dram_tensor("out", (1, LAT, D), F32, kind="ExternalOutput").ap()
    build(nc, dram, out)
    r = run_bass_kernel_spmd(nc, [{f"in_{n}": a for n, a in arrays.items()}], core_ids=[0])
    return r.results[0]["out"]
```
